# Optimizing a Trainium2 kernel written in Bass

```python
import jax, jax.numpy as jnp
from jax import lax
import numpy as np

D_MODEL = 1024
BATCH = 1
SEQ = 256
DEPTH = 2

CHUNK = 64
N_MIXERS = 2
LRU_WIDTH = D_MODEL
LRU_BLOCKS = 8
LRU_BLOCK = LRU_WIDTH // LRU_BLOCKS
CONV_WIDTH = 4
LRU_C = 8.0
FOX_HEADS = 16
FOX_HEAD_DIM = D_MODEL // FOX_HEADS
Q_BLOCK = 2 * CHUNK
D_FF = 7 * D_MODEL // 2
N_EXPERTS = 8
TOP_K = 2
RMS_EPS = 1e-6
N_LRU = (DEPTH + 1) // 2
N_FOX = DEPTH // 2
N_DENSE = (DEPTH + 1) // 2
N_MOE = DEPTH // 2

kernel_name = "hybrid_rglru_fox_moe_trunk"

def rms_norm(x, g):
    xf = x.astype(jnp.float32)
    y = xf * lax.rsqrt(jnp.mean(xf * xf, axis=-1, keepdims=True) + RMS_EPS)
    return (y * g.astype(jnp.float32)).astype(x.dtype)

def _lin_combine(c1, c2):
    a1, b1 = c1
    a2, b2 = c2
    return a1 * a2, a2 * b1 + b2

def rg_lru_mixer(h, w_in, conv_w, conv_b, w_a, b_a, w_x, b_x, log_lambda, w_out):
    B, S, _ = h.shape
    proj = h @ w_in
    y_branch, x_branch = jnp.split(proj, 2, axis=-1)
    y_branch = jax.nn.gelu(y_branch)
    xc = lax.conv_general_dilated(
        x_branch, conv_w[:, None, :].astype(x_branch.dtype), window_strides=(1,),
        padding=[(CONV_WIDTH - 1, 0)], dimension_numbers=('NWC', 'WIO', 'NWC'),
        feature_group_count=LRU_WIDTH) + conv_b
    xb = xc.reshape(B, S, LRU_BLOCKS, LRU_BLOCK)
    r = jax.nn.sigmoid(jnp.einsum('bshi,hij->bshj', xb, w_a).reshape(B, S, LRU_WIDTH) + b_a)
    gi = jax.nn.sigmoid(jnp.einsum('bshi,hij->bshj', xb, w_x).reshape(B, S, LRU_WIDTH) + b_x)
    log_a = -LRU_C * r.astype(jnp.float32) * jax.nn.softplus(-log_lambda.astype(jnp.float32))
    a = jnp.exp(log_a)
    mult = jnp.sqrt(-jnp.expm1(2.0 * log_a))
    b = mult * (gi * xc).astype(jnp.float32)
    _, hseq = lax.associative_scan(_lin_combine, (a, b), axis=1)
    return (hseq.astype(h.dtype) * y_branch) @ w_out

def fox_mixer(h, w_in, b_f, q_gain, k_gain, w_out):
    B, S, D = h.shape
    proj = h @ w_in
    q, k, v, g, f = jnp.split(proj, [D, 2 * D, 3 * D, 4 * D], axis=-1)
    q = rms_norm(q.reshape(B, S, FOX_HEADS, FOX_HEAD_DIM), q_gain)
    k = rms_norm(k.reshape(B, S, FOX_HEADS, FOX_HEAD_DIM), k_gain)
    v = v.reshape(B, S, FOX_HEADS, FOX_HEAD_DIM)
    log_f = jax.nn.log_sigmoid(f.astype(jnp.float32) + b_f.astype(jnp.float32))
    F = jnp.cumsum(log_f, axis=1).transpose(0, 2, 1)
    qh = q.transpose(0, 2, 1, 3)
    kh = k.transpose(0, 2, 1, 3)
    vh = v.transpose(0, 2, 1, 3)
    nb = S // Q_BLOCK
    q_blocks = qh.reshape(B, FOX_HEADS, nb, Q_BLOCK, FOX_HEAD_DIM).transpose(2, 0, 1, 3, 4)
    F_blocks = F.reshape(B, FOX_HEADS, nb, Q_BLOCK).transpose(2, 0, 1, 3)
    key_pos = jnp.arange(S)
    scale = FOX_HEAD_DIM ** -0.5

    def attend(args):
        qb, Fq, blk = args
        s = jnp.einsum('bhqd,bhkd->bhqk', qb, kh, preferred_element_type=jnp.float32) * scale
        s = s + Fq[..., None] - F[:, :, None, :]
        q_pos = blk * Q_BLOCK + jnp.arange(Q_BLOCK)
        s = jnp.where(key_pos[None, :] <= q_pos[:, None], s, -jnp.inf)
        p = jax.nn.softmax(s, axis=-1)
        return jnp.einsum('bhqk,bhkd->bhqd', p.astype(vh.dtype), vh)

    o = lax.map(attend, (q_blocks, F_blocks, jnp.arange(nb)))
    o = o.transpose(1, 0, 3, 2, 4).reshape(B, S, D)
    o = o * jax.nn.sigmoid(g)
    return o @ w_out

def swiglu(h, w_gate, w_up, w_down):
    return (jax.nn.silu(h @ w_gate) * (h @ w_up)) @ w_down

def moe_swiglu(h, router, w_gate, w_up, w_down):
    B, S, D = h.shape
    t = h.reshape(B * S, D)
    logits = (t @ router).astype(jnp.float32)
    top_v, top_i = lax.top_k(logits, TOP_K)
    w = jax.nn.softmax(top_v, axis=-1)
    combine = jnp.sum(jax.nn.one_hot(top_i, N_EXPERTS, dtype=jnp.float32) * w[..., None], axis=1)
    out = jnp.zeros_like(t)
    for e in range(N_EXPERTS):
        out = out + combine[:, e:e + 1].astype(t.dtype) * swiglu(t, w_gate[e], w_up[e], w_down[e])
    return out.reshape(B, S, D)

def setup_inputs(seed: int = 0) -> dict:
    key = jax.random.key(seed)
    ks = jax.random.split(key, 24)
    f32 = jnp.float32
    nrm = lambda k, shape, s: jax.random.normal(k, shape, f32) * s
    D = D_MODEL
    u = jax.random.uniform(ks[8], (N_LRU, LRU_WIDTH), f32, minval=0.9, maxval=0.999)
    a0 = u ** (1.0 / LRU_C)
    log_lambda = jnp.log(a0) - jnp.log1p(-a0)
    return {
        "x": nrm(ks[0], (BATCH, SEQ, D), 1.0),
        "norm_mix": 1.0 + nrm(ks[1], (DEPTH, D), 0.01),
        "norm_ffn": 1.0 + nrm(ks[2], (DEPTH, D), 0.01),
        "lru_w_in": nrm(ks[3], (N_LRU, D, 2 * LRU_WIDTH), D ** -0.5),
        "lru_conv_w": nrm(ks[4], (N_LRU, CONV_WIDTH, LRU_WIDTH), CONV_WIDTH ** -0.5),
        "lru_conv_b": nrm(ks[5], (N_LRU, LRU_WIDTH), 0.01),
        "lru_w_a": nrm(ks[6], (N_LRU, LRU_BLOCKS, LRU_BLOCK, LRU_BLOCK), LRU_BLOCK ** -0.5),
        "lru_b_a": nrm(ks[7], (N_LRU, LRU_WIDTH), 0.01),
        "lru_w_x": nrm(ks[9], (N_LRU, LRU_BLOCKS, LRU_BLOCK, LRU_BLOCK), LRU_BLOCK ** -0.5),
        "lru_b_x": nrm(ks[10], (N_LRU, LRU_WIDTH), 0.01),
        "lru_log_lambda": log_lambda,
        "lru_w_out": nrm(ks[11], (N_LRU, LRU_WIDTH, D), LRU_WIDTH ** -0.5),
        "fox_w_in": nrm(ks[12], (N_FOX, D, 4 * D + FOX_HEADS), D ** -0.5),
        "fox_b_f": jax.random.uniform(ks[13], (N_FOX, FOX_HEADS), f32, minval=1.0, maxval=6.0),
        "fox_q_gain": 1.0 + nrm(ks[14], (N_FOX, FOX_HEAD_DIM), 0.01),
        "fox_k_gain": 1.0 + nrm(ks[15], (N_FOX, FOX_HEAD_DIM), 0.01),
        "fox_w_out": nrm(ks[16], (N_FOX, D, D), D ** -0.5),
        "ffn_w_gate": nrm(ks[17], (N_DENSE, D, D_FF), D ** -0.5),
        "ffn_w_up": nrm(ks[18], (N_DENSE, D, D_FF), D ** -0.5),
        "ffn_w_down": nrm(ks[19], (N_DENSE, D_FF, D), D_FF ** -0.5),
        "moe_router": nrm(ks[20], (N_MOE, D, N_EXPERTS), D ** -0.5),
        "moe_w_gate": nrm(ks[21], (N_MOE, N_EXPERTS, D, D_FF), D ** -0.5),
        "moe_w_up": nrm(ks[22], (N_MOE, N_EXPERTS, D, D_FF), D ** -0.5),
        "moe_w_down": nrm(ks[23], (N_MOE, N_EXPERTS, D_FF, D), D_FF ** -0.5),
    }

def reference(x, norm_mix, norm_ffn, lru_w_in, lru_conv_w, lru_conv_b, lru_w_a, lru_b_a,
              lru_w_x, lru_b_x, lru_log_lambda, lru_w_out, fox_w_in, fox_b_f, fox_q_gain,
              fox_k_gain, fox_w_out, ffn_w_gate, ffn_w_up, ffn_w_down, moe_router,
              moe_w_gate, moe_w_up, moe_w_down):
    for i in range(DEPTH):
        j = i // 2
        hn = rms_norm(x, norm_mix[i])
        if i % N_MIXERS == 0:
            x = x + rg_lru_mixer(hn, lru_w_in[j], lru_conv_w[j], lru_conv_b[j], lru_w_a[j],
                                 lru_b_a[j], lru_w_x[j], lru_b_x[j], lru_log_lambda[j], lru_w_out[j])
        else:
            x = x + fox_mixer(hn, fox_w_in[j], fox_b_f[j], fox_q_gain[j], fox_k_gain[j], fox_w_out[j])
        hn = rms_norm(x, norm_ffn[i])
        if i % 2 == 0:
            x = x + swiglu(hn, ffn_w_gate[j], ffn_w_up[j], ffn_w_down[j])
        else:
            x = x + moe_swiglu(hn, moe_router[j], moe_w_gate[j], moe_w_up[j], moe_w_down[j])
    return x


_drawn_inputs = setup_inputs


def setup_inputs(seed=0):
    import zlib

    import numpy as np

    out = dict(_drawn_inputs(seed))
    spreads = {}
    factors = {'lru_b_a': 8.0, 'lru_b_x': 4.031, 'fox_q_gain': 4.012, 'fox_k_gain': 4.042}
    for name, (base, spread) in spreads.items():
        noise = np.random.default_rng([zlib.crc32(name.encode()), seed]).standard_normal(out[name].shape)
        drawn = base * np.exp(spread * noise) if base else spread * noise
        out[name] = __import__('jax').numpy.asarray(drawn.astype(out[name].dtype))
    for name, factor in factors.items():
        out[name] = (out[name] * factor).astype(out[name].dtype)
    return out
```

```python
from contextlib import ExitStack

import concourse.bass as bass
from concourse import mybir

P = 128
D = 1024
KT = D // P
T = 256
TT = T // P
F = 3584
CW = 512
UK = 4
FC = F // CW
H = 16
HD = D // H
E = 8
CONV = 4
LRU_C = 8.0
EPS = 1e-6
NEG = -1e30
BIG = 3e38

HR = 3
RR = 7
FFN_UNITS = FC * 6
N_IN = 8
N_FFN = N_IN + 4
N_FOX = N_FFN + FFN_UNITS
N_FOXOUT = N_FOX + 16
N_MOE = N_FOXOUT + 4
assert FFN_UNITS % HR == 0 and FFN_UNITS % RR == 0

F32 = mybir.dt.float32
F32R = mybir.dt.float32r
I32 = mybir.dt.int32
ALU = mybir.AluOpType
ACT = mybir.ActivationFunctionType
AX_X = mybir.AxisListType.X


def base(c):
    return 0 if c == 0 else 4 + 6 * (c - 1)


def down(c):
    return base(c + 1) + 4 if c < FC - 1 else FFN_UNITS - 2


def at(count, per, b):
    return count if b is None else b * per + count


def hybrid_trunk(nc, x, norm_mix, norm_ffn, lru_w_in, lru_conv_w, lru_conv_b, lru_w_a, lru_b_a, lru_w_x, lru_b_x,
                 lru_log_lambda, lru_w_out, fox_w_in, fox_b_f, fox_q_gain, fox_k_gain, fox_w_out, ffn_w_gate,
                 ffn_w_up, ffn_w_down, moe_router, moe_w_gate, moe_w_up, moe_w_down, out):
    with ExitStack() as ctx:
        def sem(name):
            return ctx.enter_context(nc.semaphore(name))

        def sb(name, shape, dt=F32, where=None):
            return (where or ctx).enter_context(nc.sbuf_tensor(name, shape, dt))

        ps = ctx.enter_context(nc.psum_tensor("ps", [P, 8, CW], F32))
        raw = sb("raw", [P, RR, UK, CW])
        whi = sb("whi", [P, HR, UK, CW], F32R)
        wlo = sb("wlo", [P, HR, UK, CW], F32R)
        X = sb("X", [P, TT, D])
        rows3 = sb("rows3", [P, 3 * D])
        xn = rows3[:, 0:TT * D].rearrange("p (t d) -> p t d", t=TT)
        junk = rows3[:, TT * D:]
        hT_hi = sb("hT_hi", [P, KT, T], F32R)
        hT_lo = sb("hT_lo", [P, KT, T], F32R)
        ident = sb("ident", [P, P])
        ident_r = sb("ident_r", [P, P], F32R)
        upper = sb("upper", [P, P])
        ones = sb("ones", [P, P])
        mask = sb("mask", [P, P])
        mask_r = sb("mask_r", [P, P], F32R)
        iota = sb("iota", [P, P])
        par_rows = sb("par_rows", [96, P])
        par = sb("par", [P, 96])
        ss = sb("ss", [P, 8])
        ms = sb("ms", [P, 8])
        rstd = sb("rstd", [P, 8])
        mhalf = sb("mhalf", [P, H])
        PAR_CONVW, PAR_CONVB, PAR_BA, PAR_BX, PAR_LAM, PAR_MIX, PAR_FFN = 0, 32, 40, 48, 56, 64, 80
        GAIN = [PAR_MIX, PAR_FFN, PAR_MIX + KT, PAR_FFN + KT]

        wf = sb("wf", [P, KT, H])
        wf_hi = sb("wf_hi", [P, KT, H], F32R)
        wf_lo = sb("wf_lo", [P, KT, H], F32R)
        bf = sb("bf", [P, H])
        qkg = sb("qkg", [P, 2])
        fx = sb("fx", [P, 8, TT, H])
        nF = sb("nF", [P, TT, H])
        nFT_hi = sb("nFT_hi", [P, T], F32R)
        nFT_lo = sb("nFT_lo", [P, T], F32R)
        ssq = sb("ssq", [P, 3, TT * 8])
        nm = sb("nm", [P, 4, 8])
        sm = sb("sm", [P, 4, 8])
        rinv = sb("rinv", [P, 4, 8])
        rw = sb("rw", [P, KT, E])
        rw_hi = sb("rw_hi", [P, KT, E], F32R)
        rw_lo = sb("rw_lo", [P, KT, E], F32R)
        cnt = sb("cnt", [P, 2])
        nblk_i = sb("nblk_i", [P, 1], I32)

        with ExitStack() as a1:
            xpad = sb("xpad", [P, KT, CONV - 1 + T], where=a1)
            xc = sb("xc", [P, KT, T], where=a1)
            rg = sb("rg", [P, KT, T], where=a1)
            gi = sb("gi", [P, KT, T], where=a1)
            av = sb("av", [P, KT, T], where=a1)
            yb = sb("yb", [P, KT, T], where=a1)
            wax = sb("wax", [P, 2, KT, P], where=a1)
            lt = sb("lt", [P, 6, 8], where=a1)
        with ExitStack() as a2:
            sil = sb("sil", [P, 4, T], where=a2)
            fT_hi = sb("fT_hi", [P, 2, 4, T], F32R, where=a2)
            fT_lo = sb("fT_lo", [P, 2, 4, T], F32R, where=a2)
        with ExitStack() as a3:
            qT_hi = sb("qT_hi", [P, KT, T], F32R, where=a3)
            qT_lo = sb("qT_lo", [P, KT, T], F32R, where=a3)
            kT_hi = sb("kT_hi", [P, KT, T], F32R, where=a3)
            kT_lo = sb("kT_lo", [P, KT, T], F32R, where=a3)
            V_hi = sb("V_hi", [P, TT, D], F32R, where=a3)
            V_lo = sb("V_lo", [P, TT, D], F32R, where=a3)
            sg = sb("sg", [P, TT, D], where=a3)
        with ExitStack() as a4:
            hn = sb("hn", [P, TT, D], where=a4)
            hn_hi = sb("hn_hi", [P, TT, D], F32R, where=a4)
            hn_lo = sb("hn_lo", [P, TT, D], F32R, where=a4)
            gb = sb("gb", [P, D], where=a4)
            gt = sb("gt", [P, 2, CW], where=a4)
            act_s = sb("act_s", [P, 2, CW], where=a4)
            aT_hi = sb("aT_hi", [P, 2, 4, P], F32R, where=a4)
            aT_lo = sb("aT_lo", [P, 2, 4, P], F32R, where=a4)
            S = sb("S", [P, TT, P], F32R, where=a4)
            ST = sb("ST", [P, T], F32R, where=a4)
            tk = sb("tk", [P, 12, TT, E], where=a4)
            tv = sb("tv", [P, 8, TT], where=a4)
            posb = sb("posb", [P, TT, 2 * E + 1], where=a4)
            combt = sb("combt", [P, TT, 2 * E + 1], where=a4)
            pcol = sb("pcol", [P, TT], where=a4)
            ccol = sb("ccol", [P, TT], where=a4)
        probs = [rows3[:, i * 12 * P:(i + 1) * 12 * P].rearrange("p (a k) -> p a k", k=P) for i in range(2)]
        pT_hi = hT_hi[:].rearrange("p k t -> p (k t)")[:, 0:12 * P].rearrange("p (a k) -> p a k", k=P)
        pT_lo = hT_lo[:].rearrange("p k t -> p (k t)")[:, 0:12 * P].rearrange("p (a k) -> p a k", k=P)
        qf = xpad[:, :, 0:T]
        hTf_hi, hTf_lo = (h[:].rearrange("p k t -> p (k t)") for h in (hT_hi, hT_lo))
        xg_hi, xg_lo = (h[:, 0:D].rearrange("p (k s) -> p k s", s=P) for h in (hTf_hi, hTf_lo))
        y_hi, y_lo = hTf_hi[:, D:2 * D], hTf_lo[:, D:2 * D]

        landed = [sem(f"landed{i}") for i in range(RR)]
        hi_done = sem("hi_done")
        lo_done = sem("lo_done")
        used = sem("used")
        x_in, par_in, wax_in, small_in, gb_in = (sem(s) for s in ("x_in", "par_in", "wax_in", "small_in", "gb_in"))
        consts, pow_done, gx_done = sem("consts"), sem("pow_done"), sem("gx_done")
        par_T, xn_T, gate_r, gate_i, f_mm, f_cum, f_T, qk_T, scored, probs_T, pv_done, o_T, routed, slotted = (
            sem(s) for s in ("par_T", "xn_T", "gate_r", "gate_i", "f_mm", "f_cum", "f_T", "qk_T", "scored",
                             "probs_T", "pv_done", "o_T", "routed", "slotted"))
        sumsq, h_hi, lam_exp, small_hi, xp_in, gelu, sig_r, sig_i, a_exp, th_done, mult_done, z_hi = (
            sem(s) for s in ("sumsq", "h_hi", "lam_exp", "small_hi", "xp_in", "gelu", "sig_r", "sig_i", "a_exp",
                             "th_done", "mult_done", "z_hi"))
        f_silu, f_ahi, squared, f_exp, fT_hi_done, qk_hi, v_hi, g_sig, exped, pT_hi_done, o_hi, w_exp, hn_hi_done = (
            sem(s) for s in ("f_silu", "f_ahi", "squared", "f_exp", "fT_hi_done", "qk_hi", "v_hi", "g_sig",
                             "exped", "pT_hi_done", "o_hi", "w_exp", "hn_hi_done"))
        chain, par_done, ms_done, xn_done, h_lo, conv_done, lam_neg, lam_done, small_lo, m2_done, z_done, z_lo = (
            sem(s) for s in ("chain", "par_done", "ms_done", "xn_done", "h_lo", "conv_done", "lam_neg", "lam_done",
                             "small_lo", "m2_done", "z_done", "z_lo"))
        x_done, f_act, f_alo, f_neg, f_log, f_negF, fT_lo_done, ssq_done, qn_done, qk_lo, v_lo, nmax = (
            sem(s) for s in ("x_done", "f_act", "f_alo", "f_neg", "f_log", "f_negF", "fT_lo_done", "ssq_done",
                             "qn_done", "qk_lo", "v_lo", "nmax"))
        pT_lo_done, o_done, o_lo, hn_done, hn_lo_done, picked, w_diff, blocks, y_zero, edges, qkg_done, const_r = (
            sem(s) for s in ("pT_lo_done", "o_done", "o_lo", "hn_done", "hn_lo_done", "picked", "w_diff", "blocks",
                             "y_zero", "edges", "qkg_done", "const_r"))
        m_scat, m_T, m_TS, m_gat = (sem(s) for s in ("m_scat", "m_T", "m_TS", "m_gat"))
        m_yhi, m_silu, m_thi, m_ST, m_xh = (sem(s) for s in ("m_yhi", "m_silu", "m_thi", "m_ST", "m_xh"))
        m_ylo, m_acc, m_act, m_tlo, m_S, m_xl, m_col, m_fin = (
            sem(s) for s in ("m_ylo", "m_acc", "m_act", "m_tlo", "m_S", "m_xl", "m_col", "m_fin"))
        out_done = sem("out_done")

        def unit_of(w, rows, col):
            return w[rows * P:(rows + UK) * P, col * CW:(col + 1) * CW].rearrange("(k p) n -> p k n", p=P)

        def swiglu_units(gate, up, dn):
            def d(c):
                return [(dn, c * UK, j) for j in range(2)]
            for c in range(FC):
                yield from [(gate, 0, c), (gate, UK, c), (up, 0, c), (up, UK, c)]
                if c:
                    yield from d(c - 1)
            yield from d(FC - 1)

        def front_units():
            for col in (2, 3, 0, 1):
                for rows in (0, UK):
                    yield lru_w_in[0], rows, col
            for col in (0, 1):
                for rows in (0, UK):
                    yield lru_w_out[0], rows, col
            yield from swiglu_units(ffn_w_gate[0], ffn_w_up[0], ffn_w_down[0])
            for col in range(8):
                for rows in (0, UK):
                    yield fox_w_in[0], rows, col
            for col in (0, 1):
                for rows in (0, UK):
                    yield fox_w_out[0], rows, col

        expert_w = [w.rearrange("a e d f -> (a e) d f") for w in (moe_w_gate, moe_w_up, moe_w_down)]
        block = ctx.enter_context(nc.Block())

        @block.sync
        def _(sp):
            sp.dma_start(X[:], x[0].rearrange("(t p) d -> p t d", p=P)).then_inc(x_in, 16)
            for n, (w, rows, col) in enumerate(front_units()):
                if n >= RR:
                    sp.wait_ge(lo_done, n - RR + 1)
                sp.dma_start(raw[:, n % RR], unit_of(w, rows, col)).then_inc(landed[n % RR], 16)
                if n == 1:
                    sp.dma_start(wax[:, 0], lru_w_a[0].rearrange("h i j -> i h j")).then_inc(wax_in, 16)
                    sp.dma_start(wax[:, 1], lru_w_x[0].rearrange("h i j -> i h j")).then_inc(wax_in, 16)

            def expert_loads(b, e):
                for i, (w, rows, col) in enumerate(swiglu_units(*expert_w)):
                    n = N_MOE + i
                    sp.wait_ge(lo_done, at(n - RR + 1, FFN_UNITS, b))
                    src = w[bass.ds(e, 1), rows * P:(rows + UK) * P, col * CW:(col + 1) * CW]
                    sp.dma_start(raw[:, n % RR], src.rearrange("o (k p) n -> p (o k) n", p=P)
                                 ).then_inc(landed[n % RR], 16)

            with sp.Fori(0, E) as b:
                expert_loads(b, b)
            sp.wait_ge(blocks, 1)
            nblk = sp.value_load(nblk_i[0:1, 0:1], min_val=E, max_val=2 * E)
            with sp.If(nblk > E):
                with sp.Fori(E, 2 * E) as b:
                    expert_loads(b, b - E)
            sp.wait_ge(m_fin, 1)
            sp.dma_start(out[0].rearrange("(t p) d -> p t d", p=P), X[:]).then_inc(out_done, 16)
            sp.wait_ge(out_done, 16)

        @block.gpsimd
        def _(pool):
            pool.memset(ident[:], 0.0).then_inc(consts, 1)
            pool.memset(upper[:], 1.0).then_inc(consts, 1)
            pool.memset(mask[:], 0.0).then_inc(consts, 1)
            pool.memset(ones[:], 1.0).then_inc(consts, 1)
            pool.memset(mhalf[:], -0.5).then_inc(consts, 1)
            pool.iota(iota[:], [[1, P]], base=1, channel_multiplier=0,
                      allow_small_or_imprecise_dtypes=True).then_inc(consts, 1)
            pool.wait_ge(consts, 6)
            pool.affine_select(out=ident[:], in_=ident[:], compare_op=ALU.not_equal, fill=1.0, base=0,
                               pattern=[[-1, P]], channel_multiplier=1).then_inc(consts, 1)
            pool.affine_select(out=upper[:], in_=upper[:], compare_op=ALU.is_ge, fill=0.0, base=0,
                               pattern=[[1, P]], channel_multiplier=-1).then_inc(consts, 1)
            pool.affine_select(out=mask[:], in_=mask[:], compare_op=ALU.is_ge, fill=NEG, base=0,
                               pattern=[[-1, P]], channel_multiplier=1).then_inc(consts, 1)
            pool.memset(nFT_hi[:].bitcast(F32), 0.0).then_inc(consts, 1)
            pool.memset(nFT_lo[:].bitcast(F32), 0.0).then_inc(consts, 1)
            def rows_of(w):
                return w.rearrange("a (c p) -> (a c) p", p=P)
            for r0, n, src in ((PAR_CONVW, 32, rows_of(lru_conv_w[0])), (PAR_CONVB, 8, rows_of(lru_conv_b)),
                               (PAR_BA, 8, rows_of(lru_b_a)), (PAR_BX, 8, rows_of(lru_b_x)),
                               (PAR_LAM, 8, rows_of(lru_log_lambda)), (PAR_MIX, 16, rows_of(norm_mix)),
                               (PAR_FFN, 16, rows_of(norm_ffn))):
                pool.dma_start(par_rows[r0:r0 + n, :], src).then_inc(par_in, 16)
            pool.dma_start(wf[:], fox_w_in[0][:, 4 * D:4 * D + H].rearrange("(k p) h -> p k h", p=P)
                           ).then_inc(small_in, 16)
            pool.dma_start(rw[:], moe_router[0].rearrange("(k p) e -> p k e", p=P)).then_inc(small_in, 16)
            pool.dma_start(bf[:], fox_b_f[0].partition_broadcast(P)).then_inc(small_in, 16)
            for half in range(2):
                for i, g in enumerate((fox_q_gain, fox_k_gain)):
                    pool.dma_start(qkg[half * HD:(half + 1) * HD, i:i + 1], g.rearrange("a d -> d a")
                                   ).then_inc(small_in, 16)

            def rms_pow(r):
                pool.wait_ge(ms_done, r + 1)
                pool.tensor_tensor(rstd[:, 2 * r:2 * r + 2], ms[:, 2 * r:2 * r + 2], mhalf[:, 0:2],
                                   ALU.pow).then_inc(pow_done, 1)
            rms_pow(0)
            for g in range(4):
                pool.wait_ge(sig_i, 2 * g + 2)
                pool.tensor_tensor(gi[:, 2 * g:2 * g + 2], gi[:, 2 * g:2 * g + 2], xc[:, 2 * g:2 * g + 2],
                                   ALU.mult).then_inc(gx_done, 1)
            rms_pow(1)
            rms_pow(2)
            for cc in range(4):
                pool.wait_ge(ssq_done, 2 * cc + 2)
                pool.tensor_tensor(ssq[:, 2], ssq[:, 1], mhalf[:], ALU.pow).then_inc(pow_done, 1)
            pool.wait_ge(o_done, 32)
            pool.dma_start(gb[:], norm_ffn[1].partition_broadcast(P)).then_inc(gb_in, 16)
            pool.wait_ge(ms_done, 4)
            pool.tensor_tensor(rstd[:, 6:8], ms[:, 6:8], mhalf[:, 0:2], ALU.pow).then_inc(pow_done, 1)

        @block.scalar
        def _(act):
            nxt = [0]

            def hi_to(n, b=None):
                first = 0 if b is None else N_MOE
                last = N_MOE - 1 if b is None else N_MOE + FFN_UNITS - 1
                while first + nxt[0] <= min(first + n, last):
                    m = first + nxt[0]
                    act.wait_ge(landed[m % RR], at(16 * (m // RR + 1), 16 * FFN_UNITS // RR, b))
                    if m >= HR:
                        act.wait_ge(used, at(m - HR + 1, FFN_UNITS, b))
                    nc.scalar.activation(whi[:, m % HR], raw[:, m % RR], ACT.Copy).then_inc(hi_done, 1)
                    nxt[0] += 1

            def squares(r):
                for t in range(TT):
                    if r or t:
                        act.wait_ge(sumsq, 2 * r + t)
                    nc.scalar.activation(junk[:], X[:, t, :], ACT.Square, accum_out=ss[:, 2 * r + t:2 * r + t + 1]
                                         ).then_inc(sumsq, 1)

            def transposed_hi(r):
                for k in range(KT):
                    act.wait_ge(xn_T, 4 * r + k // 2 + 1)
                    nc.scalar.activation(hT_hi[:, k], ps[:, k // 2, (k % 2) * T:(k % 2 + 1) * T], ACT.Copy,
                                         scale=par[:, GAIN[r] + k:GAIN[r] + k + 1]).then_inc(h_hi, 1)

            act.wait_ge(x_in, 16)
            squares(0)
            hi_to(2)
            act.wait_ge(par_done, 1)
            transposed_hi(0)
            act.wait_ge(lam_neg, 1)
            nc.scalar.activation(lt[:, 1], lt[:, 0], ACT.Exp).then_inc(lam_exp, 1)
            act.wait_ge(small_in, 16 * 7)
            nc.scalar.activation(wf_hi[:], wf[:], ACT.Copy).then_inc(small_hi, 1)
            nc.scalar.activation(rw_hi[:], rw[:], ACT.Copy).then_inc(small_hi, 1)
            for ch in range(2):
                hi_to(2 * ch + 3)
                act.wait_ge(used, 2 * ch + 2)
                for i in range(2):
                    bank = 4 + 2 * ch + i
                    nc.scalar.activation(xpad[:, 4 * ch + 2 * i:4 * ch + 2 * i + 2, CONV - 1:],
                                         ps[:, bank].rearrange("p (c t) -> p c t", t=T), ACT.Copy).then_inc(xp_in, 1)
            for ch in range(2):
                hi_to(2 * ch + 7)
                act.wait_ge(used, 2 * ch + 6)
                nc.scalar.activation(yb[:, 4 * ch:4 * ch + 4].rearrange("p c t -> p (c t)"),
                                     ps[:, 2 * ch:2 * ch + 2].rearrange("p b n -> p (b n)"),
                                     ACT.Gelu_apprx_tanh).then_inc(gelu, 1)
            hi_to(10)
            for ready, done, dst, par0, bank0 in ((gate_r, sig_r, rg, PAR_BA, 4), (gate_i, sig_i, gi, PAR_BX, 0)):
                for c in range(KT):
                    act.wait_ge(ready, 2 * (c // 2) + 2)
                    nc.scalar.activation(dst[:, c], ps[:, bank0 + c // 2, (c % 2) * T:(c % 2 + 1) * T], ACT.Sigmoid,
                                         bias=par[:, par0 + c:par0 + c + 1]).then_inc(done, 1)
            act.wait_ge(lam_done, 2)
            act.wait_ge(sig_r, KT)
            for c in range(KT):
                nc.scalar.activation(av[:, c], rg[:, c], ACT.Exp, scale=lt[:, 4, c:c + 1]).then_inc(a_exp, 1)
                nc.scalar.activation(rg[:, c], rg[:, c], ACT.Tanh, scale=lt[:, 5, c:c + 1]).then_inc(th_done, 1)
            for g in range(2):
                act.wait_ge(m2_done, g + 1)
                nc.scalar.activation(qf[:, 4 * g:4 * g + 4], qf[:, 4 * g:4 * g + 4], ACT.Sqrt).then_inc(mult_done, 1)
            for g in range(2):
                act.wait_ge(z_done, g + 1)
                nc.scalar.activation(hT_hi[:, 4 * g:4 * g + 4], yb[:, 4 * g:4 * g + 4], ACT.Copy).then_inc(z_hi, 1)
            hi_to(N_FFN + 1)

            act.wait_ge(x_done, 2)
            squares(1)
            transposed_hi(1)
            for c in range(FC):
                hi_to(N_FFN + base(c) + 3)
                act.wait_ge(used, N_FFN + base(c) + 2)
                if c:
                    act.wait_ge(f_alo, c)
                nc.scalar.activation(sil[:].rearrange("p c t -> p (c t)"),
                                     ps[:, 0:2].rearrange("p b n -> p (b n)"), ACT.Silu).then_inc(f_silu, 1)
                hi_to(N_FFN + base(c) + 6)
                act.wait_ge(f_act, c + 1)
                nc.scalar.activation(fT_hi[:, c % 2], sil[:], ACT.Copy).then_inc(f_ahi, 1)
            hi_to(N_FOX + 1)

            act.wait_ge(x_done, 4)
            squares(2)
            transposed_hi(2)
            for cc in range(8):
                m = N_FOX + 2 * cc + 1
                bank = 2 * (cc % 4)
                hi_to(m + 2)
                act.wait_ge(used, m + 1)
                both = ps[:, bank:bank + 2].rearrange("p b n -> p (b n)")
                if cc < 4:
                    if cc:
                        act.wait_ge(ssq_done, 2 * cc)
                    nc.scalar.activation(junk[:], both, ACT.Square).then_inc(squared, 1)
                elif cc < 6:
                    nc.scalar.activation(V_hi[:, :, (cc - 4) * CW:(cc - 3) * CW], ps[:, bank:bank + 2], ACT.Copy
                                         ).then_inc(v_hi, 1)
                else:
                    nc.scalar.activation(sg[:, :, (cc - 6) * CW:(cc - 5) * CW], ps[:, bank:bank + 2], ACT.Sigmoid
                                         ).then_inc(g_sig, 1)
                if cc == 0:
                    act.wait_ge(f_neg, 1)
                    nc.scalar.activation(fx[:, 2], fx[:, 1], ACT.Exp).then_inc(f_exp, 1)
                if cc == 2:
                    act.wait_ge(f_T, 1)
                    nc.scalar.activation(nFT_hi[0:H, :], ps[0:H, 7, P:P + T], ACT.Copy).then_inc(fT_hi_done, 1)
                if 1 <= cc <= 4:
                    q = cc - 1
                    dst = (qT_hi if q < 2 else kT_hi)[:, 4 * (q % 2):4 * (q % 2) + 4]
                    act.wait_ge(qk_T, q + 1)
                    nc.scalar.activation(dst.rearrange("p c t -> p (c t)"),
                                         ps[:, 2 * q:2 * q + 2].rearrange("p b n -> p (b n)"), ACT.Copy,
                                         scale=qkg[:, q // 2:q // 2 + 1]).then_inc(qk_hi, 1)
            hi_to(N_FOXOUT + 2)

            def exps(i):
                a = 3 * (i % 2)
                act.wait_ge(nmax, 2 * i + 2)
                for j in range(4):
                    nc.scalar.activation(probs[i % 2][:, j], ps[:, a, j * P:(j + 1) * P], ACT.Exp,
                                         bias=nm[:, i, j:j + 1], accum_out=sm[:, i, j:j + 1]).then_inc(exped, 1)
                for j in range(4):
                    nc.scalar.activation(probs[i % 2][:, 4 + 2 * j:6 + 2 * j].rearrange("p a k -> p (a k)"),
                                         ps[:, a + 1 + j // 2, (j % 2) * T:(j % 2 + 1) * T], ACT.Exp,
                                         bias=nm[:, i, 4 + j:5 + j], accum_out=sm[:, i, 4 + j:5 + j]
                                         ).then_inc(exped, 1)
            exps(0)
            for i in range(4):
                if i < 3:
                    exps(i + 1)
                if i:
                    act.wait_ge(pv_done, i)
                for r in range(3):
                    act.wait_ge(probs_T, 3 * i + r + 1)
                    nc.scalar.activation(pT_hi[:, 4 * r:4 * r + 4].rearrange("p a k -> p (a k)"),
                                         ps[:, 3 * (i % 2) + r], ACT.Copy).then_inc(pT_hi_done, 1)
            for r in range(4):
                act.wait_ge(o_T, r + 1)
                nc.scalar.activation(qT_hi[:, 2 * r:2 * r + 2].rearrange("p k t -> p (k t)"), ps[:, r], ACT.Copy
                                     ).then_inc(o_hi, 1)
            hi_to(N_MOE - 1)

            act.wait_ge(x_done, 6)
            squares(3)
            transposed_hi(3)
            for t in range(TT):
                act.wait_ge(hn_done, t + 1)
                nc.scalar.activation(hn_hi[:, t], hn[:, t], ACT.Copy).then_inc(hn_hi_done, 1)
            act.wait_ge(w_diff, 1)
            nc.scalar.activation(tv[:, 3], tv[:, 2], ACT.Exp).then_inc(w_exp, 1)

            def gathered_hi(count):
                act.wait_ge(m_gat, count)
                nc.scalar.activation(xg_hi[:].rearrange("p k s -> p (k s)"),
                                     ps[:, 2:4].rearrange("p b n -> p (b n)"), ACT.Copy).then_inc(m_xh, 1)
            gathered_hi(1)
            nc.scalar.activation(junk[:, 0:2], junk[:, 0:2], ACT.Copy).then_inc(m_silu, 1)

            def y_to_hi(b):
                act.wait_ge(y_zero, 1)
                act.wait_ge(used, at(N_MOE, FFN_UNITS, b))
                nc.scalar.activation(y_hi[:], ps[:, 0:2].rearrange("p b n -> p (b n)"), ACT.Copy).then_inc(m_yhi, 1)

            def act_T_hi(b, c):
                act.wait_ge(m_T, at(c + 1, FC, b))
                nc.scalar.activation(aT_hi[:, c % 2].rearrange("p a s -> p (a s)"), ps[:, 6], ACT.Copy
                                     ).then_inc(m_thi, 1)

            act.wait_ge(blocks, 1)
            nblk = act.value_load(nblk_i[0:1, 0:1], min_val=E, max_val=2 * E)
            with act.Fori(0, nblk) as b:
                nxt[0] = 0
                hi_to(1, b)
                y_to_hi(b)
                for c in range(FC):
                    if c == 1:
                        hi_to(6, b)
                        act.wait_ge(m_TS, at(1, 1, b))
                        nc.scalar.activation(ST[:], ps[:, 7, 0:T], ACT.Copy).then_inc(m_ST, 1)
                        act_T_hi(b, 0)
                    hi_to(base(c) + 3, b)
                    act.wait_ge(used, at(N_MOE + base(c) + 2, FFN_UNITS, b))
                    act.wait_ge(m_act, at(max(c, 1), FC, b))
                    nc.scalar.activation(gt[:, c % 2], ps[:, 2 + c % 2], ACT.Silu).then_inc(m_silu, 1)
                    if c:
                        hi_to(base(c) + 6, b)
                        act_T_hi(b, c)
                hi_to(FFN_UNITS - 1, b)
                gathered_hi(at(2, 1, b))
            y_to_hi(nblk)

        @block.tensor
        def _(pe):
            mm = nc.tensor.matmul

            def tokens_unit(m, b, src, k0, tiles, dst, first, last):
                pe.wait_ge(lo_done, at(m + 1, FFN_UNITS, b))
                for k in range(UK):
                    for t in range(tiles):
                        hi, lo = src(k0 + k, t)
                        mm(dst(t), hi, whi[:, m % HR, k], start=first and k == 0, stop=False)
                        mm(dst(t), hi, wlo[:, m % HR, k], start=False, stop=False)
                        ins = mm(dst(t), lo, whi[:, m % HR, k], start=False, stop=last and k == UK - 1)
                ins.then_inc(used, 1)

            def weights_unit(m, bank, half):
                pe.wait_ge(lo_done, m + 1)
                for c in range(4):
                    dst = ps[:, bank + c // 2, (c % 2) * T:(c % 2 + 1) * T]
                    for k in range(UK):
                        kk = half * UK + k
                        wh, wl = (w[:, m % HR, k, c * P:(c + 1) * P] for w in (whi, wlo))
                        mm(dst, wh, hT_hi[:, kk], start=half == 0 and k == 0 and c % 2 == 0, stop=False,
                           skip_group_check=True)
                        mm(dst, wh, hT_lo[:, kk], start=False, stop=False, skip_group_check=True)
                        ins = mm(dst, wl, hT_hi[:, kk], start=False, stop=half == 1 and k == UK - 1,
                                 skip_group_check=True)
                ins.then_inc(used, 1)

            def transposes(src, done):
                for bank in range(4):
                    for k in range(2):
                        for t in range(TT):
                            kk = 2 * bank + k
                            ins = nc.tensor.transpose(ps[:, bank, k * T + t * P:k * T + (t + 1) * P],
                                                      src[:, t, kk * P:(kk + 1) * P], ident[:])
                    ins.then_inc(done, 1)

            def of_hT(k, t):
                return hT_hi[:, k, t * P:(t + 1) * P], hT_lo[:, k, t * P:(t + 1) * P]

            pe.wait_ge(consts, 9)
            pe.wait_ge(par_in, 16 * 7)
            nc.tensor.transpose(ps[:, 7, 0:96], par_rows[:], ident[0:96, 0:96]).then_inc(par_T, 1)
            pe.wait_ge(xn_done, 2)
            transposes(xn, xn_T)
            for n in range(8):
                if n < 2:
                    pe.wait_ge(h_lo, 4 * n + 4)
                if n == 0:
                    pe.wait_ge(par_done, 1)
                weights_unit(n, (4, 6, 0, 2)[n // 2], n % 2)
            pe.wait_ge(wax_in, 32)
            for g, (bank0, done) in enumerate(((4, gate_r), (0, gate_i))):
                for c in range(KT):
                    if g == 0:
                        pe.wait_ge(conv_done, c + 1)
                    elif c % 4 == 0:
                        pe.wait_ge(gelu, 2)
                    mm(ps[:, bank0 + c // 2, (c % 2) * T:(c % 2 + 1) * T], wax[:, g, c], xc[:, c],
                       start=c % 2 == 0, stop=True, skip_group_check=True).then_inc(done, 1)
            for i in range(4):
                if i < 2:
                    pe.wait_ge(z_lo, i + 1)
                tokens_unit(N_IN + i, None, of_hT, UK * (i % 2), TT, lambda t: ps[:, 2 * (i // 2) + t],
                            i % 2 == 0, i % 2 == 1)

            pe.wait_ge(xn_done, 4)
            transposes(xn, xn_T)

            def ffn_down(c):
                pe.wait_ge(f_alo, c + 1)
                for j in range(2):
                    tokens_unit(N_FFN + down(c) + j, None,
                                lambda k, t: (fT_hi[:, c % 2, k, t * P:(t + 1) * P],
                                              fT_lo[:, c % 2, k, t * P:(t + 1) * P]),
                                0, TT, lambda t: ps[:, 4 + 2 * j + t], c == 0, c == FC - 1)

            for c in range(FC):
                n = N_FFN + base(c)
                for half in range(2):
                    if c == 0:
                        pe.wait_ge(h_lo, 8 + 4 * half + 4)
                    elif half == 0:
                        pe.wait_ge(f_silu, c)
                    weights_unit(n + half, 0, half)
                if c:
                    pe.wait_ge(f_act, c)
                for half in range(2):
                    weights_unit(n + 2 + half, 2, half)
                if c:
                    ffn_down(c - 1)
            ffn_down(FC - 1)

            pe.wait_ge(xn_done, 6)
            transposes(xn, xn_T)

            def qk_transposes(q):
                pe.wait_ge(qn_done, q + 1)
                src = xn[:, q % 2].rearrange("p (t n) -> p t n", t=TT)
                for c in range(4):
                    for t in range(TT):
                        ins = nc.tensor.transpose(ps[:, 2 * q + c // 2, (c % 2) * T + t * P:(c % 2) * T + (t + 1) * P],
                                                  src[:, t, c * P:(c + 1) * P], ident[:])
                ins.then_inc(qk_T, 1)

            for cc in range(8):
                if cc == 3:
                    pe.wait_ge(fT_lo_done, 1)
                if cc >= 4:
                    pe.wait_ge(qk_lo, cc - 3)
                for half in range(2):
                    if cc == 0:
                        pe.wait_ge(h_lo, 16 + 4 * half + 4)
                    tokens_unit(N_FOX + 2 * cc + half, None, of_hT, UK * half, TT,
                                lambda t: ps[:, 2 * (cc % 4) + t], half == 0, half == 1)
                if cc == 0:
                    pe.wait_ge(small_lo, 2)
                    for t in range(TT):
                        for k in range(KT):
                            hi, lo = of_hT(k, t)
                            for a, w in ((hi, wf_hi), (hi, wf_lo), (lo, wf_hi)):
                                ins = mm(ps[:, 7, t * H:(t + 1) * H], a, w[:, k], start=t == 0 and k == 0 and w is wf_hi and a is hi,
                                         stop=k == KT - 1 and a is lo, skip_group_check=True)
                    ins.then_inc(f_mm, 1)
                if cc == 1:
                    pe.wait_ge(f_log, 1)
                    mm(ps[:, 7, 64:64 + H], upper[:], fx[:, 7, 0], start=True, stop=True, skip_group_check=True)
                    mm(ps[:, 7, 64 + H:64 + 2 * H], ones[:], fx[:, 7, 0], start=False, stop=False, skip_group_check=True)
                    mm(ps[:, 7, 64 + H:64 + 2 * H], upper[:], fx[:, 7, 1], start=False, stop=True,
                       skip_group_check=True).then_inc(f_cum, 1)
                if cc == 2:
                    pe.wait_ge(f_negF, 1)
                    for t in range(TT):
                        ins = nc.tensor.transpose(ps[0:H, 7, P + t * P:P + (t + 1) * P], nF[:, t], ident[:])
                    ins.then_inc(f_T, 1)
                if 1 <= cc <= 4:
                    qk_transposes(cc - 1)

            def scores(i):
                s, p = i // 2, i % 2
                rows = slice(p * HD, (p + 1) * HD)
                for qt in range(TT):
                    for part in range(1 + qt):
                        bank = 3 * (i % 2) + qt + part
                        js = range(4) if qt == 0 else range(2 * part, 2 * part + 2)
                        w = (qt + 1) * P
                        for n, j in enumerate(js):
                            h = 8 * s + 2 * j + p
                            dst = ps[:, bank, n * w:(n + 1) * w]
                            pick = ident_r[:, h:h + 1].to_broadcast([P, P])
                            mm(dst, pick, nFT_hi[:, 0:w], start=n == 0, stop=False, skip_group_check=True)
                            mm(dst, pick, nFT_lo[:, 0:w], start=False, stop=False, skip_group_check=True)
                            mm(ps[:, bank, (n + 1) * w - P:(n + 1) * w], ident_r[:], mask_r[:], start=False,
                               stop=False, skip_group_check=True)
                        for n, j in enumerate(js):
                            c = 4 * s + j
                            dst = ps[:, bank, n * w:(n + 1) * w]
                            qs = slice(qt * P, (qt + 1) * P)
                            mm(dst, qT_hi[rows, c, qs], kT_hi[rows, c, 0:w], start=False, stop=False,
                               skip_group_check=True)
                            mm(dst, qT_hi[rows, c, qs], kT_lo[rows, c, 0:w], start=False, stop=False,
                               skip_group_check=True)
                            ins = mm(dst, qT_lo[rows, c, qs], kT_hi[rows, c, 0:w], start=False, stop=True,
                                     skip_group_check=True)
                ins.then_inc(scored, 1)

            pe.wait_ge(v_lo, 2)
            pe.wait_ge(g_sig, 2)
            pe.wait_ge(qk_lo, 4)
            pe.wait_ge(const_r, 2)
            scores(0)
            for i in range(4):
                if i < 3:
                    scores(i + 1)
                s, p = i // 2, i % 2
                pe.wait_ge(exped, 8 * i + 8)
                for r in range(3):
                    for a in range(4):
                        ins = nc.tensor.transpose(ps[:, 3 * (i % 2) + r, a * P:(a + 1) * P],
                                                  probs[i % 2][:, 4 * r + a], ident[:])
                    ins.then_inc(probs_T, 1)
                pe.wait_ge(pT_lo_done, 3 * i + 3)
                if i >= 2:
                    pe.wait_ge(o_done, 8 * (i - 1))
                for qt in range(TT):
                    for j in range(4):
                        h = 8 * s + 2 * j + p
                        dst = ps[:, 6 + i % 2, (4 * qt + j) * HD:(4 * qt + j + 1) * HD]
                        for kt in range(qt + 1):
                            blk = j if qt == 0 else 4 + 2 * j + kt
                            vs = slice(h * HD, (h + 1) * HD)
                            mm(dst, pT_hi[:, blk], V_hi[:, kt, vs], start=qt == 0 and j == 0, stop=False,
                               skip_group_check=True)
                            mm(dst, pT_hi[:, blk], V_lo[:, kt, vs], start=False, stop=False, skip_group_check=True)
                            ins = mm(dst, pT_lo[:, blk], V_hi[:, kt, vs], start=False, stop=kt == qt,
                                     skip_group_check=True)
                ins.then_inc(pv_done, 1)
            pe.wait_ge(o_done, 32)
            transposes(sg, o_T)
            for i in range(4):
                if i < 2:
                    pe.wait_ge(o_lo, 2 * i + 2)
                tokens_unit(N_FOXOUT + i, None,
                            lambda k, t: (qT_hi[:, k, t * P:(t + 1) * P], qT_lo[:, k, t * P:(t + 1) * P]),
                            UK * (i % 2), TT, lambda t: ps[:, 4 + 2 * (i // 2) + t], i % 2 == 0, i % 2 == 1)

            pe.wait_ge(xn_done, 8)
            transposes(xn, xn_T)
            pe.wait_ge(h_lo, 32)
            for t in range(TT):
                for k in range(KT):
                    hi, lo = of_hT(k, t)
                    for n, (a, w) in enumerate(((hi, rw_hi), (hi, rw_lo), (lo, rw_hi))):
                        ins = mm(ps[:, 7, t * E:(t + 1) * E], a, w[:, k], start=t == 0 and k == 0 and n == 0,
                                 stop=k == KT - 1 and n == 2, skip_group_check=True)
            ins.then_inc(routed, 1)
            pe.wait_ge(picked, 1)
            sel = tk[:, 9]
            mm(ps[:, 7, 32:32 + E], upper[:], sel[:, 0], start=True, stop=True, skip_group_check=True)
            mm(ps[:, 7, 40:40 + E], ones[:], sel[:, 0], start=False, stop=False, skip_group_check=True)
            mm(ps[:, 7, 40:40 + E], upper[:], sel[:, 1], start=False, stop=True, skip_group_check=True)
            mm(ps[:, 7, 64:64 + E], ones[:], sel[:, 0], start=False, stop=False, skip_group_check=True)
            mm(ps[:, 7, 64:64 + E], ones[:], sel[:, 1], start=False, stop=True,
               skip_group_check=True).then_inc(slotted, 1)

            def gather(count):
                pe.wait_ge(m_S, count)
                for q, h in enumerate((hn_hi, hn_lo)):
                    for k in range(KT):
                        for t in range(TT):
                            ins = mm(ps[:, 2 + 2 * q + k // 4, (k % 4) * P:(k % 4 + 1) * P],
                                     h[:, t, k * P:(k + 1) * P], S[:, t], start=k % 4 == 0 and t == 0, stop=t == 1,
                                     skip_group_check=True)
                ins.then_inc(m_gat, 1)

            pe.wait_ge(hn_lo_done, 2)
            gather(1)

            def scatter(b):
                pe.wait_ge(m_ylo, at(1, 1, b))
                for n, bank in enumerate((3, 5, 6, 7)):
                    t, j = n // 2, n % 2
                    for q, y in enumerate((y_hi, y_lo)):
                        ins = mm(ps[:, bank], ST[:, t * P:(t + 1) * P], y[:, j * CW:(j + 1) * CW], start=q == 0,
                                 stop=q == 1)
                ins.then_inc(m_scat, 1)

            def act_transposes(b, c):
                pe.wait_ge(m_act, at(c + 2, FC, b))
                for a in range(4):
                    ins = nc.tensor.transpose(ps[:, 6, a * P:(a + 1) * P], act_s[:, c % 2, a * P:(a + 1) * P], ident[:])
                ins.then_inc(m_T, 1)

            def moe_unit(b, i, src, k0, bank, first, last):
                tokens_unit(N_MOE + i, b, src, k0, 1, lambda t: ps[:, bank], first, last)

            def of_xg(k, t):
                return xg_hi[:, k], xg_lo[:, k]

            pe.wait_ge(blocks, 1)
            nblk = pe.value_load(nblk_i[0:1, 0:1], min_val=E, max_val=2 * E)
            with pe.Fori(0, nblk) as b:
                pe.wait_ge(m_xl, at(1, 1, b))
                for c in range(FC):
                    if c == 1:
                        pe.wait_ge(m_acc, at(2, 1, b))
                    pe.wait_ge(m_silu, at(max(c, 1), FC, b))
                    for half in range(2):
                        moe_unit(b, base(c) + half, of_xg, UK * half, 2 + c % 2, half == 0, half == 1)
                        if c == 0 and half == 1:
                            scatter(b)
                        if c == 1 and half == 0:
                            act_transposes(b, 0)
                            for t in range(TT):
                                ins = mm(ps[:, 7, t * P:(t + 1) * P], S[:, t], ident_r[:], start=t == 0, stop=True,
                                         skip_group_check=True)
                            ins.then_inc(m_TS, 1)
                    pe.wait_ge(m_act, at(max(c, 1), FC, b))
                    for half in range(2):
                        moe_unit(b, base(c) + 2 + half, of_xg, UK * half, 4 + c % 2, half == 0, half == 1)
                    for d in ([c - 1] if c else []) + ([c] if c == FC - 1 else []):
                        pe.wait_ge(m_tlo, at(d + 1, FC, b))
                        for j in range(2):
                            moe_unit(b, down(d) + j,
                                     lambda k, t: (aT_hi[:, d % 2, k], aT_lo[:, d % 2, k]), 0, j, d == 0, d == FC - 1)
                            if j == 0 and d < FC - 1:
                                act_transposes(b, d + 1)
                            if j == 1 and d == FC - 2:
                                gather(at(2, 1, b))
            pe.wait_ge(m_ST, nblk)
            scatter(nblk)

        @block.vector
        def _(dve):
            links = [0]

            def link(ins):
                links[0] += 1
                ins.then_inc(chain, 1)
                dve.wait_ge(chain, links[0])

            nxt = [0]

            def lo_to(n, b=None):
                first = 0 if b is None else N_MOE
                last = N_MOE - 1 if b is None else N_MOE + FFN_UNITS - 1
                while first + nxt[0] <= min(first + n, last):
                    m = first + nxt[0]
                    dve.wait_ge(hi_done, at(m + 1, FFN_UNITS, b))
                    nc.vector.tensor_tensor(wlo[:, m % HR], raw[:, m % RR], whi[:, m % HR].bitcast(F32),
                                            ALU.subtract).then_inc(lo_done, 1)
                    nxt[0] += 1

            def mean_squares(r):
                dve.wait_ge(sumsq, 2 * r + 2)
                nc.vector.tensor_scalar(ms[:, 2 * r:2 * r + 2], ss[:, 2 * r:2 * r + 2], 1.0 / D, EPS, ALU.mult, ALU.add
                                        ).then_inc(ms_done, 1)

            def normalise(r, count):
                dve.wait_ge(pow_done, count)
                for t in range(TT):
                    nc.vector.tensor_scalar(xn[:, t], X[:, t], rstd[:, 2 * r + t:2 * r + t + 1], None, ALU.mult
                                            ).then_inc(xn_done, 1)

            def transposed_lo(r):
                for k in range(KT):
                    dve.wait_ge(h_hi, 8 * r + 2 * (k // 2) + 2)
                    nc.vector.scalar_tensor_tensor(out=hT_lo[:, k], in0=ps[:, k // 2, (k % 2) * T:(k % 2 + 1) * T],
                                                   scalar=par[:, GAIN[r] + k:GAIN[r] + k + 1],
                                                   in1=hT_hi[:, k].bitcast(F32), op0=ALU.mult, op1=ALU.subtract
                                                   ).then_inc(h_lo, 1)

            def log1p(y, tmp):
                den, s, s2 = tmp
                link(nc.vector.tensor_scalar(den, y, 2.0, None, ALU.add))
                link(nc.vector.reciprocal(den, den))
                link(nc.vector.tensor_tensor(s, y, den, ALU.mult))
                link(nc.vector.tensor_tensor(s2, s, s, ALU.mult))
                link(nc.vector.tensor_scalar(den, s2, 1.0 / 17, None, ALU.mult))
                for odd in (15, 13, 11, 9, 7, 5, 3):
                    link(nc.vector.scalar_tensor_tensor(out=den, in0=den, scalar=1.0 / odd, in1=s2, op0=ALU.add,
                                                        op1=ALU.mult))
                link(nc.vector.scalar_tensor_tensor(out=den, in0=den, scalar=1.0, in1=s, op0=ALU.add, op1=ALU.mult))
                return den

            def add_to_x(bank, j):
                xj = X[:, :, j * CW:(j + 1) * CW]
                nc.vector.tensor_tensor(xj, ps[:, bank:bank + 2], xj, ALU.add).then_inc(x_done, 1)

            mean_squares(0)
            nc.vector.memset(xpad[:, :, 0:CONV - 1], 0.0).then_inc(edges, 1)
            normalise(0, 1)
            dve.wait_ge(par_T, 1)
            nc.vector.tensor_copy(par[:], ps[:, 7, 0:96]).then_inc(par_done, 1)
            lo_to(2)
            dve.wait_ge(par_done, 1)
            transposed_lo(0)
            lam = par[:, PAR_LAM:PAR_LAM + KT]
            nc.vector.scalar_tensor_tensor(out=lt[:, 0], in0=lam, scalar=-1.0, in1=lam, op0=ALU.mult, op1=ALU.min
                                           ).then_inc(lam_neg, 1)
            dve.wait_ge(lam_exp, 1)
            half_log = log1p(lt[:, 1], (lt[:, 2], lt[:, 3], lt[:, 4]))
            link(nc.vector.tensor_scalar(lt[:, 3], lam, -1.0, 0.0, ALU.mult, ALU.max))
            link(nc.vector.scalar_tensor_tensor(out=lt[:, 1], in0=half_log, scalar=2.0, in1=lt[:, 3], op0=ALU.mult,
                                                op1=ALU.add))
            nc.vector.tensor_scalar(lt[:, 4], lt[:, 1], -LRU_C, None, ALU.mult).then_inc(lam_done, 1)
            nc.vector.tensor_scalar(lt[:, 5], lt[:, 1], LRU_C, None, ALU.mult).then_inc(lam_done, 1)
            dve.wait_ge(edges, 1)
            for ch in range(2):
                lo_to(2 * ch + 3)
                cs = range(4 * ch, 4 * ch + 4)
                for w in range(CONV):
                    for c in cs:
                        src = xpad[:, c, w:w + T]
                        scale = par[:, PAR_CONVW + 8 * w + c:PAR_CONVW + 8 * w + c + 1]
                        if w == 0:
                            dve.wait_ge(xp_in, c // 2 + 1)
                            ins = nc.vector.tensor_scalar(xc[:, c], src, scale, par[:, PAR_CONVB + c:PAR_CONVB + c + 1],
                                                          ALU.mult, ALU.add)
                        else:
                            ins = nc.vector.scalar_tensor_tensor(out=xc[:, c], in0=src, scalar=scale, in1=xc[:, c],
                                                                 op0=ALU.mult, op1=ALU.add)
                        if w == CONV - 1:
                            ins.then_inc(conv_done, 1)
                        elif c == cs[-1]:
                            link(ins)
            lo_to(9)
            for g in range(2):
                q = qf[:, 4 * g:4 * g + 4]
                dve.wait_ge(a_exp, 4 * g + 4)
                link(nc.vector.tensor_tensor(q, av[:, 4 * g:4 * g + 4], av[:, 4 * g:4 * g + 4], ALU.mult))
                dve.wait_ge(th_done, 4 * g + 4)
                nc.vector.scalar_tensor_tensor(out=q, in0=q, scalar=1.0, in1=rg[:, 4 * g:4 * g + 4], op0=ALU.add,
                                               op1=ALU.mult).then_inc(m2_done, 1)
            for g in range(2):
                cs = slice(4 * g, 4 * g + 4)
                dve.wait_ge(mult_done, g + 1)
                dve.wait_ge(gx_done, 2 * g + 2)
                link(nc.vector.tensor_tensor(gi[:, cs], qf[:, cs], gi[:, cs], ALU.mult))
                for c in range(4 * g, 4 * g + 4):
                    ins = nc.vector.tensor_tensor_scan(xc[:, c], av[:, c], gi[:, c], 0.0, ALU.mult, ALU.add)
                link(ins)
                dve.wait_ge(gelu, 2)
                nc.vector.tensor_tensor(yb[:, cs], xc[:, cs], yb[:, cs], ALU.mult).then_inc(z_done, 1)
            for g in range(2):
                cs = slice(4 * g, 4 * g + 4)
                dve.wait_ge(z_hi, g + 1)
                nc.vector.tensor_tensor(hT_lo[:, cs], yb[:, cs], hT_hi[:, cs].bitcast(F32), ALU.subtract
                                        ).then_inc(z_lo, 1)
            dve.wait_ge(small_hi, 2)
            nc.vector.tensor_tensor(wf_lo[:], wf[:], wf_hi[:].bitcast(F32), ALU.subtract).then_inc(small_lo, 1)
            nc.vector.tensor_tensor(rw_lo[:], rw[:], rw_hi[:].bitcast(F32), ALU.subtract).then_inc(small_lo, 1)
            dve.wait_ge(consts, 11)
            nc.vector.tensor_copy(ident_r[:], ident[:]).then_inc(const_r, 1)
            nc.vector.tensor_copy(mask_r[:], mask[:]).then_inc(const_r, 1)
            nc.vector.tensor_scalar(qkg[:, 0:1], qkg[:, 0:1], float(HD) ** -0.5, None, ALU.mult).then_inc(qkg_done, 1)
            for j in range(2):
                lo_to(N_IN + 2 * j + 3)
                dve.wait_ge(used, N_IN + 2 * j + 2)
                add_to_x(2 * j, j)

            dve.wait_ge(x_done, 2)
            mean_squares(1)
            normalise(1, 2)
            transposed_lo(1)
            for c in range(FC):
                lo_to(N_FFN + base(c) + 5)
                dve.wait_ge(used, N_FFN + base(c) + 4)
                dve.wait_ge(f_silu, c + 1)
                nc.vector.tensor_tensor(sil[:].rearrange("p c t -> p (c t)"), sil[:].rearrange("p c t -> p (c t)"),
                                        ps[:, 2:4].rearrange("p b n -> p (b n)"), ALU.mult).then_inc(f_act, 1)
                lo_to(N_FFN + base(c) + 6)
                dve.wait_ge(f_ahi, c + 1)
                nc.vector.tensor_tensor(fT_lo[:, c % 2], sil[:], fT_hi[:, c % 2].bitcast(F32), ALU.subtract
                                        ).then_inc(f_alo, 1)
            for j in range(2):
                lo_to(N_FOX + j)
                dve.wait_ge(used, N_FOX - 1 + j)
                add_to_x(4 + 2 * j, j)

            dve.wait_ge(x_done, 4)
            mean_squares(2)
            normalise(2, 3)
            transposed_lo(2)
            for cc in range(8):
                m = N_FOX + 2 * cc + 1
                bank = 2 * (cc % 4)
                lo_to(m + 2)
                if cc < 4:
                    dve.wait_ge(squared, cc + 1)
                    nc.vector.tensor_reduce(ssq[:, 0], junk[:].rearrange("p (h d) -> p h d", d=HD), AX_X, ALU.add
                                            ).then_inc(ssq_done, 1)
                    dve.wait_ge(ssq_done, 2 * cc + 1)
                    nc.vector.tensor_scalar(ssq[:, 1], ssq[:, 0], 1.0 / HD, EPS, ALU.mult, ALU.add
                                            ).then_inc(ssq_done, 1)
                elif cc < 6:
                    dve.wait_ge(v_hi, cc - 3)
                    cols = slice((cc - 4) * CW, (cc - 3) * CW)
                    nc.vector.tensor_tensor(V_lo[:, :, cols], ps[:, bank:bank + 2], V_hi[:, :, cols].bitcast(F32),
                                            ALU.subtract).then_inc(v_lo, 1)
                if cc < 4:
                    dve.wait_ge(pow_done, 3 + cc + 1)
                    nc.vector.tensor_tensor(xn[:, cc % 2].rearrange("p (h d) -> p h d", d=HD),
                                            ps[:, bank:bank + 2].rearrange("p b (h d) -> p (b h) d", d=HD),
                                            ssq[:, 2].unsqueeze(2).to_broadcast([P, TT * 8, HD]), ALU.mult
                                            ).then_inc(qn_done, 1)
                if cc == 0:
                    dve.wait_ge(f_mm, 1)
                    for t in range(TT):
                        ins = nc.vector.tensor_tensor(fx[:, 0, t], ps[:, 7, t * H:(t + 1) * H], bf[:], ALU.add)
                    link(ins)
                    nc.vector.scalar_tensor_tensor(out=fx[:, 1], in0=fx[:, 0], scalar=-1.0, in1=fx[:, 0], op0=ALU.mult,
                                                   op1=ALU.min).then_inc(f_neg, 1)
                    dve.wait_ge(f_exp, 1)
                    half_log = log1p(fx[:, 2], (fx[:, 3], fx[:, 4], fx[:, 5]))
                    link(nc.vector.tensor_scalar(fx[:, 6], fx[:, 0], 0.0, None, ALU.min))
                    nc.vector.scalar_tensor_tensor(out=fx[:, 7], in0=half_log, scalar=-2.0, in1=fx[:, 6], op0=ALU.mult,
                                                   op1=ALU.add).then_inc(f_log, 1)
                if cc == 1:
                    dve.wait_ge(f_cum, 1)
                    nc.vector.tensor_scalar(nF[:].rearrange("p t h -> p (t h)"), ps[:, 7, 64:64 + 2 * H], -1.0, None,
                                            ALU.mult).then_inc(f_negF, 1)
                if cc == 2:
                    dve.wait_ge(fT_hi_done, 1)
                    nc.vector.tensor_tensor(nFT_lo[0:H, :], ps[0:H, 7, P:P + T], nFT_hi[0:H, :].bitcast(F32),
                                            ALU.subtract).then_inc(fT_lo_done, 1)
                if 1 <= cc <= 4:
                    q = cc - 1
                    hi, lo = (a[:, 4 * (q % 2):4 * (q % 2) + 4].rearrange("p c t -> p (c t)")
                              for a in ((qT_hi, qT_lo) if q < 2 else (kT_hi, kT_lo)))
                    dve.wait_ge(qk_hi, q + 1)
                    dve.wait_ge(qkg_done, 1)
                    nc.vector.scalar_tensor_tensor(out=lo, in0=ps[:, 2 * q:2 * q + 2].rearrange("p b n -> p (b n)"),
                                                   scalar=qkg[:, q // 2:q // 2 + 1], in1=hi.bitcast(F32),
                                                   op0=ALU.mult, op1=ALU.subtract).then_inc(qk_lo, 1)
            lo_to(N_FOXOUT + 2)

            def row_max(i):
                a = 3 * (i % 2)
                dve.wait_ge(scored, i + 1)
                nc.vector.tensor_reduce(nm[:, i, 0:4], ps[:, a].rearrange("p (j k) -> p j k", k=P), AX_X, ALU.max,
                                        negate=True).then_inc(nmax, 1)
                nc.vector.tensor_reduce(nm[:, i, 4:8],
                                        ps[:, a + 1:a + 3].rearrange("p b (j k) -> p (b j) k", k=T), AX_X,
                                        ALU.max, negate=True).then_inc(nmax, 1)
            row_max(0)
            for i in range(4):
                if i < 3:
                    row_max(i + 1)
                s, p = i // 2, i % 2
                for r in range(3):
                    dve.wait_ge(pT_hi_done, 3 * i + r + 1)
                    nc.vector.tensor_tensor(pT_lo[:, 4 * r:4 * r + 4].rearrange("p a k -> p (a k)"),
                                            ps[:, 3 * (i % 2) + r],
                                            pT_hi[:, 4 * r:4 * r + 4].rearrange("p a k -> p (a k)").bitcast(F32),
                                            ALU.subtract).then_inc(pT_lo_done, 1)
                dve.wait_ge(exped, 8 * i + 8)
                link(nc.vector.reciprocal(rinv[:, i], sm[:, i]))
                dve.wait_ge(pv_done, i + 1)
                dve.wait_ge(g_sig, 2)
                for qt in range(TT):
                    for j in range(4):
                        h = 8 * s + 2 * j + p
                        g = sg[:, qt, h * HD:(h + 1) * HD]
                        r = 4 * qt + j
                        nc.vector.scalar_tensor_tensor(out=g, in0=ps[:, 6 + i % 2, r * HD:(r + 1) * HD],
                                                       scalar=rinv[:, i, r:r + 1], in1=g, op0=ALU.mult,
                                                       op1=ALU.mult).then_inc(o_done, 1)
            for r in range(4):
                dve.wait_ge(o_hi, r + 1)
                nc.vector.tensor_tensor(qT_lo[:, 2 * r:2 * r + 2].rearrange("p k t -> p (k t)"), ps[:, r],
                                        qT_hi[:, 2 * r:2 * r + 2].rearrange("p k t -> p (k t)").bitcast(F32),
                                        ALU.subtract).then_inc(o_lo, 1)
            for j in range(2):
                lo_to(N_MOE - 1)
                dve.wait_ge(used, N_FOXOUT + 2 * j + 2)
                add_to_x(4 + 2 * j, j)

            dve.wait_ge(x_done, 6)
            mean_squares(3)
            normalise(3, 8)
            dve.wait_ge(gb_in, 16)
            for t in range(TT):
                dve.wait_ge(xn_done, 7 + t)
                nc.vector.tensor_tensor(hn[:, t], xn[:, t], gb[:], ALU.mult).then_inc(hn_done, 1)
            transposed_lo(3)
            for t in range(TT):
                dve.wait_ge(hn_hi_done, t + 1)
                nc.vector.tensor_tensor(hn_lo[:, t], hn[:, t], hn_hi[:, t].bitcast(F32), ALU.subtract
                                        ).then_inc(hn_lo_done, 1)
            dve.wait_ge(h_lo, 32)
            nc.vector.memset(ps[:, 0:2], 0.0).then_inc(y_zero, 1)
            nc.vector.memset(ST[:].bitcast(F32), 0.0).then_inc(y_zero, 1)
            nc.vector.memset(act_s[:, 0, 0:2], 0.0).then_inc(m_act, 1)
            nc.vector.memset(tk[:, 11, 0], 0.0).then_inc(m_acc, 1)
            link(nc.vector.memset(posb[:], 0.0))
            link(nc.vector.memset(combt[:], 0.0))

            def bc(a):
                return a.unsqueeze(2).to_broadcast([P, TT, E])
            rank = tk[:, 1]
            for t in range(TT):
                ins = nc.vector.tensor_scalar(rank[:, t], iota[:, 0:E], -1.0, float(E + 1), ALU.mult, ALU.add)
            link(ins)
            dve.wait_ge(routed, 1)
            link(nc.vector.tensor_copy(tk[:, 0].rearrange("p t e -> p (t e)"), ps[:, 7, 0:TT * E]))

            def pick(src, top, eq, first):
                link(nc.vector.tensor_reduce(tv[:, top], src, AX_X, ALU.max))
                link(nc.vector.tensor_tensor(eq, src, bc(tv[:, top]), ALU.is_equal))
                link(nc.vector.tensor_tensor(eq, eq, rank, ALU.mult))
                link(nc.vector.tensor_reduce(tv[:, 7], eq, AX_X, ALU.max))
                link(nc.vector.tensor_tensor(first, eq, bc(tv[:, 7]), ALU.is_equal))
            pick(tk[:, 0], 0, tk[:, 2], tk[:, 3])
            link(nc.vector.scalar_tensor_tensor(out=tk[:, 4], in0=tk[:, 3], scalar=-BIG, in1=tk[:, 0], op0=ALU.mult,
                                                op1=ALU.add))
            pick(tk[:, 4], 1, tk[:, 5], tk[:, 6])
            nc.vector.tensor_tensor(tk[:, 9], tk[:, 3], tk[:, 6], ALU.add).then_inc(picked, 1)
            nc.vector.tensor_tensor(tv[:, 2], tv[:, 1], tv[:, 0], ALU.subtract).then_inc(w_diff, 1)
            dve.wait_ge(w_exp, 1)
            link(nc.vector.tensor_scalar(tv[:, 4], tv[:, 3], 1.0, None, ALU.add))
            link(nc.vector.reciprocal(tv[:, 5], tv[:, 4]))
            link(nc.vector.tensor_tensor(tv[:, 6], tv[:, 3], tv[:, 5], ALU.mult))
            link(nc.vector.tensor_tensor(tk[:, 7], tk[:, 3], bc(tv[:, 5]), ALU.mult))
            link(nc.vector.tensor_tensor(tk[:, 8], tk[:, 6], bc(tv[:, 6]), ALU.mult))
            for half in range(2):
                ins = nc.vector.tensor_tensor(combt[:, :, 1 + half * E:1 + (half + 1) * E], tk[:, 7], tk[:, 8], ALU.add)
            link(ins)
            dve.wait_ge(slotted, 1)
            link(nc.vector.tensor_tensor(posb[:, :, 0:E], ps[:, 7, 32:48].rearrange("p (t e) -> p t e", e=E), tk[:, 9],
                                         ALU.mult))
            link(nc.vector.tensor_scalar(posb[:, :, E:2 * E], posb[:, :, 0:E], -float(P), None, ALU.add))
            link(nc.vector.tensor_reduce(cnt[:, 0:1], ps[:, 7, 64:64 + E], AX_X, ALU.max))
            link(nc.vector.tensor_scalar(cnt[:, 1:2], cnt[:, 0:1], float(P) + 0.5, float(E), ALU.is_gt, ALU.mult))
            link(nc.vector.tensor_scalar(cnt[:, 0:1], cnt[:, 1:2], float(E), None, ALU.add))
            nc.vector.tensor_copy(nblk_i[:], cnt[:, 0:1]).then_inc(blocks, 1)

            def one_hot(col, count):
                nc.vector.tensor_copy(pcol[:], posb[:, :, col].rearrange("p t o -> p (t o)")).then_inc(m_col, 1)
                dve.wait_ge(m_col, count)
                for t in range(TT):
                    ins = nc.vector.tensor_scalar(S[:, t], iota[:], pcol[:, t:t + 1], None, ALU.is_equal)
                ins.then_inc(m_S, 1)

            def gathered_lo(count):
                dve.wait_ge(m_xh, count)
                nc.vector.tensor_copy(xg_lo[:].rearrange("p k s -> p (k s)"),
                                      ps[:, 4:6].rearrange("p b n -> p (b n)")).then_inc(m_xl, 1)

            one_hot(slice(0, 1), 1)
            gathered_lo(1)

            def y_to_lo(b):
                dve.wait_ge(m_yhi, at(1, 1, b))
                nc.vector.tensor_tensor(y_lo[:], ps[:, 0:2].rearrange("p b n -> p (b n)"), y_hi[:].bitcast(F32),
                                        ALU.subtract).then_inc(m_ylo, 1)
                nc.vector.tensor_copy(ccol[:], combt[:, :, bass.ds(b, 1)].rearrange("p t o -> p (t o)")
                                      ).then_inc(m_col, 1)

            def accumulate(b):
                dve.wait_ge(m_scat, at(1, 1, b))
                dve.wait_ge(m_acc, at(1, 1, b))
                dve.wait_ge(m_col, at(2, 2, b))
                for n, bank in enumerate((3, 5, 6, 7)):
                    t, j = n // 2, n % 2
                    xj = X[:, t, j * CW:(j + 1) * CW]
                    ins = nc.vector.scalar_tensor_tensor(out=xj, in0=ps[:, bank], scalar=ccol[:, t:t + 1], in1=xj,
                                                         op0=ALU.mult, op1=ALU.add)
                ins.then_inc(m_acc, 1)

            def act_T_lo(b, c):
                dve.wait_ge(m_thi, at(c + 1, FC, b))
                nc.vector.tensor_tensor(aT_lo[:, c % 2].rearrange("p a s -> p (a s)"), ps[:, 6],
                                        aT_hi[:, c % 2].rearrange("p a s -> p (a s)").bitcast(F32), ALU.subtract
                                        ).then_inc(m_tlo, 1)

            dve.wait_ge(blocks, 1)
            nblk = dve.value_load(nblk_i[0:1, 0:1], min_val=E, max_val=2 * E)
            with dve.Fori(0, nblk) as b:
                nxt[0] = 0
                lo_to(1, b)
                y_to_lo(b)
                lo_to(3, b)
                accumulate(b)
                for c in range(FC):
                    lo_to(base(c) + 5, b)
                    dve.wait_ge(used, at(N_MOE + base(c) + 4, FFN_UNITS, b))
                    dve.wait_ge(m_silu, at(c + 2, FC, b))
                    nc.vector.tensor_tensor(act_s[:, c % 2], gt[:, c % 2], ps[:, 4 + c % 2], ALU.mult
                                            ).then_inc(m_act, 1)
                    lo_to(base(c) + 6, b)
                    act_T_lo(b, c)
                    if c == 2:
                        dve.wait_ge(m_TS, at(1, 1, b))
                        one_hot(bass.ds(b + 1, 1), at(3, 2, b))
                lo_to(FFN_UNITS - 1, b)
                gathered_lo(at(2, 1, b))
            y_to_lo(nblk)
            accumulate(nblk)
            dve.wait_ge(m_acc, at(2, 1, nblk))
            nc.vector.memset(cnt[:, 0:1], 0.0).then_inc(m_fin, 1)


_INS = ['x', 'norm_mix', 'norm_ffn', 'lru_w_in', 'lru_conv_w', 'lru_conv_b', 'lru_w_a', 'lru_b_a', 'lru_w_x',
        'lru_b_x', 'lru_log_lambda', 'lru_w_out', 'fox_w_in', 'fox_b_f', 'fox_q_gain', 'fox_k_gain', 'fox_w_out',
        'ffn_w_gate', 'ffn_w_up', 'ffn_w_down', 'moe_router', 'moe_w_gate', 'moe_w_up', 'moe_w_down']
_OUTS = [((1, T, D), 'float32')]


def kernel(**inputs):
    import numpy as _np
    import concourse.bacc as _bacc
    from concourse import mybir as _mybir
    from concourse.bass_utils import run_bass_kernel_spmd as _run

    nc = _bacc.Bacc("TRN2", target_bir_lowering=False, num_devices=1)
    arrays, args = {}, []
    for name in _INS:
        a = _np.ascontiguousarray(inputs[name])
        arrays[f"in_{name}_dram"] = a
        args.append(nc.dram_tensor(f"in_{name}_dram", a.shape, _mybir.dt.from_np(a.dtype), kind="ExternalInput").ap())
    for i, (shape, dtype) in enumerate(_OUTS):
        dt = _mybir.dt.from_np(_np.dtype(dtype))
        args.append(nc.dram_tensor(f"out_{i}_dram", shape, dt, kind="ExternalOutput").ap())
    hybrid_trunk(nc, *args)
    r = _run(nc, [arrays], core_ids=[0])
    return r.results[0]["out_0_dram"]
```

```python
from contextlib import ExitStack

import concourse.bass as bass
from concourse import mybir

P = 128
D = 1024
KT = D // P
T = 256
TT = T // P
F = 3584
CW = 512
UK = 4
FC = F // CW
H = 16
HD = D // H
E = 8
CONV = 4
LRU_C = 8.0
EPS = 1e-6
NEG = -1e30
BIG = 3e38

HR = 3
RR = 7
FFN_UNITS = FC * 6
N_IN = 8
N_FFN = N_IN + 4
N_FOX = N_FFN + FFN_UNITS
N_FOXOUT = N_FOX + 16
N_MOE = N_FOXOUT + 4
assert FFN_UNITS % HR == 0 and FFN_UNITS % RR == 0

F32 = mybir.dt.float32
F32R = mybir.dt.float32r
I32 = mybir.dt.int32
ALU = mybir.AluOpType
ACT = mybir.ActivationFunctionType
AX_X = mybir.AxisListType.X


def base(c):
    return 0 if c == 0 else 4 + 6 * (c - 1)


def down(c):
    return base(c + 1) + 4 if c < FC - 1 else FFN_UNITS - 2


def at(count, per, b):
    return count if b is None else b * per + count


def hybrid_trunk(nc, x, norm_mix, norm_ffn, lru_w_in, lru_conv_w, lru_conv_b, lru_w_a, lru_b_a, lru_w_x, lru_b_x,
                 lru_log_lambda, lru_w_out, fox_w_in, fox_b_f, fox_q_gain, fox_k_gain, fox_w_out, ffn_w_gate,
                 ffn_w_up, ffn_w_down, moe_router, moe_w_gate, moe_w_up, moe_w_down, out):
    with ExitStack() as ctx:
        def sem(name):
            return ctx.enter_context(nc.semaphore(name))

        def sb(name, shape, dt=F32, where=None):
            return (where or ctx).enter_context(nc.sbuf_tensor(name, shape, dt))

        ps = ctx.enter_context(nc.psum_tensor("ps", [P, 8, CW], F32))
        raw = sb("raw", [P, RR, UK, CW])
        whi = sb("whi", [P, HR, UK, CW], F32R)
        wlo = sb("wlo", [P, HR, UK, CW], F32R)
        X = sb("X", [P, TT, D])
        rows3 = sb("rows3", [P, 3 * D])
        xn = rows3[:, 0:TT * D].rearrange("p (t d) -> p t d", t=TT)
        junk = rows3[:, TT * D:]
        hT_hi = sb("hT_hi", [P, KT, T], F32R)
        hT_lo = sb("hT_lo", [P, KT, T], F32R)
        ident = sb("ident", [P, P])
        ident_r = sb("ident_r", [P, P], F32R)
        upper = sb("upper", [P, P])
        ones = sb("ones", [P, P])
        mask = sb("mask", [P, T])
        mask_r = sb("mask_r", [P, T], F32R)
        head_row = sb("head_row", [P, H], F32R)
        iota = sb("iota", [P, P])
        par_rows = sb("par_rows", [96, P])
        par = sb("par", [P, 96])
        ss = sb("ss", [P, 8])
        ms = sb("ms", [P, 8])
        rstd = sb("rstd", [P, 8])
        mhalf = sb("mhalf", [P, H])
        PAR_CONVW, PAR_CONVB, PAR_BA, PAR_BX, PAR_LAM, PAR_MIX, PAR_FFN = 0, 32, 40, 48, 56, 64, 80
        GAIN = [PAR_MIX, PAR_FFN, PAR_MIX + KT, PAR_FFN + KT]

        wf = sb("wf", [P, KT, H])
        wf2 = sb("wf2", [P, KT, 2 * H], F32R)
        bf = sb("bf", [P, H])
        qkg = sb("qkg", [P, 2])
        fx = sb("fx", [P, 8, TT, H])
        nF = sb("nF", [P, TT, H])
        nFT = sb("nFT", [P, T], F32R)
        ssq = sb("ssq", [P, 3, TT * 8])
        nm = sb("nm", [P, 4, 8])
        sm = sb("sm", [P, 4, 8])
        rinv = sb("rinv", [P, 4, 8])
        rw = sb("rw", [P, KT, E])
        rw2 = sb("rw2", [P, KT, 2 * E], F32R)
        cnt = sb("cnt", [P, 2])
        nblk_i = sb("nblk_i", [P, 1], I32)

        with ExitStack() as a1:
            xpad = sb("xpad", [P, KT, CONV - 1 + T], where=a1)
            xc = sb("xc", [P, KT, T], where=a1)
            rg = sb("rg", [P, KT, T], where=a1)
            gi = sb("gi", [P, KT, T], where=a1)
            av = sb("av", [P, KT, T], where=a1)
            yb = sb("yb", [P, KT, T], where=a1)
            wax = yb[:].rearrange("p k t -> p (k t)").rearrange("p (g c j) -> p g c j", g=2, c=KT)
            lt = sb("lt", [P, 6, 8], where=a1)
        with ExitStack() as a2:
            sil = sb("sil", [P, 4, T], where=a2)
            fT_hi = sb("fT_hi", [P, 2, 4, T], F32R, where=a2)
            fT_lo = sb("fT_lo", [P, 2, 4, T], F32R, where=a2)
        with ExitStack() as a3:
            qT_hi = sb("qT_hi", [P, KT, T], F32R, where=a3)
            qT_lo = sb("qT_lo", [P, KT, T], F32R, where=a3)
            V_hi = sb("V_hi", [P, TT, D], F32R, where=a3)
            V_lo = sb("V_lo", [P, TT, D], F32R, where=a3)
            pT_hi = sb("pT_hi", [P, 2, 4, P], F32R, where=a3)
            pT_lo = sb("pT_lo", [P, 2, 4, P], F32R, where=a3)
            with ExitStack() as k3:
                kT_hi = sb("kT_hi", [P, KT, T], F32R, where=k3)
                kT_lo = sb("kT_lo", [P, KT, T], F32R, where=k3)
            with ExitStack() as g3:
                sg = [sb("sg_a", [P, TT, CW], where=g3)]
                sb("kT_hi_rest", [P, KT // 2, T], where=g3)
                sg.append(sb("sg_b", [P, TT, CW], where=g3))
        with ExitStack() as a4:
            hn = sb("hn", [P, TT, D], where=a4)
            hn_hi = sb("hn_hi", [P, TT, D], F32R, where=a4)
            hn_lo = sb("hn_lo", [P, TT, D], F32R, where=a4)
            gb = sb("gb", [P, D], where=a4)
            gt = sb("gt", [P, 2, CW], where=a4)
            act_s = sb("act_s", [P, 2, CW], where=a4)
            aT_hi = sb("aT_hi", [P, 2, 4, P], F32R, where=a4)
            aT_lo = sb("aT_lo", [P, 2, 4, P], F32R, where=a4)
            S = sb("S", [P, TT, P], F32R, where=a4)
            ST = sb("ST", [P, T], F32R, where=a4)
            tk = sb("tk", [P, 12, TT, E], where=a4)
            tv = sb("tv", [P, 8, TT], where=a4)
            posb = sb("posb", [P, TT, 2 * E + 1], where=a4)
            combt = sb("combt", [P, TT, 2 * E + 1], where=a4)
            pcol = sb("pcol", [P, TT], where=a4)
            ccol = sb("ccol", [P, TT], where=a4)
        probs = [rows3[:, i * 12 * P:(i + 1) * 12 * P].rearrange("p (a k) -> p a k", k=P) for i in range(2)]
        qf = xpad[:, :, 0:T]
        hTf_hi, hTf_lo = (h[:].rearrange("p k t -> p (k t)") for h in (hT_hi, hT_lo))
        xg_hi, xg_lo = (h[:, 0:D].rearrange("p (k s) -> p k s", s=P) for h in (hTf_hi, hTf_lo))
        y_hi, y_lo = hTf_hi[:, D:2 * D], hTf_lo[:, D:2 * D]

        O_BANKS = (6, 7, 4, 5)
        X_BANKS = (6, 1)

        landed = [sem(f"landed{i}") for i in range(RR)]
        hi_done = sem("hi_done")
        lo_done = sem("lo_done")
        used = sem("used")
        x_in, par_in, wax_in, small_in, gb_in = (sem(s) for s in ("x_in", "par_in", "wax_in", "small_in", "gb_in"))
        consts, pow_done, gx_done = sem("consts"), sem("pow_done"), sem("gx_done")
        par_T, xn_T, gate_r, gate_i, f_mm, f_cum, f_T, qk_T, scored, probs_T, pv_done, o_T, routed, slotted = (
            sem(s) for s in ("par_T", "xn_T", "gate_r", "gate_i", "f_mm", "f_cum", "f_T", "qk_T", "scored",
                             "probs_T", "pv_done", "o_T", "routed", "slotted"))
        sumsq, h_hi, lam_exp, small_hi, xp_in, gelu, sig_r, sig_i, a_exp, th_done, mult_done, z_hi = (
            sem(s) for s in ("sumsq", "h_hi", "lam_exp", "small_hi", "xp_in", "gelu", "sig_r", "sig_i", "a_exp",
                             "th_done", "mult_done", "z_hi"))
        f_silu, f_ahi, squared, f_exp, fT_hi_done, qk_hi, v_hi, g_sig, exped, pT_hi_done, o_hi, w_exp, hn_hi_done = (
            sem(s) for s in ("f_silu", "f_ahi", "squared", "f_exp", "fT_hi_done", "qk_hi", "v_hi", "g_sig",
                             "exped", "pT_hi_done", "o_hi", "w_exp", "hn_hi_done"))
        chain, par_done, ms_done, xn_done, h_lo, conv_done, lam_neg, lam_done, small_lo, m2_done, z_done, z_lo = (
            sem(s) for s in ("chain", "par_done", "ms_done", "xn_done", "h_lo", "conv_done", "lam_neg", "lam_done",
                             "small_lo", "m2_done", "z_done", "z_lo"))
        x_done, f_act, f_alo, f_neg, f_log, f_negF, fT_lo_done, ssq_done, qn_done, qk_lo, v_lo, nmax = (
            sem(s) for s in ("x_done", "f_act", "f_alo", "f_neg", "f_log", "f_negF", "fT_lo_done", "ssq_done",
                             "qn_done", "qk_lo", "v_lo", "nmax"))
        pT_lo_done, o_done, o_lo, hn_done, hn_lo_done, picked, w_diff, blocks, y_zero, edges, qkg_done, const_r = (
            sem(s) for s in ("pT_lo_done", "o_done", "o_lo", "hn_done", "hn_lo_done", "picked", "w_diff", "blocks",
                             "y_zero", "edges", "qkg_done", "const_r"))
        m_scat, m_T, m_TS, m_gat = (sem(s) for s in ("m_scat", "m_T", "m_TS", "m_gat"))
        m_yhi, m_silu, m_thi, m_ST, m_xh = (sem(s) for s in ("m_yhi", "m_silu", "m_thi", "m_ST", "m_xh"))
        m_ylo, m_acc, m_act, m_tlo, m_S, m_xl, m_col, m_fin = (
            sem(s) for s in ("m_ylo", "m_acc", "m_act", "m_tlo", "m_S", "m_xl", "m_col", "m_fin"))
        out_done, sumsq_v = sem("out_done"), sem("sumsq_v")

        def unit_of(w, rows, col):
            return w[rows * P:(rows + UK) * P, col * CW:(col + 1) * CW].rearrange("(k p) n -> p k n", p=P)

        def swiglu_units(gate, up, dn):
            def d(c):
                return [(dn, c * UK, j) for j in range(2)]
            for c in range(FC):
                yield from [(gate, 0, c), (gate, UK, c), (up, 0, c), (up, UK, c)]
                if c:
                    yield from d(c - 1)
            yield from d(FC - 1)

        def front_units():
            for col in (2, 3, 0, 1):
                for rows in (0, UK):
                    yield lru_w_in[0], rows, col
            for col in (0, 1):
                for rows in (0, UK):
                    yield lru_w_out[0], rows, col
            yield from swiglu_units(ffn_w_gate[0], ffn_w_up[0], ffn_w_down[0])
            for col in range(8):
                for rows in (0, UK):
                    yield fox_w_in[0], rows, col
            for rows in (0, UK):
                for col in (0, 1):
                    yield fox_w_out[0], rows, col

        expert_w = [w.rearrange("a e d f -> (a e) d f") for w in (moe_w_gate, moe_w_up, moe_w_down)]
        block = ctx.enter_context(nc.Block())

        @block.sync
        def _(sp):
            for t in range(TT):
                sp.dma_start(X[:, t], x[0, t * P:(t + 1) * P, :]).then_inc(x_in, 16)
            for n, (w, rows, col) in enumerate(front_units()):
                if n >= RR:
                    sp.wait_ge(lo_done, n - RR + 1)
                sp.dma_start(raw[:, n % RR], unit_of(w, rows, col)).then_inc(landed[n % RR], 16)
                if n == 1:
                    sp.dma_start(wax[:, 0], lru_w_a[0].rearrange("h i j -> i h j")).then_inc(wax_in, 16)
                    sp.dma_start(wax[:, 1], lru_w_x[0].rearrange("h i j -> i h j")).then_inc(wax_in, 16)

            def expert_loads(b, e):
                for i, (w, rows, col) in enumerate(swiglu_units(*expert_w)):
                    n = N_MOE + i
                    sp.wait_ge(lo_done, at(n - RR + 1, FFN_UNITS, b))
                    src = w[bass.ds(e, 1), rows * P:(rows + UK) * P, col * CW:(col + 1) * CW]
                    sp.dma_start(raw[:, n % RR], src.rearrange("o (k p) n -> p (o k) n", p=P)
                                 ).then_inc(landed[n % RR], 16)

            with sp.Fori(0, E) as b:
                expert_loads(b, b)
            sp.wait_ge(blocks, 1)
            nblk = sp.value_load(nblk_i[0:1, 0:1], min_val=E, max_val=2 * E)
            with sp.If(nblk > E):
                with sp.Fori(E, 2 * E) as b:
                    expert_loads(b, b - E)
            for n in range(4):
                t, j = n // 2, n % 2
                sp.wait_ge(m_fin, n + 1)
                sp.dma_start(out[0, t * P:(t + 1) * P, j * CW:(j + 1) * CW], X[:, t, j * CW:(j + 1) * CW]
                             ).then_inc(out_done, 16)
            sp.wait_ge(out_done, 64)

        @block.gpsimd
        def _(pool):
            pool.memset(ident[:], 0.0).then_inc(consts, 1)
            pool.memset(upper[:], 1.0).then_inc(consts, 1)
            pool.memset(mask[:], 0.0).then_inc(consts, 1)
            pool.memset(ones[:], 1.0).then_inc(consts, 1)
            pool.memset(mhalf[:], -0.5).then_inc(consts, 1)
            pool.iota(iota[:], [[1, P]], base=1, channel_multiplier=0,
                      allow_small_or_imprecise_dtypes=True).then_inc(consts, 1)
            pool.wait_ge(consts, 6)
            pool.affine_select(out=ident[:], in_=ident[:], compare_op=ALU.not_equal, fill=1.0, base=0,
                               pattern=[[-1, P]], channel_multiplier=1).then_inc(consts, 1)
            pool.affine_select(out=upper[:], in_=upper[:], compare_op=ALU.is_ge, fill=0.0, base=0,
                               pattern=[[1, P]], channel_multiplier=-1).then_inc(consts, 1)
            pool.affine_select(out=mask[:, P:T], in_=mask[:, P:T], compare_op=ALU.is_ge, fill=NEG, base=0,
                               pattern=[[-1, P]], channel_multiplier=1).then_inc(consts, 1)
            pool.memset(nFT[:].bitcast(F32), 0.0).then_inc(consts, 1)
            def rms_pow(r):
                pool.wait_ge(ms_done, r + 1)
                pool.tensor_tensor(rstd[:, 2 * r:2 * r + 2], ms[:, 2 * r:2 * r + 2], mhalf[:, 0:2],
                                   ALU.pow).then_inc(pow_done, 1)
            rms_pow(0)
            pool.dma_start(wf[:], fox_w_in[0][:, 4 * D:4 * D + H].rearrange("(k p) h -> p k h", p=P)
                           ).then_inc(small_in, 16)
            pool.dma_start(rw[:], moe_router[0].rearrange("(k p) e -> p k e", p=P)).then_inc(small_in, 16)
            pool.dma_start(bf[:], fox_b_f[0].partition_broadcast(P)).then_inc(small_in, 16)
            for half in range(2):
                for i, g in enumerate((fox_q_gain, fox_k_gain)):
                    pool.dma_start(qkg[half * HD:(half + 1) * HD, i:i + 1], g.rearrange("a d -> d a")
                                   ).then_inc(small_in, 16)
            for g in range(4):
                pool.wait_ge(sig_i, 2 * g + 2)
                pool.tensor_tensor(gi[:, 2 * g:2 * g + 2], gi[:, 2 * g:2 * g + 2], xc[:, 2 * g:2 * g + 2],
                                   ALU.mult).then_inc(gx_done, 1)
            rms_pow(1)
            rms_pow(2)
            for cc in range(4):
                pool.wait_ge(ssq_done, 2 * cc + 2)
                pool.tensor_tensor(ssq[:, 2], ssq[:, 1], mhalf[:], ALU.pow).then_inc(pow_done, 1)
            pool.wait_ge(o_T, 4)
            pool.dma_start(gb[:], norm_ffn[1].partition_broadcast(P)).then_inc(gb_in, 16)
            pool.wait_ge(ms_done, 4)
            pool.tensor_tensor(rstd[:, 6:8], ms[:, 6:8], mhalf[:, 0:2], ALU.pow).then_inc(pow_done, 1)

        @block.scalar
        def _(act):
            nxt = [0]

            def hi_to(n, b=None):
                first = 0 if b is None else N_MOE
                last = N_MOE + HR - 1 if b is None else N_MOE + FFN_UNITS - 1
                while first + nxt[0] <= min(first + n, last):
                    m = first + nxt[0]
                    act.wait_ge(landed[m % RR], at(16 * (m // RR + 1), 16 * FFN_UNITS // RR, b))
                    if m >= HR:
                        act.wait_ge(used, at(m - HR + 1, FFN_UNITS, b))
                    nc.scalar.activation(whi[:, m % HR], raw[:, m % RR], ACT.Copy).then_inc(hi_done, 1)
                    nxt[0] += 1

            def squares(r):
                if r:
                    act.wait_ge(sumsq, r)
                nc.scalar.activation(junk[:], X[:, 0, :], ACT.Square, accum_out=ss[:, 2 * r:2 * r + 1]
                                     ).then_inc(sumsq, 1)

            def transposed_hi(r):
                for k in range(KT):
                    act.wait_ge(xn_T, 4 * r + k // 2 + 1)
                    nc.scalar.activation(hT_hi[:, k], ps[:, k // 2, (k % 2) * T:(k % 2 + 1) * T], ACT.Copy,
                                         scale=par[:, GAIN[r] + k:GAIN[r] + k + 1]).then_inc(h_hi, 1)

            def rows_of(w):
                return w.rearrange("a (c p) -> (a c) p", p=P)
            for r0, n, src in ((PAR_CONVW, 32, rows_of(lru_conv_w[0])), (PAR_CONVB, 8, rows_of(lru_conv_b)),
                               (PAR_BA, 8, rows_of(lru_b_a)), (PAR_BX, 8, rows_of(lru_b_x)),
                               (PAR_LAM, 8, rows_of(lru_log_lambda)), (PAR_MIX, 16, rows_of(norm_mix)),
                               (PAR_FFN, 16, rows_of(norm_ffn))):
                act.dma_start(par_rows[r0:r0 + n, :], src).then_inc(par_in, 16)
            act.wait_ge(x_in, 32)
            squares(0)
            hi_to(2)
            act.wait_ge(par_done, 1)
            transposed_hi(0)
            act.wait_ge(lam_neg, 1)
            nc.scalar.activation(lt[:, 1], lt[:, 0], ACT.Exp).then_inc(lam_exp, 1)
            for ch in range(2):
                hi_to(2 * ch + 3)
                act.wait_ge(used, 2 * ch + 2)
                for i in range(2):
                    bank = 4 + 2 * ch + i
                    nc.scalar.activation(xpad[:, 4 * ch + 2 * i:4 * ch + 2 * i + 2, CONV - 1:],
                                         ps[:, bank].rearrange("p (c t) -> p c t", t=T), ACT.Copy).then_inc(xp_in, 1)
            for ch in range(2):
                hi_to(6 + ch)
                for ready, done, dst, par0, bank0 in ((gate_r, sig_r, rg, PAR_BA, 4), (gate_i, sig_i, gi, PAR_BX, 6)):
                    for i in range(4):
                        c = 4 * ch + i
                        act.wait_ge(ready, 2 * (c // 2) + 2)
                        nc.scalar.activation(dst[:, c], ps[:, bank0 + i // 2, (i % 2) * T:(i % 2 + 1) * T],
                                             ACT.Sigmoid, bias=par[:, par0 + c:par0 + c + 1]).then_inc(done, 1)
            hi_to(8)
            act.wait_ge(lam_done, 2)
            act.wait_ge(sig_r, KT)
            for c in range(KT):
                nc.scalar.activation(av[:, c], rg[:, c], ACT.Exp, scale=lt[:, 4, c:c + 1]).then_inc(a_exp, 1)
                nc.scalar.activation(rg[:, c], rg[:, c], ACT.Tanh, scale=lt[:, 5, c:c + 1]).then_inc(th_done, 1)
            for g in range(2):
                act.wait_ge(m2_done, g + 1)
                nc.scalar.activation(qf[:, 4 * g:4 * g + 4], qf[:, 4 * g:4 * g + 4], ACT.Sqrt).then_inc(mult_done, 1)
            for ch in range(2):
                hi_to(9)
                act.wait_ge(used, 2 * ch + 6)
                nc.scalar.activation(yb[:, 4 * ch:4 * ch + 4].rearrange("p c t -> p (c t)"),
                                     ps[:, 2 * ch:2 * ch + 2].rearrange("p b n -> p (b n)"),
                                     ACT.Gelu_apprx_tanh).then_inc(gelu, 1)
            for g in range(2):
                act.wait_ge(z_done, g + 1)
                nc.scalar.activation(hT_hi[:, 4 * g:4 * g + 4], yb[:, 4 * g:4 * g + 4], ACT.Copy).then_inc(z_hi, 1)
            hi_to(N_FFN)
            act.wait_ge(small_in, 16 * 7)
            nc.scalar.activation(wf2[:, :, 0:H], wf[:], ACT.Copy).then_inc(small_hi, 1)
            nc.scalar.activation(rw2[:, :, 0:E], rw[:], ACT.Copy).then_inc(small_hi, 1)
            hi_to(N_FFN + 1)

            act.wait_ge(x_done, 2)
            squares(1)
            transposed_hi(1)
            for c in range(FC):
                hi_to(N_FFN + base(c) + 3)
                act.wait_ge(used, N_FFN + base(c) + 2)
                if c:
                    act.wait_ge(f_alo, c)
                nc.scalar.activation(sil[:].rearrange("p c t -> p (c t)"),
                                     ps[:, 0:2].rearrange("p b n -> p (b n)"), ACT.Silu).then_inc(f_silu, 1)
                hi_to(N_FFN + base(c) + 6)
                act.wait_ge(f_act, c + 1)
                nc.scalar.activation(fT_hi[:, c % 2], sil[:], ACT.Copy).then_inc(f_ahi, 1)
            hi_to(N_FOX + 1)

            act.wait_ge(x_done, 4)
            squares(2)
            transposed_hi(2)
            for cc in range(6):
                m = N_FOX + 2 * cc + 1
                bank = 2 * (cc % 4)
                hi_to(m + 2)
                act.wait_ge(used, m + 1)
                both = ps[:, bank:bank + 2].rearrange("p b n -> p (b n)")
                if cc < 4:
                    if cc:
                        act.wait_ge(ssq_done, 2 * cc)
                    nc.scalar.activation(junk[:], both, ACT.Square).then_inc(squared, 1)
                else:
                    nc.scalar.activation(V_hi[:, :, (cc - 4) * CW:(cc - 3) * CW], ps[:, bank:bank + 2], ACT.Copy
                                         ).then_inc(v_hi, 1)
                if cc == 0:
                    act.wait_ge(f_neg, 1)
                    nc.scalar.activation(fx[:, 2], fx[:, 1], ACT.Exp).then_inc(f_exp, 1)
                if cc == 4:
                    act.wait_ge(f_T, 1)
                    nc.scalar.activation(nFT[0:H, :], ps[0:H, 4, 0:T], ACT.Copy).then_inc(fT_hi_done, 1)
                if 1 <= cc <= 4:
                    q = cc - 1
                    dst = (qT_hi if q < 2 else kT_hi)[:, 4 * (q % 2):4 * (q % 2) + 4]
                    act.wait_ge(qk_T, q + 1)
                    nc.scalar.activation(dst.rearrange("p c t -> p (c t)"),
                                         ps[:, 2 * q:2 * q + 2].rearrange("p b n -> p (b n)"), ACT.Copy,
                                         scale=qkg[:, q // 2:q // 2 + 1]).then_inc(qk_hi, 1)
            def exps(i):
                a = 3 * (i % 2)
                act.wait_ge(nmax, 2 * i + 2)
                for j in range(4):
                    nc.scalar.activation(probs[i % 2][:, j], ps[:, a, j * P:(j + 1) * P], ACT.Exp,
                                         bias=nm[:, i, j:j + 1], accum_out=sm[:, i, j:j + 1]).then_inc(exped, 1)
                for j in range(4):
                    nc.scalar.activation(probs[i % 2][:, 4 + 2 * j:6 + 2 * j].rearrange("p a k -> p (a k)"),
                                         ps[:, a + 1 + j // 2, (j % 2) * T:(j % 2 + 1) * T], ACT.Exp,
                                         bias=nm[:, i, 4 + j:5 + j], accum_out=sm[:, i, 4 + j:5 + j]
                                         ).then_inc(exped, 1)
            def probs_hi(*rounds):
                for r in rounds:
                    act.wait_ge(probs_T, r + 1)
                    if r >= 2:
                        act.wait_ge(pv_done, r - 1)
                    nc.scalar.activation(pT_hi[:, r % 2].rearrange("p a k -> p (a k)"),
                                         ps[:, 3 * (r // 3 % 2) + r % 3], ACT.Copy).then_inc(pT_hi_done, 1)

            def gate_sigmoid(half):
                act.wait_ge(used, N_FOX + 14 + 2 * half)
                nc.scalar.activation(sg[half][:], ps[:, 6:8], ACT.Sigmoid).then_inc(g_sig, 1)

            def outputs_T_hi(*rounds):
                for r in rounds:
                    act.wait_ge(o_T, r + 1)
                    nc.scalar.activation(qT_hi[:, 2 * r:2 * r + 2].rearrange("p k t -> p (k t)"), ps[:, O_BANKS[r]],
                                         ACT.Copy).then_inc(o_hi, 1)

            exps(0)
            hi_to(N_FOX + 14)
            exps(1)
            hi_to(N_FOX + 15)
            gate_sigmoid(0)
            hi_to(N_FOXOUT)
            probs_hi(0, 1, 2)
            hi_to(N_FOXOUT + 1)
            probs_hi(3, 4)
            exps(2)
            probs_hi(5)
            hi_to(N_FOXOUT + 2)
            gate_sigmoid(1)
            probs_hi(6, 7)
            exps(3)
            probs_hi(8)
            outputs_T_hi(0, 1)
            probs_hi(9, 10)
            hi_to(N_FOXOUT + 3)
            probs_hi(11)
            outputs_T_hi(2, 3)
            hi_to(N_MOE + 1)

            act.wait_ge(x_done, 6)
            squares(3)
            transposed_hi(3)
            hi_to(N_MOE + 2)
            for t in range(TT):
                act.wait_ge(hn_done, t + 1)
                nc.scalar.activation(hn_hi[:, t], hn[:, t], ACT.Copy).then_inc(hn_hi_done, 1)
            act.wait_ge(w_diff, 1)
            nc.scalar.activation(tv[:, 3], tv[:, 2], ACT.Exp).then_inc(w_exp, 1)

            def gathered_hi(count):
                act.wait_ge(m_gat, count)
                nc.scalar.activation(xg_hi[:].rearrange("p k s -> p (k s)"),
                                     ps[:, 2:4].rearrange("p b n -> p (b n)"), ACT.Copy).then_inc(m_xh, 1)
            gathered_hi(1)
            nc.scalar.activation(junk[:, 0:2], junk[:, 0:2], ACT.Copy).then_inc(m_silu, 1)

            def y_to_hi(b):
                act.wait_ge(y_zero, 2)
                act.wait_ge(used, at(N_MOE, FFN_UNITS, b))
                nc.scalar.activation(y_hi[:], ps[:, 0:2].rearrange("p b n -> p (b n)"), ACT.Copy).then_inc(m_yhi, 1)

            def act_T_hi(b, c):
                act.wait_ge(m_T, at(c + 1, FC, b))
                nc.scalar.activation(aT_hi[:, c % 2].rearrange("p a s -> p (a s)"), ps[:, 6], ACT.Copy
                                     ).then_inc(m_thi, 1)

            def expert_block(b, converted):
                nxt[0] = converted
                hi_to(1, b)
                y_to_hi(b)
                for c in range(FC):
                    if c == 1:
                        hi_to(6, b)
                        act.wait_ge(m_TS, at(1, 1, b))
                        nc.scalar.activation(ST[:], ps[:, 7, 0:T], ACT.Copy).then_inc(m_ST, 1)
                        act_T_hi(b, 0)
                    hi_to(base(c) + 3, b)
                    act.wait_ge(used, at(N_MOE + base(c) + 2, FFN_UNITS, b))
                    act.wait_ge(m_act, at(max(c, 1), FC, b))
                    nc.scalar.activation(gt[:, c % 2], ps[:, 2 + c % 2], ACT.Silu).then_inc(m_silu, 1)
                    if c:
                        hi_to(base(c) + 6, b)
                        act_T_hi(b, c)
                hi_to(FFN_UNITS - 1, b)
                gathered_hi(at(2, 1, b))

            expert_block(0, HR)
            act.wait_ge(blocks, 1)
            nblk = act.value_load(nblk_i[0:1, 0:1], min_val=E, max_val=2 * E)
            with act.Fori(1, nblk) as b:
                expert_block(b, 0)
            y_to_hi(nblk)

        @block.tensor
        def _(pe):
            mm = nc.tensor.matmul

            def tokens_unit(m, b, src, k0, tiles, dst, first, last):
                pe.wait_ge(lo_done, at(m + 1, FFN_UNITS, b))
                for k in range(UK):
                    for t in range(tiles):
                        hi, lo = src(k0 + k, t)
                        mm(dst(t), hi, whi[:, m % HR, k], start=first and k == 0, stop=False)
                        mm(dst(t), hi, wlo[:, m % HR, k], start=False, stop=False)
                        ins = mm(dst(t), lo, whi[:, m % HR, k], start=False, stop=last and k == UK - 1)
                ins.then_inc(used, 1)

            def weights_unit(m, bank, half):
                pe.wait_ge(lo_done, m + 1)
                for c in range(4):
                    dst = ps[:, bank + c // 2, (c % 2) * T:(c % 2 + 1) * T]
                    for k in range(UK):
                        kk = half * UK + k
                        wh, wl = (w[:, m % HR, k, c * P:(c + 1) * P] for w in (whi, wlo))
                        mm(dst, wh, hT_hi[:, kk], start=half == 0 and k == 0 and c % 2 == 0, stop=False,
                           skip_group_check=True)
                        mm(dst, wh, hT_lo[:, kk], start=False, stop=False, skip_group_check=True)
                        ins = mm(dst, wl, hT_hi[:, kk], start=False, stop=half == 1 and k == UK - 1,
                                 skip_group_check=True)
                ins.then_inc(used, 1)

            def transposes(src, done, banks=(0, 1, 2, 3), k0=0):
                for n, bank in enumerate(banks):
                    for k in range(2):
                        for t in range(TT):
                            ins = nc.tensor.transpose(ps[:, bank, k * T + t * P:k * T + (t + 1) * P],
                                                      src(t, k0 + 2 * n + k), ident[:])
                    ins.then_inc(done, 1)

            def of_xn(t, k):
                return xn[:, t, k * P:(k + 1) * P]

            def of_hT(k, t):
                return hT_hi[:, k, t * P:(t + 1) * P], hT_lo[:, k, t * P:(t + 1) * P]

            pe.wait_ge(consts, 9)
            pe.wait_ge(par_in, 16 * 7)
            nc.tensor.transpose(ps[:, 7, 0:96], par_rows[:], ident[0:96, 0:96]).then_inc(par_T, 1)
            pe.wait_ge(xn_done, 2)
            transposes(of_xn, xn_T)
            def lru_gates(ch):
                for g, (bank0, done, read) in enumerate(((4, gate_r, sig_r), (6, gate_i, sig_i))):
                    for i in range(4):
                        c = 4 * ch + i
                        if g == 0:
                            pe.wait_ge(conv_done, c + 1)
                        if i == 0 and ch:
                            pe.wait_ge(read, 4)
                        mm(ps[:, bank0 + i // 2, (i % 2) * T:(i % 2 + 1) * T], wax[:, g, c], xc[:, c],
                           start=i % 2 == 0, stop=True, skip_group_check=True).then_inc(done, 1)

            for n in range(8):
                if n < 2:
                    pe.wait_ge(h_lo, 4 * n + 4)
                if n == 0:
                    pe.wait_ge(par_done, 1)
                weights_unit(n, (4, 6, 0, 2)[n // 2], n % 2)
                if n == 4:
                    pe.wait_ge(wax_in, 32)
                    pe.wait_ge(xp_in, 4)
                    lru_gates(0)
                if n == 5:
                    lru_gates(1)
            for i in range(4):
                if i < 2:
                    pe.wait_ge(z_lo, i + 1)
                tokens_unit(N_IN + i, None, of_hT, UK * (i % 2), TT, lambda t: ps[:, 2 * (i // 2) + t],
                            i % 2 == 0, i % 2 == 1)

            pe.wait_ge(xn_done, 4)
            transposes(of_xn, xn_T)

            def ffn_down(c):
                pe.wait_ge(f_alo, c + 1)
                for j in range(2):
                    tokens_unit(N_FFN + down(c) + j, None,
                                lambda k, t: (fT_hi[:, c % 2, k, t * P:(t + 1) * P],
                                              fT_lo[:, c % 2, k, t * P:(t + 1) * P]),
                                0, TT, lambda t: ps[:, 4 + 2 * j + t], c == 0, c == FC - 1)

            for c in range(FC):
                n = N_FFN + base(c)
                for half in range(2):
                    if c == 0:
                        pe.wait_ge(h_lo, 8 + 4 * half + 4)
                    elif half == 0:
                        pe.wait_ge(f_silu, c)
                    weights_unit(n + half, 0, half)
                if c:
                    pe.wait_ge(f_act, c)
                for half in range(2):
                    weights_unit(n + 2 + half, 2, half)
                if c:
                    ffn_down(c - 1)
            ffn_down(FC - 1)

            pe.wait_ge(xn_done, 6)
            transposes(of_xn, xn_T)

            def qk_transposes(q):
                pe.wait_ge(qn_done, q + 1)
                src = xn[:, q % 2].rearrange("p (t n) -> p t n", t=TT)
                for c in range(4):
                    for t in range(TT):
                        ins = nc.tensor.transpose(ps[:, 2 * q + c // 2, (c % 2) * T + t * P:(c % 2) * T + (t + 1) * P],
                                                  src[:, t, c * P:(c + 1) * P], ident[:])
                ins.then_inc(qk_T, 1)

            for cc in range(6):
                if cc == 3:
                    pe.wait_ge(f_negF, 1)
                if cc >= 4:
                    pe.wait_ge(qk_lo, cc - 3)
                for half in range(2):
                    if cc == 0:
                        pe.wait_ge(h_lo, 16 + 4 * half + 4)
                    tokens_unit(N_FOX + 2 * cc + half, None, of_hT, UK * half, TT,
                                lambda t: ps[:, 2 * (cc % 4) + t], half == 0, half == 1)
                if cc == 0:
                    pe.wait_ge(small_lo, 2)
                    for t in range(TT):
                        for k in range(KT):
                            hi, lo = of_hT(k, t)
                            for n, a in enumerate((hi, lo)):
                                ins = mm(ps[:, 7, t * 2 * H:(t + 1) * 2 * H], a, wf2[:, k],
                                         start=t == 0 and k == 0 and n == 0, stop=k == KT - 1 and n == 1,
                                         skip_group_check=True)
                    ins.then_inc(f_mm, 1)
                if cc == 1:
                    pe.wait_ge(f_log, 1)
                    mm(ps[:, 7, 64:64 + H], upper[:], fx[:, 7, 0], start=True, stop=True, skip_group_check=True)
                    mm(ps[:, 7, 64 + H:64 + 2 * H], ones[:], fx[:, 7, 0], start=False, stop=False, skip_group_check=True)
                    mm(ps[:, 7, 64 + H:64 + 2 * H], upper[:], fx[:, 7, 1], start=False, stop=True,
                       skip_group_check=True).then_inc(f_cum, 1)
                if cc == 4:
                    pe.wait_ge(qk_lo, 3)
                    for t in range(TT):
                        ins = nc.tensor.transpose(ps[0:H, 4, t * P:(t + 1) * P], nF[:, t], ident[:])
                    ins.then_inc(f_T, 1)
                if 1 <= cc <= 4:
                    qk_transposes(cc - 1)

            def scores(i):
                s, p = i // 2, i % 2
                rows = slice(p * HD, (p + 1) * HD)
                for qt in range(TT):
                    for part in range(1 + qt):
                        bank = 3 * (i % 2) + qt + part
                        js = range(4) if qt == 0 else range(2 * part, 2 * part + 2)
                        w = (qt + 1) * P
                        for n, j in enumerate(js):
                            h = 8 * s + 2 * j + p
                            mm(ps[:, bank, n * w:(n + 1) * w], head_row[:, h:h + 1].to_broadcast([P, P]), nFT[:, 0:w],
                               start=n == 0, stop=False, skip_group_check=True)
                        mm(ps[:, bank].rearrange("p (j k) -> p j k", k=w), ident_r[:],
                           mask_r[:, T - w:T].unsqueeze(1).to_broadcast([P, CW // w, w]), start=False, stop=False,
                           skip_group_check=True)
                        for n, j in enumerate(js):
                            c = 4 * s + j
                            dst = ps[:, bank, n * w:(n + 1) * w]
                            qs = slice(qt * P, (qt + 1) * P)
                            mm(dst, qT_hi[rows, c, qs], kT_hi[rows, c, 0:w], start=False, stop=False,
                               skip_group_check=True)
                            mm(dst, qT_hi[rows, c, qs], kT_lo[rows, c, 0:w], start=False, stop=False,
                               skip_group_check=True)
                            ins = mm(dst, qT_lo[rows, c, qs], kT_hi[rows, c, 0:w], start=False, stop=True,
                                     skip_group_check=True)
                ins.then_inc(scored, 1)

            def probs_transposes(*rounds):
                for r in rounds:
                    i = r // 3
                    pe.wait_ge(exped, 8 * i + 8)
                    for a in range(4):
                        ins = nc.tensor.transpose(ps[:, 3 * (i % 2) + r % 3, a * P:(a + 1) * P],
                                                  probs[i % 2][:, 4 * (r % 3) + a], ident[:])
                    ins.then_inc(probs_T, 1)

            def values(*rounds):
                for r in rounds:
                    i = r // 3
                    s, p, qt = i // 2, i % 2, int(r % 3 > 0)
                    pe.wait_ge(pT_lo_done, r + 1)
                    for a in range(4):
                        j = a if qt == 0 else 2 * (r % 3 - 1) + a // 2
                        kt = 0 if qt == 0 else a % 2
                        h = 8 * s + 2 * j + p
                        vs = slice(h * HD, (h + 1) * HD)
                        dst = ps[:, 3 * (i % 2), (4 * qt + j) * HD:(4 * qt + j + 1) * HD]
                        mm(dst, pT_hi[:, r % 2, a], V_hi[:, kt, vs], start=r % 3 == 0 and a == 0, stop=False,
                           skip_group_check=True)
                        mm(dst, pT_hi[:, r % 2, a], V_lo[:, kt, vs], start=False, stop=False, skip_group_check=True)
                        ins = mm(dst, pT_lo[:, r % 2, a], V_hi[:, kt, vs], start=False, stop=kt == qt,
                                 skip_group_check=True)
                    ins.then_inc(pv_done, 1)

            def gate_unit(n):
                tokens_unit(N_FOX + 12 + n, None, of_hT, UK * (n % 2), TT, lambda t: ps[:, 6 + t], n % 2 == 0,
                            n % 2 == 1)

            def gated(t, k):
                return sg[k // UK][:, t, (k % UK) * P:(k % UK + 1) * P]

            def out_unit(n):
                pe.wait_ge(o_lo, 2 * (n // 2) + 2)
                tokens_unit(N_FOXOUT + n, None,
                            lambda k, t: (qT_hi[:, k, t * P:(t + 1) * P], qT_lo[:, k, t * P:(t + 1) * P]),
                            UK * (n // 2), TT, lambda t: ps[:, X_BANKS[n % 2] + t], n // 2 == 0, n // 2 == 1)

            pe.wait_ge(v_lo, 2)
            pe.wait_ge(qk_lo, 4)
            pe.wait_ge(fT_lo_done, 1)
            pe.wait_ge(const_r, 3)
            scores(0)
            gate_unit(0)
            scores(1)
            gate_unit(1)
            probs_transposes(0, 1)
            pe.wait_ge(g_sig, 1)
            gate_unit(2)
            values(0)
            probs_transposes(2)
            values(1, 2)
            probs_transposes(3, 4)
            pe.wait_ge(o_done, 8)
            scores(2)
            gate_unit(3)
            values(3)
            probs_transposes(5)
            values(4, 5)
            probs_transposes(6, 7)
            pe.wait_ge(o_done, 16)
            scores(3)
            values(6)
            probs_transposes(8)
            pe.wait_ge(g_sig, 2)
            transposes(gated, o_T, O_BANKS[0:2], 0)
            values(7, 8)
            probs_transposes(9, 10)
            out_unit(0)
            values(9)
            probs_transposes(11)
            values(10, 11)
            out_unit(1)
            pe.wait_ge(o_done, 32)
            transposes(gated, o_T, O_BANKS[2:4], UK)
            out_unit(2)
            out_unit(3)

            pe.wait_ge(xn_done, 8)
            transposes(of_xn, xn_T)
            pe.wait_ge(h_lo, 32)
            for t in range(TT):
                for k in range(KT):
                    hi, lo = of_hT(k, t)
                    for n, a in enumerate((hi, lo)):
                        ins = mm(ps[:, 7, t * 2 * E:(t + 1) * 2 * E], a, rw2[:, k],
                                 start=t == 0 and k == 0 and n == 0, stop=k == KT - 1 and n == 1,
                                 skip_group_check=True)
            ins.then_inc(routed, 1)
            pe.wait_ge(picked, 1)
            sel = tk[:, 9]
            mm(ps[:, 7, 32:32 + E], upper[:], sel[:, 0], start=True, stop=True, skip_group_check=True)
            mm(ps[:, 7, 40:40 + E], ones[:], sel[:, 0], start=False, stop=False, skip_group_check=True)
            mm(ps[:, 7, 40:40 + E], upper[:], sel[:, 1], start=False, stop=True, skip_group_check=True)
            mm(ps[:, 7, 64:64 + E], ones[:], sel[:, 0], start=False, stop=False, skip_group_check=True)
            mm(ps[:, 7, 64:64 + E], ones[:], sel[:, 1], start=False, stop=True,
               skip_group_check=True).then_inc(slotted, 1)

            def gather(count):
                pe.wait_ge(m_S, count)
                for q, h in enumerate((hn_hi, hn_lo)):
                    for k in range(KT):
                        for t in range(TT):
                            ins = mm(ps[:, 2 + 2 * q + k // 4, (k % 4) * P:(k % 4 + 1) * P],
                                     h[:, t, k * P:(k + 1) * P], S[:, t], start=k % 4 == 0 and t == 0, stop=t == 1,
                                     skip_group_check=True)
                ins.then_inc(m_gat, 1)

            pe.wait_ge(hn_lo_done, 2)
            gather(1)

            def scatter(b):
                pe.wait_ge(m_ylo, at(1, 1, b))
                for n, bank in enumerate((3, 5, 6, 7)):
                    t, j = n // 2, n % 2
                    for q, y in enumerate((y_hi, y_lo)):
                        ins = mm(ps[:, bank], ST[:, t * P:(t + 1) * P], y[:, j * CW:(j + 1) * CW], start=q == 0,
                                 stop=q == 1)
                ins.then_inc(m_scat, 1)

            def act_transposes(b, c):
                pe.wait_ge(m_act, at(c + 2, FC, b))
                for a in range(4):
                    ins = nc.tensor.transpose(ps[:, 6, a * P:(a + 1) * P], act_s[:, c % 2, a * P:(a + 1) * P], ident[:])
                ins.then_inc(m_T, 1)

            def moe_unit(b, i, src, k0, bank, first, last):
                tokens_unit(N_MOE + i, b, src, k0, 1, lambda t: ps[:, bank], first, last)

            def of_xg(k, t):
                return xg_hi[:, k], xg_lo[:, k]

            pe.wait_ge(blocks, 1)
            nblk = pe.value_load(nblk_i[0:1, 0:1], min_val=E, max_val=2 * E)
            with pe.Fori(0, nblk) as b:
                pe.wait_ge(m_xl, at(1, 1, b))
                for c in range(FC):
                    if c == 1:
                        pe.wait_ge(m_acc, at(2, 1, b))
                    pe.wait_ge(m_silu, at(max(c, 1), FC, b))
                    for half in range(2):
                        moe_unit(b, base(c) + half, of_xg, UK * half, 2 + c % 2, half == 0, half == 1)
                        if c == 0 and half == 1:
                            scatter(b)
                        if c == 1 and half == 0:
                            act_transposes(b, 0)
                            for t in range(TT):
                                ins = mm(ps[:, 7, t * P:(t + 1) * P], S[:, t], ident_r[:], start=t == 0, stop=True,
                                         skip_group_check=True)
                            ins.then_inc(m_TS, 1)
                    pe.wait_ge(m_act, at(max(c, 1), FC, b))
                    for half in range(2):
                        moe_unit(b, base(c) + 2 + half, of_xg, UK * half, 4 + c % 2, half == 0, half == 1)
                    for d in ([c - 1] if c else []) + ([c] if c == FC - 1 else []):
                        pe.wait_ge(m_tlo, at(d + 1, FC, b))
                        for j in range(2):
                            moe_unit(b, down(d) + j,
                                     lambda k, t: (aT_hi[:, d % 2, k], aT_lo[:, d % 2, k]), 0, j, d == 0, d == FC - 1)
                            if j == 0 and d < FC - 1:
                                act_transposes(b, d + 1)
                            if j == 1 and d == FC - 2:
                                gather(at(2, 1, b))
            pe.wait_ge(m_ST, nblk)
            scatter(nblk)

        @block.vector
        def _(dve):
            links = [0]

            def link(ins):
                links[0] += 1
                ins.then_inc(chain, 1)
                dve.wait_ge(chain, links[0])

            nxt = [0]

            def lo_to(n, b=None):
                first = 0 if b is None else N_MOE
                last = N_MOE + HR - 1 if b is None else N_MOE + FFN_UNITS - 1
                while first + nxt[0] <= min(first + n, last):
                    m = first + nxt[0]
                    dve.wait_ge(hi_done, at(m + 1, FFN_UNITS, b))
                    nc.vector.tensor_tensor(wlo[:, m % HR], raw[:, m % RR], whi[:, m % HR].bitcast(F32),
                                            ALU.subtract).then_inc(lo_done, 1)
                    nxt[0] += 1

            def mean_squares(r):
                nc.vector.tensor_tensor_reduce(xn[:, 1], X[:, 1], X[:, 1], 1.0, 0.0, ALU.mult, ALU.add,
                                               ss[:, 2 * r + 1:2 * r + 2]).then_inc(sumsq_v, 1)
                dve.wait_ge(sumsq, r + 1)
                dve.wait_ge(sumsq_v, r + 1)
                nc.vector.tensor_scalar(ms[:, 2 * r:2 * r + 2], ss[:, 2 * r:2 * r + 2], 1.0 / D, EPS, ALU.mult, ALU.add
                                        ).then_inc(ms_done, 1)

            def normalise(r, count):
                dve.wait_ge(pow_done, count)
                for t in range(TT):
                    nc.vector.tensor_scalar(xn[:, t], X[:, t], rstd[:, 2 * r + t:2 * r + t + 1], None, ALU.mult
                                            ).then_inc(xn_done, 1)

            def transposed_lo(r):
                for k in range(KT):
                    dve.wait_ge(h_hi, 8 * r + 2 * (k // 2) + 2)
                    nc.vector.scalar_tensor_tensor(out=hT_lo[:, k], in0=ps[:, k // 2, (k % 2) * T:(k % 2 + 1) * T],
                                                   scalar=par[:, GAIN[r] + k:GAIN[r] + k + 1],
                                                   in1=hT_hi[:, k].bitcast(F32), op0=ALU.mult, op1=ALU.subtract
                                                   ).then_inc(h_lo, 1)

            def log1p(y, tmp):
                den, s, s2 = tmp
                link(nc.vector.tensor_scalar(den, y, 2.0, None, ALU.add))
                link(nc.vector.reciprocal(den, den))
                link(nc.vector.tensor_tensor(s, y, den, ALU.mult))
                link(nc.vector.tensor_tensor(s2, s, s, ALU.mult))
                link(nc.vector.tensor_scalar(den, s2, 1.0 / 17, None, ALU.mult))
                for odd in (15, 13, 11, 9, 7, 5, 3):
                    link(nc.vector.scalar_tensor_tensor(out=den, in0=den, scalar=1.0 / odd, in1=s2, op0=ALU.add,
                                                        op1=ALU.mult))
                link(nc.vector.scalar_tensor_tensor(out=den, in0=den, scalar=1.0, in1=s, op0=ALU.add, op1=ALU.mult))
                return den

            def add_to_x(bank, j):
                xj = X[:, :, j * CW:(j + 1) * CW]
                nc.vector.tensor_tensor(xj, ps[:, bank:bank + 2], xj, ALU.add).then_inc(x_done, 1)

            dve.wait_ge(x_in, 32)
            mean_squares(0)
            nc.vector.memset(xpad[:, :, 0:CONV - 1], 0.0).then_inc(edges, 1)
            normalise(0, 1)
            dve.wait_ge(par_T, 1)
            nc.vector.tensor_copy(par[:], ps[:, 7, 0:96]).then_inc(par_done, 1)
            lo_to(2)
            dve.wait_ge(par_done, 1)
            transposed_lo(0)
            lam = par[:, PAR_LAM:PAR_LAM + KT]
            nc.vector.scalar_tensor_tensor(out=lt[:, 0], in0=lam, scalar=-1.0, in1=lam, op0=ALU.mult, op1=ALU.min
                                           ).then_inc(lam_neg, 1)
            dve.wait_ge(lam_exp, 1)
            half_log = log1p(lt[:, 1], (lt[:, 2], lt[:, 3], lt[:, 4]))
            link(nc.vector.tensor_scalar(lt[:, 3], lam, -1.0, 0.0, ALU.mult, ALU.max))
            link(nc.vector.scalar_tensor_tensor(out=lt[:, 1], in0=half_log, scalar=2.0, in1=lt[:, 3], op0=ALU.mult,
                                                op1=ALU.add))
            nc.vector.tensor_scalar(lt[:, 4], lt[:, 1], -LRU_C, None, ALU.mult).then_inc(lam_done, 1)
            nc.vector.tensor_scalar(lt[:, 5], lt[:, 1], LRU_C, None, ALU.mult).then_inc(lam_done, 1)
            dve.wait_ge(edges, 1)
            for ch in range(2):
                lo_to(2 * ch + 3)
                cs = range(4 * ch, 4 * ch + 4)
                for w in range(CONV):
                    for c in cs:
                        src = xpad[:, c, w:w + T]
                        scale = par[:, PAR_CONVW + 8 * w + c:PAR_CONVW + 8 * w + c + 1]
                        if w == 0:
                            dve.wait_ge(xp_in, c // 2 + 1)
                            ins = nc.vector.tensor_scalar(xc[:, c], src, scale, par[:, PAR_CONVB + c:PAR_CONVB + c + 1],
                                                          ALU.mult, ALU.add)
                        else:
                            ins = nc.vector.scalar_tensor_tensor(out=xc[:, c], in0=src, scalar=scale, in1=xc[:, c],
                                                                 op0=ALU.mult, op1=ALU.add)
                        if w == CONV - 1:
                            ins.then_inc(conv_done, 1)
                        elif c == cs[-1]:
                            link(ins)
            lo_to(7)
            lo_to(8)
            for g in range(2):
                q = qf[:, 4 * g:4 * g + 4]
                dve.wait_ge(a_exp, 4 * g + 4)
                link(nc.vector.tensor_tensor(q, av[:, 4 * g:4 * g + 4], av[:, 4 * g:4 * g + 4], ALU.mult))
                dve.wait_ge(th_done, 4 * g + 4)
                nc.vector.scalar_tensor_tensor(out=q, in0=q, scalar=1.0, in1=rg[:, 4 * g:4 * g + 4], op0=ALU.add,
                                               op1=ALU.mult).then_inc(m2_done, 1)
            for g in range(2):
                cs = slice(4 * g, 4 * g + 4)
                dve.wait_ge(mult_done, g + 1)
                dve.wait_ge(gx_done, 2 * g + 2)
                link(nc.vector.tensor_tensor(gi[:, cs], qf[:, cs], gi[:, cs], ALU.mult))
                for c in range(4 * g, 4 * g + 4):
                    ins = nc.vector.tensor_tensor_scan(xc[:, c], av[:, c], gi[:, c], 0.0, ALU.mult, ALU.add)
                link(ins)
                if g == 0:
                    lo_to(9)
                dve.wait_ge(gelu, 2)
                nc.vector.tensor_tensor(yb[:, cs], xc[:, cs], yb[:, cs], ALU.mult).then_inc(z_done, 1)
            for g in range(2):
                cs = slice(4 * g, 4 * g + 4)
                dve.wait_ge(z_hi, g + 1)
                nc.vector.tensor_tensor(hT_lo[:, cs], yb[:, cs], hT_hi[:, cs].bitcast(F32), ALU.subtract
                                        ).then_inc(z_lo, 1)
            dve.wait_ge(consts, 10)
            nc.vector.tensor_copy(ident_r[:], ident[:]).then_inc(const_r, 1)
            nc.vector.tensor_tensor(head_row[:], ident[:, 0:H], ident[:, 32:32 + H], ALU.add).then_inc(const_r, 1)
            nc.vector.tensor_copy(mask_r[:], mask[:]).then_inc(const_r, 1)
            dve.wait_ge(small_in, 16 * 7)
            nc.vector.tensor_scalar(qkg[:, 0:1], qkg[:, 0:1], float(HD) ** -0.5, None, ALU.mult).then_inc(qkg_done, 1)
            for j in range(2):
                lo_to(N_IN + 2 * j + 3)
                dve.wait_ge(used, N_IN + 2 * j + 2)
                add_to_x(2 * j, j)

                if j == 0:
                    dve.wait_ge(small_hi, 2)
                    nc.vector.tensor_tensor(wf2[:, :, H:], wf[:], wf2[:, :, 0:H].bitcast(F32), ALU.subtract
                                            ).then_inc(small_lo, 1)
                    nc.vector.tensor_tensor(rw2[:, :, E:], rw[:], rw2[:, :, 0:E].bitcast(F32), ALU.subtract
                                            ).then_inc(small_lo, 1)

            dve.wait_ge(x_done, 2)
            mean_squares(1)
            normalise(1, 2)
            transposed_lo(1)
            for c in range(FC):
                lo_to(N_FFN + base(c) + 5)
                dve.wait_ge(used, N_FFN + base(c) + 4)
                dve.wait_ge(f_silu, c + 1)
                nc.vector.tensor_tensor(sil[:].rearrange("p c t -> p (c t)"), sil[:].rearrange("p c t -> p (c t)"),
                                        ps[:, 2:4].rearrange("p b n -> p (b n)"), ALU.mult).then_inc(f_act, 1)
                lo_to(N_FFN + base(c) + 6)
                dve.wait_ge(f_ahi, c + 1)
                nc.vector.tensor_tensor(fT_lo[:, c % 2], sil[:], fT_hi[:, c % 2].bitcast(F32), ALU.subtract
                                        ).then_inc(f_alo, 1)
            for j in range(2):
                lo_to(N_FOX + j)
                dve.wait_ge(used, N_FOX - 1 + j)
                add_to_x(4 + 2 * j, j)

            dve.wait_ge(x_done, 4)
            mean_squares(2)
            normalise(2, 3)
            transposed_lo(2)
            for cc in range(6):
                m = N_FOX + 2 * cc + 1
                bank = 2 * (cc % 4)
                lo_to(m + 2)
                if cc < 4:
                    dve.wait_ge(squared, cc + 1)
                    nc.vector.tensor_reduce(ssq[:, 0], junk[:].rearrange("p (h d) -> p h d", d=HD), AX_X, ALU.add
                                            ).then_inc(ssq_done, 1)
                    dve.wait_ge(ssq_done, 2 * cc + 1)
                    nc.vector.tensor_scalar(ssq[:, 1], ssq[:, 0], 1.0 / HD, EPS, ALU.mult, ALU.add
                                            ).then_inc(ssq_done, 1)
                else:
                    dve.wait_ge(v_hi, cc - 3)
                    cols = slice((cc - 4) * CW, (cc - 3) * CW)
                    nc.vector.tensor_tensor(V_lo[:, :, cols], ps[:, bank:bank + 2], V_hi[:, :, cols].bitcast(F32),
                                            ALU.subtract).then_inc(v_lo, 1)
                if cc < 4:
                    dve.wait_ge(pow_done, 3 + cc + 1)
                    nc.vector.tensor_tensor(xn[:, cc % 2].rearrange("p (h d) -> p h d", d=HD),
                                            ps[:, bank:bank + 2].rearrange("p b (h d) -> p (b h) d", d=HD),
                                            ssq[:, 2].unsqueeze(2).to_broadcast([P, TT * 8, HD]), ALU.mult
                                            ).then_inc(qn_done, 1)
                if cc == 0:
                    dve.wait_ge(f_mm, 1)
                    for part in range(2):
                        for t in range(TT):
                            c0 = (2 * t + part) * H
                            ins = nc.vector.tensor_tensor(fx[:, 0, t], ps[:, 7, c0:c0 + H],
                                                          fx[:, 0, t] if part else bf[:], ALU.add)
                        link(ins)
                    nc.vector.scalar_tensor_tensor(out=fx[:, 1], in0=fx[:, 0], scalar=-1.0, in1=fx[:, 0], op0=ALU.mult,
                                                   op1=ALU.min).then_inc(f_neg, 1)
                    dve.wait_ge(f_exp, 1)
                    half_log = log1p(fx[:, 2], (fx[:, 3], fx[:, 4], fx[:, 5]))
                    link(nc.vector.tensor_scalar(fx[:, 6], fx[:, 0], 0.0, None, ALU.min))
                    nc.vector.scalar_tensor_tensor(out=fx[:, 7], in0=half_log, scalar=-2.0, in1=fx[:, 6], op0=ALU.mult,
                                                   op1=ALU.add).then_inc(f_log, 1)
                if cc == 1:
                    dve.wait_ge(f_cum, 1)
                    nc.vector.tensor_scalar(nF[:].rearrange("p t h -> p (t h)"), ps[:, 7, 64:64 + 2 * H], -1.0, None,
                                            ALU.mult).then_inc(f_negF, 1)
                if cc == 4:
                    dve.wait_ge(fT_hi_done, 1)
                    nc.vector.tensor_tensor(nFT[32:32 + H, :], ps[0:H, 4, 0:T], nFT[0:H, :].bitcast(F32),
                                            ALU.subtract).then_inc(fT_lo_done, 1)
                if 1 <= cc <= 4:
                    q = cc - 1
                    hi, lo = (a[:, 4 * (q % 2):4 * (q % 2) + 4].rearrange("p c t -> p (c t)")
                              for a in ((qT_hi, qT_lo) if q < 2 else (kT_hi, kT_lo)))
                    dve.wait_ge(qk_hi, q + 1)
                    dve.wait_ge(qkg_done, 1)
                    nc.vector.scalar_tensor_tensor(out=lo, in0=ps[:, 2 * q:2 * q + 2].rearrange("p b n -> p (b n)"),
                                                   scalar=qkg[:, q // 2:q // 2 + 1], in1=hi.bitcast(F32),
                                                   op0=ALU.mult, op1=ALU.subtract).then_inc(qk_lo, 1)
            def row_max(i):
                a = 3 * (i % 2)
                dve.wait_ge(scored, i + 1)
                nc.vector.tensor_reduce(nm[:, i, 0:4], ps[:, a].rearrange("p (j k) -> p j k", k=P), AX_X, ALU.max,
                                        negate=True).then_inc(nmax, 1)
                nc.vector.tensor_reduce(nm[:, i, 4:8],
                                        ps[:, a + 1:a + 3].rearrange("p b (j k) -> p (b j) k", k=T), AX_X,
                                        ALU.max, negate=True).then_inc(nmax, 1)

            def probs_lo(*rounds):
                for r in rounds:
                    dve.wait_ge(pT_hi_done, r + 1)
                    nc.vector.tensor_tensor(pT_lo[:, r % 2].rearrange("p a k -> p (a k)"),
                                            ps[:, 3 * (r // 3 % 2) + r % 3],
                                            pT_hi[:, r % 2].rearrange("p a k -> p (a k)").bitcast(F32),
                                            ALU.subtract).then_inc(pT_lo_done, 1)

            def outputs(i):
                s, p = i // 2, i % 2
                dve.wait_ge(exped, 8 * i + 8)
                link(nc.vector.reciprocal(rinv[:, i], sm[:, i]))
                dve.wait_ge(pv_done, 3 * i + 3)
                dve.wait_ge(g_sig, s + 1)
                for qt in range(TT):
                    for j in range(4):
                        h = 8 * s + 2 * j + p
                        g = sg[s][:, qt, (h - 8 * s) * HD:(h - 8 * s + 1) * HD]
                        r = 4 * qt + j
                        nc.vector.scalar_tensor_tensor(out=g, in0=ps[:, 3 * (i % 2), r * HD:(r + 1) * HD],
                                                       scalar=rinv[:, i, r:r + 1], in1=g, op0=ALU.mult,
                                                       op1=ALU.mult).then_inc(o_done, 1)
            def outputs_T_lo(*rounds):
                for r in rounds:
                    dve.wait_ge(o_hi, r + 1)
                    nc.vector.tensor_tensor(qT_lo[:, 2 * r:2 * r + 2].rearrange("p k t -> p (k t)"), ps[:, O_BANKS[r]],
                                            qT_hi[:, 2 * r:2 * r + 2].rearrange("p k t -> p (k t)").bitcast(F32),
                                            ALU.subtract).then_inc(o_lo, 1)

            row_max(0)
            lo_to(N_FOX + 14)
            row_max(1)
            lo_to(N_FOXOUT)
            probs_lo(0, 1, 2)
            outputs(0)
            lo_to(N_FOXOUT + 1)
            probs_lo(3, 4)
            row_max(2)
            probs_lo(5)
            outputs(1)
            lo_to(N_FOXOUT + 2)
            probs_lo(6, 7)
            row_max(3)
            probs_lo(8)
            outputs_T_lo(0, 1)
            outputs(2)
            probs_lo(9, 10)
            lo_to(N_FOXOUT + 3)
            probs_lo(11)
            outputs(3)
            outputs_T_lo(2, 3)
            for j in range(2):
                lo_to(N_MOE + j)
                dve.wait_ge(used, N_FOXOUT + j + 3)
                add_to_x(X_BANKS[j], j)

            link(nc.vector.memset(posb[:], 0.0))
            link(nc.vector.memset(combt[:], 0.0))
            rank = tk[:, 1]
            for t in range(TT):
                ins = nc.vector.tensor_scalar(rank[:, t], iota[:, 0:E], -1.0, float(E + 1), ALU.mult, ALU.add)
            link(ins)
            dve.wait_ge(x_done, 6)
            mean_squares(3)
            normalise(3, 8)
            transposed_lo(3)
            lo_to(N_MOE + 2)
            dve.wait_ge(gb_in, 16)
            for t in range(TT):
                dve.wait_ge(xn_done, 7 + t)
                nc.vector.tensor_tensor(hn[:, t], xn[:, t], gb[:], ALU.mult).then_inc(hn_done, 1)
            nc.vector.memset(ST[:].bitcast(F32), 0.0).then_inc(y_zero, 1)
            nc.vector.memset(act_s[:, 0, 0:2], 0.0).then_inc(m_act, 1)
            nc.vector.memset(tk[:, 11, 0], 0.0).then_inc(m_acc, 1)

            def bc(a):
                return a.unsqueeze(2).to_broadcast([P, TT, E])
            dve.wait_ge(routed, 1)
            halves = ps[:, 7, 0:TT * 2 * E].rearrange("p (t h e) -> p t h e", t=TT, h=2)
            link(nc.vector.tensor_copy(tk[:, 10], halves[:, :, 0]))
            link(nc.vector.tensor_tensor(tk[:, 0], halves[:, :, 1], tk[:, 10], ALU.add))

            def pick(src, top, eq, first):
                link(nc.vector.tensor_reduce(tv[:, top], src, AX_X, ALU.max))
                link(nc.vector.tensor_tensor(eq, src, bc(tv[:, top]), ALU.is_equal))
                link(nc.vector.tensor_tensor(eq, eq, rank, ALU.mult))
                link(nc.vector.tensor_reduce(tv[:, 7], eq, AX_X, ALU.max))
                link(nc.vector.tensor_tensor(first, eq, bc(tv[:, 7]), ALU.is_equal))
            pick(tk[:, 0], 0, tk[:, 2], tk[:, 3])
            link(nc.vector.scalar_tensor_tensor(out=tk[:, 4], in0=tk[:, 3], scalar=-BIG, in1=tk[:, 0], op0=ALU.mult,
                                                op1=ALU.add))
            pick(tk[:, 4], 1, tk[:, 5], tk[:, 6])
            nc.vector.tensor_tensor(tk[:, 9], tk[:, 3], tk[:, 6], ALU.add).then_inc(picked, 1)
            nc.vector.tensor_tensor(tv[:, 2], tv[:, 1], tv[:, 0], ALU.subtract).then_inc(w_diff, 1)
            for t in range(TT):
                dve.wait_ge(hn_hi_done, t + 1)
                nc.vector.tensor_tensor(hn_lo[:, t], hn[:, t], hn_hi[:, t].bitcast(F32), ALU.subtract
                                        ).then_inc(hn_lo_done, 1)
            dve.wait_ge(h_lo, 32)
            nc.vector.memset(ps[:, 0:2], 0.0).then_inc(y_zero, 1)
            dve.wait_ge(w_exp, 1)
            link(nc.vector.tensor_scalar(tv[:, 4], tv[:, 3], 1.0, None, ALU.add))
            link(nc.vector.reciprocal(tv[:, 5], tv[:, 4]))
            link(nc.vector.tensor_tensor(tv[:, 6], tv[:, 3], tv[:, 5], ALU.mult))
            link(nc.vector.tensor_tensor(tk[:, 7], tk[:, 3], bc(tv[:, 5]), ALU.mult))
            link(nc.vector.tensor_tensor(tk[:, 8], tk[:, 6], bc(tv[:, 6]), ALU.mult))
            for half in range(2):
                ins = nc.vector.tensor_tensor(combt[:, :, 1 + half * E:1 + (half + 1) * E], tk[:, 7], tk[:, 8], ALU.add)
            link(ins)
            dve.wait_ge(slotted, 1)
            link(nc.vector.tensor_tensor(posb[:, :, 0:E], ps[:, 7, 32:48].rearrange("p (t e) -> p t e", e=E), tk[:, 9],
                                         ALU.mult))
            link(nc.vector.tensor_scalar(posb[:, :, E:2 * E], posb[:, :, 0:E], -float(P), None, ALU.add))
            link(nc.vector.tensor_reduce(cnt[:, 0:1], ps[:, 7, 64:64 + E], AX_X, ALU.max))
            link(nc.vector.tensor_scalar(cnt[:, 1:2], cnt[:, 0:1], float(P) + 0.5, float(E), ALU.is_gt, ALU.mult))
            link(nc.vector.tensor_scalar(cnt[:, 0:1], cnt[:, 1:2], float(E), None, ALU.add))
            nc.vector.tensor_copy(nblk_i[:], cnt[:, 0:1]).then_inc(blocks, 1)

            def one_hot(col, count):
                nc.vector.tensor_copy(pcol[:], posb[:, :, col].rearrange("p t o -> p (t o)")).then_inc(m_col, 1)
                dve.wait_ge(m_col, count)
                for t in range(TT):
                    ins = nc.vector.tensor_scalar(S[:, t], iota[:], pcol[:, t:t + 1], None, ALU.is_equal)
                ins.then_inc(m_S, 1)

            def gathered_lo(count):
                dve.wait_ge(m_xh, count)
                nc.vector.tensor_copy(xg_lo[:].rearrange("p k s -> p (k s)"),
                                      ps[:, 4:6].rearrange("p b n -> p (b n)")).then_inc(m_xl, 1)

            one_hot(slice(0, 1), 1)
            gathered_lo(1)

            def y_to_lo(b):
                dve.wait_ge(m_yhi, at(1, 1, b))
                nc.vector.tensor_tensor(y_lo[:], ps[:, 0:2].rearrange("p b n -> p (b n)"), y_hi[:].bitcast(F32),
                                        ALU.subtract).then_inc(m_ylo, 1)
                nc.vector.tensor_copy(ccol[:], combt[:, :, bass.ds(b, 1)].rearrange("p t o -> p (t o)")
                                      ).then_inc(m_col, 1)

            def accumulate(b, each=None):
                dve.wait_ge(m_scat, at(1, 1, b))
                dve.wait_ge(m_acc, at(1, 1, b))
                dve.wait_ge(m_col, at(2, 2, b))
                for n, bank in enumerate((3, 5, 6, 7)):
                    t, j = n // 2, n % 2
                    xj = X[:, t, j * CW:(j + 1) * CW]
                    ins = nc.vector.scalar_tensor_tensor(out=xj, in0=ps[:, bank], scalar=ccol[:, t:t + 1], in1=xj,
                                                         op0=ALU.mult, op1=ALU.add)
                    if each is not None:
                        ins.then_inc(each, 1)
                if each is None:
                    ins.then_inc(m_acc, 1)

            def act_T_lo(b, c):
                dve.wait_ge(m_thi, at(c + 1, FC, b))
                nc.vector.tensor_tensor(aT_lo[:, c % 2].rearrange("p a s -> p (a s)"), ps[:, 6],
                                        aT_hi[:, c % 2].rearrange("p a s -> p (a s)").bitcast(F32), ALU.subtract
                                        ).then_inc(m_tlo, 1)

            def expert_block(b, converted):
                nxt[0] = converted
                lo_to(1, b)
                y_to_lo(b)
                lo_to(3, b)
                accumulate(b)
                for c in range(FC):
                    lo_to(base(c) + 5, b)
                    dve.wait_ge(used, at(N_MOE + base(c) + 4, FFN_UNITS, b))
                    dve.wait_ge(m_silu, at(c + 2, FC, b))
                    nc.vector.tensor_tensor(act_s[:, c % 2], gt[:, c % 2], ps[:, 4 + c % 2], ALU.mult
                                            ).then_inc(m_act, 1)
                    lo_to(base(c) + 6, b)
                    act_T_lo(b, c)
                    if c == 2:
                        dve.wait_ge(m_TS, at(1, 1, b))
                        one_hot(bass.ds(b + 1, 1), at(3, 2, b))
                lo_to(FFN_UNITS - 1, b)
                gathered_lo(at(2, 1, b))

            expert_block(0, HR)
            dve.wait_ge(blocks, 1)
            nblk = dve.value_load(nblk_i[0:1, 0:1], min_val=E, max_val=2 * E)
            with dve.Fori(1, nblk) as b:
                expert_block(b, 0)
            y_to_lo(nblk)
            accumulate(nblk, m_fin)


_INS = ['x', 'norm_mix', 'norm_ffn', 'lru_w_in', 'lru_conv_w', 'lru_conv_b', 'lru_w_a', 'lru_b_a', 'lru_w_x',
        'lru_b_x', 'lru_log_lambda', 'lru_w_out', 'fox_w_in', 'fox_b_f', 'fox_q_gain', 'fox_k_gain', 'fox_w_out',
        'ffn_w_gate', 'ffn_w_up', 'ffn_w_down', 'moe_router', 'moe_w_gate', 'moe_w_up', 'moe_w_down']
_OUTS = [((1, T, D), 'float32')]


def kernel(**inputs):
    import numpy as _np
    import concourse.bacc as _bacc
    from concourse import mybir as _mybir
    from concourse.bass_utils import run_bass_kernel_spmd as _run

    nc = _bacc.Bacc("TRN2", target_bir_lowering=False, num_devices=1)
    arrays, args = {}, []
    for name in _INS:
        a = _np.ascontiguousarray(inputs[name])
        arrays[f"in_{name}_dram"] = a
        args.append(nc.dram_tensor(f"in_{name}_dram", a.shape, _mybir.dt.from_np(a.dtype), kind="ExternalInput").ap())
    for i, (shape, dtype) in enumerate(_OUTS):
        dt = _mybir.dt.from_np(_np.dtype(dtype))
        args.append(nc.dram_tensor(f"out_{i}_dram", shape, dt, kind="ExternalOutput").ap())
    hybrid_trunk(nc, *args)
    r = _run(nc, [arrays], core_ids=[0])
    return r.results[0]["out_0_dram"]
```

```python
from contextlib import ExitStack

import concourse.bass as bass
from concourse import mybir

P = 128
D = 1024
KT = D // P
T = 256
TT = T // P
F = 3584
CW = 512
UK = 4
FC = F // CW
H = 16
HD = D // H
E = 8
CONV = 4
LRU_C = 8.0
EPS = 1e-6
NEG = -1e30
BIG = 3e38

HR = 3
RR = 7
FFN_UNITS = FC * 6
N_IN = 8
N_FFN = N_IN + 4
N_FOX = N_FFN + FFN_UNITS
N_FOXOUT = N_FOX + 16
N_MOE = N_FOXOUT + 4
EARLY = (N_MOE + FFN_UNITS - RR - 2, N_MOE + FFN_UNITS - RR - 1)
assert FFN_UNITS % HR == 0 and FFN_UNITS % RR == 0

F32 = mybir.dt.float32
F32R = mybir.dt.float32r
I32 = mybir.dt.int32
ALU = mybir.AluOpType
ACT = mybir.ActivationFunctionType
AX_X = mybir.AxisListType.X


def base(c):
    return 0 if c == 0 else 4 + 6 * (c - 1)


def down(c):
    return base(c + 1) + 4 if c < FC - 1 else FFN_UNITS - 2


def early_at(m, b):
    return EARLY.index(m) if (b is None or isinstance(b, int)) and m in EARLY else None


def raw_place(m, b):
    first = b is None or isinstance(b, int)
    if first and m < EARLY[0]:
        return m, m - RR
    return m - len(EARLY), m - RR - (len(EARLY) if first and m <= EARLY[-1] + RR else 0)


def at(count, per, b):
    return count if b is None else b * per + count


def hybrid_trunk(nc, x, norm_mix, norm_ffn, lru_w_in, lru_conv_w, lru_conv_b, lru_w_a, lru_b_a, lru_w_x, lru_b_x,
                 lru_log_lambda, lru_w_out, fox_w_in, fox_b_f, fox_q_gain, fox_k_gain, fox_w_out, ffn_w_gate,
                 ffn_w_up, ffn_w_down, moe_router, moe_w_gate, moe_w_up, moe_w_down, out):
    with ExitStack() as ctx:
        def sem(name):
            return ctx.enter_context(nc.semaphore(name))

        def sb(name, shape, dt=F32, where=None):
            return (where or ctx).enter_context(nc.sbuf_tensor(name, shape, dt))

        ps = ctx.enter_context(nc.psum_tensor("ps", [P, 8, CW], F32))
        raw = sb("raw", [P, RR, UK, CW])
        whi = sb("whi", [P, HR, UK, CW], F32R)
        wlo = sb("wlo", [P, HR, UK, CW], F32R)
        X = sb("X", [P, TT, D])
        rows3 = sb("rows3", [P, 3 * D])
        xn = rows3[:, 0:TT * D].rearrange("p (t d) -> p t d", t=TT)
        junk = rows3[:, TT * D:]
        hT_hi = sb("hT_hi", [P, KT, T], F32R)
        hT_lo = sb("hT_lo", [P, KT, T], F32R)
        ident = sb("ident", [P, P])
        ident_r = sb("ident_r", [P, P], F32R)
        upper = sb("upper", [P, P])
        ones = sb("ones", [P, P])
        mask = sb("mask", [P, T])
        mask_r = sb("mask_r", [P, T], F32R)
        head_row = sb("head_row", [P, H], F32R)
        iota = sb("iota", [P, P])
        par_rows = sb("par_rows", [96, P])
        par = sb("par", [P, 96])
        ss = sb("ss", [P, 8])
        ssh = sb("ssh", [P, 2, 2, TT])
        ms = sb("ms", [P, 8])
        rms2 = sb("rms2", [P, TT])
        rstd = sb("rstd", [P, 8])
        mhalf = sb("mhalf", [P, H])
        PAR_CONVW, PAR_CONVB, PAR_BA, PAR_BX, PAR_LAM, PAR_MIX, PAR_FFN = 0, 32, 40, 48, 56, 64, 80
        GAIN = [PAR_MIX, PAR_FFN, PAR_MIX + KT, PAR_FFN + KT]

        wf = sb("wf", [P, KT, H])
        wf2 = sb("wf2", [P, KT, 2 * H], F32R)
        bf = sb("bf", [P, H])
        qkg = sb("qkg", [P, 2])
        fx = sb("fx", [P, 8, TT, H])
        nF = sb("nF", [P, TT, H])
        nFT = sb("nFT", [P, T], F32R)
        ssq = sb("ssq", [P, 3, TT * 8])
        nm = sb("nm", [P, 4, 8])
        sm = sb("sm", [P, 4, 8])
        rinv = sb("rinv", [P, 4, 8])
        rw = sb("rw", [P, KT, E])
        rw2 = sb("rw2", [P, KT, 2 * E], F32R)
        cnt = sb("cnt", [P, 2])
        nblk_i = sb("nblk_i", [P, 1], I32)

        with ExitStack() as a1:
            xpad = sb("xpad", [P, KT, CONV - 1 + T], where=a1)
            xc = sb("xc", [P, KT, T], where=a1)
            rg = sb("rg", [P, KT, T], where=a1)
            gi = sb("gi", [P, KT, T], where=a1)
            av = sb("av", [P, KT, T], where=a1)
            yb = sb("yb", [P, KT, T], where=a1)
            wax = yb[:].rearrange("p k t -> p (k t)").rearrange("p (g c j) -> p g c j", g=2, c=KT)
            lt = sb("lt", [P, 6, 8], where=a1)
        with ExitStack() as a2:
            sil = sb("sil", [P, 4, T], where=a2)
            fT_hi = sb("fT_hi", [P, 2, 4, T], F32R, where=a2)
            fT_lo = sb("fT_lo", [P, 2, 4, T], F32R, where=a2)
        with ExitStack() as a3:
            qT_hi = sb("qT_hi", [P, KT, T], F32R, where=a3)
            qT_lo = sb("qT_lo", [P, KT, T], F32R, where=a3)
            V_hi = sb("V_hi", [P, TT, D], F32R, where=a3)
            V_lo = sb("V_lo", [P, TT, D], F32R, where=a3)
            pT_hi = sb("pT_hi", [P, 2, 4, P], F32R, where=a3)
            pT_lo = sb("pT_lo", [P, 2, 4, P], F32R, where=a3)
            with ExitStack() as k3:
                kT_hi = sb("kT_hi", [P, KT, T], F32R, where=k3)
                kT_lo = sb("kT_lo", [P, KT, T], F32R, where=k3)
            with ExitStack() as g3:
                sg = [sb("sg_a", [P, TT, CW], where=g3)]
                sb("kT_hi_rest", [P, KT // 2, T], where=g3)
                sg.append(sb("sg_b", [P, TT, CW], where=g3))
        with ExitStack() as a4:
            hn = sb("hn", [P, TT, D], where=a4)
            hn_hi = sb("hn_hi", [P, TT, D], F32R, where=a4)
            hn_lo = sb("hn_lo", [P, TT, D], F32R, where=a4)
            gb = sb("gb", [P, D], where=a4)
            gt = sb("gt", [P, 2, CW], where=a4)
            act_s = sb("act_s", [P, 2, CW], where=a4)
            aT_hi = sb("aT_hi", [P, 2, 4, P], F32R, where=a4)
            aT_lo = sb("aT_lo", [P, 2, 4, P], F32R, where=a4)
            S = sb("S", [P, TT, P], F32R, where=a4)
            ST = sb("ST", [P, T], F32R, where=a4)
            tk = sb("tk", [P, 12, TT, E], where=a4)
            tv = sb("tv", [P, 8, TT], where=a4)
            early_b = sb("early_b", [P, UK, CW], where=a4)
            posb = sb("posb", [P, TT, 2 * E + 1], where=a4)
            combt = sb("combt", [P, TT, 2 * E + 1], where=a4)
            pcol = sb("pcol", [P, TT], where=a4)
            ccol = sb("ccol", [P, TT], where=a4)
        probs = [rows3[:, i * 12 * P:(i + 1) * 12 * P].rearrange("p (a k) -> p a k", k=P) for i in range(2)]
        qf = xpad[:, :, 0:T]
        early = [rows3[:, 0:UK * CW].rearrange("p (k n) -> p k n", k=UK), early_b[:]]
        hTf_hi, hTf_lo = (h[:].rearrange("p k t -> p (k t)") for h in (hT_hi, hT_lo))
        xg_hi, xg_lo = (h[:, 0:D].rearrange("p (k s) -> p k s", s=P) for h in (hTf_hi, hTf_lo))
        y_hi, y_lo = hTf_hi[:, D:2 * D], hTf_lo[:, D:2 * D]

        O_BANKS = (6, 7, 1, 2)
        SCATTER_BANKS = ((2, 3), (6, 7))
        X_BANKS = (6, 4)

        landed = [sem(f"landed{i}") for i in range(RR)]
        hi_done = sem("hi_done")
        lo_done = sem("lo_done")
        used = sem("used")
        x_in, par_in, wax_in, small_in, gb_in = (sem(s) for s in ("x_in", "par_in", "wax_in", "small_in", "gb_in"))
        consts, pow_done, gx_done = sem("consts"), sem("pow_done"), sem("gx_done")
        par_T, xn_T, gate_r, gate_i, f_mm, f_cum, f_T, qk_T, scored, probs_T, pv_done, o_T, routed, slotted = (
            sem(s) for s in ("par_T", "xn_T", "gate_r", "gate_i", "f_mm", "f_cum", "f_T", "qk_T", "scored",
                             "probs_T", "pv_done", "o_T", "routed", "slotted"))
        sumsq, h_hi, lam_exp, small_hi, xp_in, gelu, sig_r, sig_i, a_exp, th_done, mult_done, z_hi = (
            sem(s) for s in ("sumsq", "h_hi", "lam_exp", "small_hi", "xp_in", "gelu", "sig_r", "sig_i", "a_exp",
                             "th_done", "mult_done", "z_hi"))
        f_silu, f_ahi, squared, f_exp, fT_hi_done, qk_hi, v_hi, g_sig, exped, pT_hi_done, o_hi, w_exp, hn_hi_done = (
            sem(s) for s in ("f_silu", "f_ahi", "squared", "f_exp", "fT_hi_done", "qk_hi", "v_hi", "g_sig",
                             "exped", "pT_hi_done", "o_hi", "w_exp", "hn_hi_done"))
        chain, par_done, ms_done, xn_done, h_lo, conv_done, lam_neg, lam_done, small_lo, m2_done, z_done, z_lo = (
            sem(s) for s in ("chain", "par_done", "ms_done", "xn_done", "h_lo", "conv_done", "lam_neg", "lam_done",
                             "small_lo", "m2_done", "z_done", "z_lo"))
        x_done, f_act, f_alo, f_neg, f_log, f_negF, fT_lo_done, ssq_done, qn_done, qk_lo, v_lo, nmax = (
            sem(s) for s in ("x_done", "f_act", "f_alo", "f_neg", "f_log", "f_negF", "fT_lo_done", "ssq_done",
                             "qn_done", "qk_lo", "v_lo", "nmax"))
        pT_lo_done, o_done, o_lo, hn_done, hn_lo_done, picked, w_diff, blocks, zeros, edges, qkg_done, const_r = (
            sem(s) for s in ("pT_lo_done", "o_done", "o_lo", "hn_done", "hn_lo_done", "picked", "w_diff", "blocks",
                             "zeros", "edges", "qkg_done", "const_r"))
        m_scat, m_T, m_TS, m_gat = (sem(s) for s in ("m_scat", "m_T", "m_TS", "m_gat"))
        m_yhi, m_silu, m_thi, m_ST, m_xh = (sem(s) for s in ("m_yhi", "m_silu", "m_thi", "m_ST", "m_xh"))
        m_ylo, m_acc, m_act, m_tlo, m_S, m_xl, m_col, m_fin = (
            sem(s) for s in ("m_ylo", "m_acc", "m_act", "m_tlo", "m_S", "m_xl", "m_col", "m_fin"))
        out_done, sumsq_v, par_in2 = sem("out_done"), sem("sumsq_v"), sem("par_in2")
        early_in = [sem(f"early_in{i}") for i in range(len(EARLY))]

        def unit_of(w, rows, col):
            return w[rows * P:(rows + UK) * P, col * CW:(col + 1) * CW].rearrange("(k p) n -> p k n", p=P)

        def swiglu_units(gate, up, dn):
            def d(c):
                return [(dn, c * UK, j) for j in range(2)]
            for c in range(FC):
                yield from [(gate, 0, c), (gate, UK, c), (up, 0, c), (up, UK, c)]
                if c:
                    yield from d(c - 1)
            yield from d(FC - 1)

        def front_units():
            for col in (2, 3, 0, 1):
                for rows in (0, UK):
                    yield lru_w_in[0], rows, col
            for col in (0, 1):
                for rows in (0, UK):
                    yield lru_w_out[0], rows, col
            yield from swiglu_units(ffn_w_gate[0], ffn_w_up[0], ffn_w_down[0])
            for col in range(8):
                for rows in (0, UK):
                    yield fox_w_in[0], rows, col
            for rows in (0, UK):
                for col in (0, 1):
                    yield fox_w_out[0], rows, col

        expert_w = [w.rearrange("a e d f -> (a e) d f") for w in (moe_w_gate, moe_w_up, moe_w_down)]
        def rows_of(w):
            return w.rearrange("a (c p) -> (a c) p", p=P)

        par_loads = [(par_rows[r0:r0 + n, :], src) for r0, n, src in (
            (PAR_CONVW, 32, rows_of(lru_conv_w[0])), (PAR_CONVB, 8, rows_of(lru_conv_b)),
            (PAR_BA, 8, rows_of(lru_b_a)), (PAR_BX, 8, rows_of(lru_b_x)), (PAR_LAM, 8, rows_of(lru_log_lambda)),
            (PAR_MIX, 16, rows_of(norm_mix)), (PAR_FFN, 16, rows_of(norm_ffn)))]
        block = ctx.enter_context(nc.Block())

        @block.sync
        def _(sp):
            for t in range(TT):
                sp.dma_start(X[:, t], x[0, t * P:(t + 1) * P, :]).then_inc(x_in, 16)
            for load in par_loads[4:]:
                sp.dma_start(*load).then_inc(par_in2, 16)
            for n, (w, rows, col) in enumerate(front_units()):
                if n >= RR:
                    sp.wait_ge(lo_done, n - RR + 1)
                sp.dma_start(raw[:, n % RR], unit_of(w, rows, col)).then_inc(landed[n % RR], 16)
                if n == 4:
                    sp.dma_start(wax[:, 0], lru_w_a[0].rearrange("h i j -> i h j")).then_inc(wax_in, 16)
                    sp.dma_start(wax[:, 1], lru_w_x[0].rearrange("h i j -> i h j")).then_inc(wax_in, 16)

            units = list(swiglu_units(*expert_w))

            def expert_load(i, b, e):
                w, rows, col = units[i]
                src = w[bass.ds(e, 1), rows * P:(rows + UK) * P, col * CW:(col + 1) * CW].rearrange(
                    "o (k p) n -> p (o k) n", p=P)
                m = N_MOE + i
                n = early_at(m, b)
                if n is not None:
                    sp.dma_start(early[n], src).then_inc(early_in[n], 16)
                else:
                    pos, before = raw_place(m, b)
                    sp.wait_ge(lo_done, at(before + 1, FFN_UNITS, b))
                    sp.dma_start(raw[:, pos % RR], src).then_inc(landed[pos % RR], 16)

            for i in range(5):
                expert_load(i, None, 0)
            sp.wait_ge(probs_T, 12)
            expert_load(EARLY[0] - N_MOE, None, 0)
            for i in (5, 6):
                expert_load(i, None, 0)
            sp.wait_ge(o_T, 4)
            expert_load(EARLY[1] - N_MOE, None, 0)
            for i in range(7, FFN_UNITS):
                if N_MOE + i not in EARLY:
                    expert_load(i, None, 0)

            def expert_loads(b, e):
                for i in range(FFN_UNITS):
                    expert_load(i, b, e)

            with sp.Fori(1, E) as b:
                expert_loads(b, b)
            sp.wait_ge(blocks, 1)
            nblk = sp.value_load(nblk_i[0:1, 0:1], min_val=E, max_val=2 * E)
            with sp.If(nblk > E):
                with sp.Fori(E, 2 * E) as b:
                    expert_loads(b, b - E)
            for n in range(4):
                j, t = n // 2, n % 2
                sp.wait_ge(m_fin, n + 1)
                sp.dma_start(out[0, t * P:(t + 1) * P, j * CW:(j + 1) * CW], X[:, t, j * CW:(j + 1) * CW]
                             ).then_inc(out_done, 16)
            sp.wait_ge(out_done, 64)

        @block.gpsimd
        def _(pool):
            pool.memset(ident[:], 0.0).then_inc(consts, 1)
            pool.memset(upper[:], 1.0).then_inc(consts, 1)
            pool.memset(mask[:], 0.0).then_inc(consts, 1)
            pool.memset(ones[:], 1.0).then_inc(consts, 1)
            pool.memset(mhalf[:], -0.5).then_inc(consts, 1)
            pool.iota(iota[:], [[1, P]], base=1, channel_multiplier=0,
                      allow_small_or_imprecise_dtypes=True).then_inc(consts, 1)
            pool.wait_ge(consts, 6)
            pool.affine_select(out=ident[:], in_=ident[:], compare_op=ALU.not_equal, fill=1.0, base=0,
                               pattern=[[-1, P]], channel_multiplier=1).then_inc(consts, 1)
            pool.affine_select(out=upper[:], in_=upper[:], compare_op=ALU.is_ge, fill=0.0, base=0,
                               pattern=[[1, P]], channel_multiplier=-1).then_inc(consts, 1)
            pool.affine_select(out=mask[:, P:T], in_=mask[:, P:T], compare_op=ALU.is_ge, fill=NEG, base=0,
                               pattern=[[-1, P]], channel_multiplier=1).then_inc(consts, 1)
            pool.memset(nFT[:].bitcast(F32), 0.0).then_inc(consts, 1)
            def rms_pow(r):
                pool.wait_ge(ms_done, r + 1)
                pool.tensor_tensor(rstd[:, 2 * r:2 * r + 2], ms[:, 2 * r:2 * r + 2], mhalf[:, 0:2],
                                   ALU.pow).then_inc(pow_done, 1)
            rms_pow(0)
            pool.dma_start(wf[:], fox_w_in[0][:, 4 * D:4 * D + H].rearrange("(k p) h -> p k h", p=P)
                           ).then_inc(small_in, 16)
            pool.dma_start(rw[:], moe_router[0].rearrange("(k p) e -> p k e", p=P)).then_inc(small_in, 16)
            pool.dma_start(bf[:], fox_b_f[0].partition_broadcast(P)).then_inc(small_in, 16)
            for half in range(2):
                for i, g in enumerate((fox_q_gain, fox_k_gain)):
                    pool.dma_start(qkg[half * HD:(half + 1) * HD, i:i + 1], g.rearrange("a d -> d a")
                                   ).then_inc(small_in, 16)
            for g in range(4):
                pool.wait_ge(sig_i, 2 * g + 2)
                pool.tensor_tensor(gi[:, 2 * g:2 * g + 2], gi[:, 2 * g:2 * g + 2], xc[:, 2 * g:2 * g + 2],
                                   ALU.mult).then_inc(gx_done, 1)
            rms_pow(1)
            rms_pow(2)
            for cc in range(4):
                pool.wait_ge(ssq_done, 2 * cc + 2)
                pool.tensor_tensor(ssq[:, 2], ssq[:, 1], mhalf[:], ALU.pow).then_inc(pow_done, 1)
                pool.wait_ge(pow_done, 3 + 2 * cc + 1)
                pool.tensor_tensor(ssq[:, 2].rearrange("p (t h) -> p t h", t=TT),
                                   ssq[:, 2].rearrange("p (t h) -> p t h", t=TT),
                                   rstd[:, 4:6].unsqueeze(2).to_broadcast([P, TT, 8]), ALU.mult).then_inc(pow_done, 1)
            pool.wait_ge(o_T, 4)
            pool.dma_start(gb[:], norm_ffn[1].partition_broadcast(P)).then_inc(gb_in, 16)
            pool.wait_ge(x_done, 6)
            pool.memset(posb[:], 0.0).then_inc(zeros, 1)
            pool.memset(combt[:], 0.0).then_inc(zeros, 1)
            pool.memset(ST[:].bitcast(F32), 0.0).then_inc(zeros, 1)
            rms_pow(3)
            pool.wait_ge(routed, 1)
            pool.memset(y_hi[:].bitcast(F32), 0.0).then_inc(zeros, 1)
            pool.memset(y_lo[:].bitcast(F32), 0.0).then_inc(zeros, 1)

        @block.scalar
        def _(act):
            nxt = [0]

            def hi_to(n, b=None):
                first = 0 if b is None else N_MOE
                last = N_MOE + HR - 1 if b is None else N_MOE + FFN_UNITS - 1
                while first + nxt[0] <= min(first + n, last):
                    m = first + nxt[0]
                    n_early = early_at(m, b)
                    if n_early is not None:
                        src = early[n_early]
                        act.wait_ge(early_in[n_early], 16)
                    else:
                        pos = raw_place(m, b)[0]
                        src = raw[:, pos % RR]
                        act.wait_ge(landed[pos % RR], at(16 * (pos // RR + 1), 16 * FFN_UNITS // RR, b))
                    if m >= HR:
                        act.wait_ge(used, at(m - HR + 1, FFN_UNITS, b))
                    nc.scalar.activation(whi[:, m % HR], src, ACT.Copy).then_inc(hi_done, 1)
                    nxt[0] += 1

            def squares(r):
                if r:
                    act.wait_ge(sumsq, r)
                nc.scalar.activation(junk[:], X[:, 0, :], ACT.Square, accum_out=ss[:, 2 * r:2 * r + 1]
                                     ).then_inc(sumsq, 1)

            def stream_squares(r, half):
                for t in range(TT):
                    act.wait_ge(x_done, 2 * r - 1 + half)
                    act.wait_ge(sumsq, 4 * r - 6 + 2 * half + t)
                    nc.scalar.activation(junk[:, 0:CW], X[:, t, half * CW:(half + 1) * CW], ACT.Square,
                                         accum_out=ssh[:, r % 2, half, t:t + 1]).then_inc(sumsq, 1)

            def transposed_hi(r):
                for k in range(KT):
                    act.wait_ge(xn_T, 4 * r + k // 2 + 1)
                    nc.scalar.activation(hT_hi[:, k], ps[:, k // 2, (k % 2) * T:(k % 2 + 1) * T], ACT.Copy,
                                         scale=par[:, GAIN[r] + k:GAIN[r] + k + 1]).then_inc(h_hi, 1)

            for load in par_loads[0:4]:
                act.dma_start(*load).then_inc(par_in, 16)
            act.wait_ge(x_in, 32)
            squares(0)
            hi_to(0)
            act.wait_ge(par_done, 1)
            transposed_hi(0)
            hi_to(2)
            act.wait_ge(lam_neg, 1)
            nc.scalar.activation(lt[:, 1], lt[:, 0], ACT.Exp).then_inc(lam_exp, 1)
            for ch in range(2):
                hi_to(2 * ch + 3)
                act.wait_ge(used, 2 * ch + 2)
                for i in range(2):
                    bank = 4 + 2 * ch + i
                    nc.scalar.activation(xpad[:, 4 * ch + 2 * i:4 * ch + 2 * i + 2, CONV - 1:],
                                         ps[:, bank].rearrange("p (c t) -> p c t", t=T), ACT.Copy).then_inc(xp_in, 1)
            for ch in range(2):
                hi_to(6 + ch)
                for ready, done, dst, par0, bank0 in ((gate_r, sig_r, rg, PAR_BA, 4), (gate_i, sig_i, gi, PAR_BX, 6)):
                    for i in range(4):
                        c = 4 * ch + i
                        act.wait_ge(ready, 2 * (c // 2) + 2)
                        nc.scalar.activation(dst[:, c], ps[:, bank0 + i // 2, (i % 2) * T:(i % 2 + 1) * T],
                                             ACT.Sigmoid, bias=par[:, par0 + c:par0 + c + 1]).then_inc(done, 1)
            act.wait_ge(lam_done, 2)
            act.wait_ge(sig_r, KT)
            for c in range(KT):
                nc.scalar.activation(av[:, c], rg[:, c], ACT.Exp, scale=lt[:, 4, c:c + 1]).then_inc(a_exp, 1)
                nc.scalar.activation(rg[:, c], rg[:, c], ACT.Tanh, scale=lt[:, 5, c:c + 1]).then_inc(th_done, 1)
                if c == 3:
                    hi_to(8)
            for g in range(2):
                act.wait_ge(m2_done, g + 1)
                nc.scalar.activation(qf[:, 4 * g:4 * g + 4], qf[:, 4 * g:4 * g + 4], ACT.Sqrt).then_inc(mult_done, 1)
            for ch in range(2):
                act.wait_ge(used, 2 * ch + 6)
                nc.scalar.activation(yb[:, 4 * ch:4 * ch + 4].rearrange("p c t -> p (c t)"),
                                     ps[:, 2 * ch:2 * ch + 2].rearrange("p b n -> p (b n)"),
                                     ACT.Gelu_apprx_tanh).then_inc(gelu, 1)
            for g in range(2):
                act.wait_ge(z_done, g + 1)
                nc.scalar.activation(hT_hi[:, 4 * g:4 * g + 4], yb[:, 4 * g:4 * g + 4], ACT.Copy).then_inc(z_hi, 1)
                if g == 0:
                    hi_to(9)
            hi_to(N_FFN)
            act.wait_ge(small_in, 16 * 7)
            nc.scalar.activation(wf2[:, :, 0:H], wf[:], ACT.Copy).then_inc(small_hi, 1)
            nc.scalar.activation(rw2[:, :, 0:E], rw[:], ACT.Copy).then_inc(small_hi, 1)
            hi_to(N_FFN + 1)

            act.wait_ge(x_done, 2)
            squares(1)
            transposed_hi(1)
            for c in range(FC):
                hi_to(N_FFN + base(c) + 3)
                act.wait_ge(used, N_FFN + base(c) + 2)
                if c:
                    act.wait_ge(f_alo, c)
                nc.scalar.activation(sil[:].rearrange("p c t -> p (c t)"),
                                     ps[:, 0:2].rearrange("p b n -> p (b n)"), ACT.Silu).then_inc(f_silu, 1)
                hi_to(N_FFN + base(c) + 6)
                act.wait_ge(f_act, c + 1)
                nc.scalar.activation(fT_hi[:, c % 2], sil[:], ACT.Copy).then_inc(f_ahi, 1)
            hi_to(N_FOX + 1)

            stream_squares(2, 0)
            transposed_hi(2)
            stream_squares(2, 1)
            for cc in range(6):
                m = N_FOX + 2 * cc + 1
                bank = 2 * (cc % 4)
                hi_to(m + 2)
                act.wait_ge(used, m + 1)
                both = ps[:, bank:bank + 2].rearrange("p b n -> p (b n)")
                if cc < 4:
                    if cc:
                        act.wait_ge(ssq_done, 2 * cc)
                    else:
                        act.wait_ge(sumsq, 6)
                    nc.scalar.activation(junk[:], both, ACT.Square).then_inc(squared, 1)
                else:
                    for t in range(TT):
                        nc.scalar.activation(V_hi[:, t, (cc - 4) * CW:(cc - 3) * CW], ps[:, bank + t], ACT.Copy,
                                             scale=rstd[:, 4 + t:5 + t]).then_inc(v_hi, 1)
                if cc == 0:
                    act.wait_ge(f_neg, 1)
                    nc.scalar.activation(fx[:, 2], fx[:, 1], ACT.Exp).then_inc(f_exp, 1)
                if cc == 4:
                    act.wait_ge(f_T, 1)
                    nc.scalar.activation(nFT[0:H, :], ps[0:H, 4, 0:T], ACT.Copy).then_inc(fT_hi_done, 1)
                if 1 <= cc <= 4:
                    q = cc - 1
                    dst = (qT_hi if q < 2 else kT_hi)[:, 4 * (q % 2):4 * (q % 2) + 4]
                    act.wait_ge(qk_T, q + 1)
                    nc.scalar.activation(dst.rearrange("p c t -> p (c t)"),
                                         ps[:, 2 * q:2 * q + 2].rearrange("p b n -> p (b n)"), ACT.Copy,
                                         scale=qkg[:, q // 2:q // 2 + 1]).then_inc(qk_hi, 1)
            def exps(i):
                a = 3 * (i % 2)
                act.wait_ge(nmax, 2 * i + 2)
                for j in range(4):
                    nc.scalar.activation(probs[i % 2][:, j], ps[:, a, j * P:(j + 1) * P], ACT.Exp,
                                         bias=nm[:, i, j:j + 1], accum_out=sm[:, i, j:j + 1]).then_inc(exped, 1)
                for j in range(4):
                    nc.scalar.activation(probs[i % 2][:, 4 + 2 * j:6 + 2 * j].rearrange("p a k -> p (a k)"),
                                         ps[:, a + 1 + j // 2, (j % 2) * T:(j % 2 + 1) * T], ACT.Exp,
                                         bias=nm[:, i, 4 + j:5 + j], accum_out=sm[:, i, 4 + j:5 + j]
                                         ).then_inc(exped, 1)
            def probs_hi(*rounds):
                for r in rounds:
                    act.wait_ge(probs_T, r + 1)
                    if r >= 2:
                        act.wait_ge(pv_done, r - 1)
                    nc.scalar.activation(pT_hi[:, r % 2].rearrange("p a k -> p (a k)"),
                                         ps[:, 3 * (r // 3 % 2) + r % 3], ACT.Copy).then_inc(pT_hi_done, 1)

            def gate_sigmoid(half):
                act.wait_ge(used, N_FOX + 14 + 2 * half)
                for t in range(TT):
                    nc.scalar.activation(sg[half][:, t], ps[:, 6 + t], ACT.Sigmoid, scale=rstd[:, 4 + t:5 + t]
                                         ).then_inc(g_sig, 1)

            def outputs_T_hi(*rounds):
                for r in rounds:
                    act.wait_ge(o_T, r + 1)
                    nc.scalar.activation(qT_hi[:, 2 * r:2 * r + 2].rearrange("p k t -> p (k t)"), ps[:, O_BANKS[r]],
                                         ACT.Copy).then_inc(o_hi, 1)

            exps(0)
            hi_to(N_FOX + 15)
            act.wait_ge(scored, 2)
            gate_sigmoid(0)
            probs_hi(0, 1)
            exps(1)
            probs_hi(2)
            hi_to(N_FOXOUT)
            hi_to(N_FOXOUT + 1)
            probs_hi(3, 4)
            exps(2)
            probs_hi(5)
            hi_to(N_FOXOUT + 2)
            gate_sigmoid(1)
            probs_hi(6, 7)
            exps(3)
            probs_hi(8)
            outputs_T_hi(0, 1)
            probs_hi(9, 10)
            probs_hi(11)
            hi_to(N_FOXOUT + 3)
            outputs_T_hi(2, 3)
            hi_to(N_MOE + 1)

            stream_squares(3, 0)
            transposed_hi(3)
            stream_squares(3, 1)
            hi_to(N_MOE + 2)
            for t in range(TT):
                act.wait_ge(hn_done, t + 1)
                nc.scalar.activation(hn_hi[:, t], hn[:, t], ACT.Copy).then_inc(hn_hi_done, 1)
            act.wait_ge(w_diff, 1)
            nc.scalar.activation(tv[:, 3], tv[:, 2], ACT.Exp).then_inc(w_exp, 1)

            def gathered_hi(b):
                act.wait_ge(m_gat, at(1, 2, b))
                nc.scalar.activation(xg_hi[:].rearrange("p k s -> p (k s)"),
                                     ps[:, 2:4].rearrange("p b n -> p (b n)"), ACT.Copy).then_inc(m_xh, 1)
            nc.scalar.activation(junk[:, 0:2], junk[:, 0:2], ACT.Copy).then_inc(m_silu, 1)

            def y_to_hi(b):
                act.wait_ge(used, at(N_MOE, FFN_UNITS, b))
                nc.scalar.activation(y_hi[:], ps[:, 0:2].rearrange("p b n -> p (b n)"), ACT.Copy).then_inc(m_yhi, 1)

            def act_T_hi(b, c):
                act.wait_ge(m_T, at(c + 1, FC, b))
                nc.scalar.activation(aT_hi[:, c % 2].rearrange("p a s -> p (a s)"), ps[:, 6], ACT.Copy
                                     ).then_inc(m_thi, 1)

            def expert_block(b, converted, first=False):
                nxt[0] = converted
                hi_to(1, b)
                if not first:
                    y_to_hi(b)
                gathered_hi(b)
                for c in range(FC):
                    if c == 1:
                        hi_to(6, b)
                        act.wait_ge(m_TS, at(1, 1, b))
                        nc.scalar.activation(ST[:], ps[:, 7, 0:T], ACT.Copy).then_inc(m_ST, 1)
                        act_T_hi(b, 0)
                    hi_to(base(c) + 3, b)
                    act.wait_ge(used, at(N_MOE + base(c) + 2, FFN_UNITS, b))
                    act.wait_ge(m_act, at(max(c, 1), FC, b))
                    nc.scalar.activation(gt[:, c % 2], ps[:, 4 + c % 2], ACT.Silu).then_inc(m_silu, 1)
                    if c:
                        hi_to(base(c) + 6, b)
                        act_T_hi(b, c)
                hi_to(FFN_UNITS - 1, b)

            expert_block(0, HR, first=True)
            act.wait_ge(blocks, 1)
            nblk = act.value_load(nblk_i[0:1, 0:1], min_val=E, max_val=2 * E)
            with act.Fori(1, nblk) as b:
                expert_block(b, 0)
            for j in range(2):
                act.wait_ge(used, at(N_MOE - 1 + j, FFN_UNITS, nblk))
                nc.scalar.activation(y_hi[:, j * CW:(j + 1) * CW], ps[:, j], ACT.Copy).then_inc(m_yhi, 1)

        @block.tensor
        def _(pe):
            mm = nc.tensor.matmul

            def tokens_unit(m, b, src, k0, tiles, dst, first, last):
                pe.wait_ge(lo_done, at(m + 1, FFN_UNITS, b))
                for k in range(UK):
                    for t in range(tiles):
                        hi, lo = src(k0 + k, t)
                        mm(dst(t), hi, whi[:, m % HR, k], start=first and k == 0, stop=False)
                        mm(dst(t), hi, wlo[:, m % HR, k], start=False, stop=False)
                        ins = mm(dst(t), lo, whi[:, m % HR, k], start=False, stop=last and k == UK - 1)
                ins.then_inc(used, 1)

            def weights_unit(m, bank, half):
                pe.wait_ge(lo_done, m + 1)
                for c in range(4):
                    dst = ps[:, bank + c // 2, (c % 2) * T:(c % 2 + 1) * T]
                    for k in range(UK):
                        kk = half * UK + k
                        wh, wl = (w[:, m % HR, k, c * P:(c + 1) * P] for w in (whi, wlo))
                        mm(dst, wh, hT_hi[:, kk], start=half == 0 and k == 0 and c % 2 == 0, stop=False,
                           skip_group_check=True)
                        mm(dst, wh, hT_lo[:, kk], start=False, stop=False, skip_group_check=True)
                        ins = mm(dst, wl, hT_hi[:, kk], start=False, stop=half == 1 and k == UK - 1,
                                 skip_group_check=True)
                ins.then_inc(used, 1)

            def transposes(src, done, banks=(0, 1, 2, 3), k0=0):
                for n, bank in enumerate(banks):
                    for k in range(2):
                        for t in range(TT):
                            ins = nc.tensor.transpose(ps[:, bank, k * T + t * P:k * T + (t + 1) * P],
                                                      src(t, k0 + 2 * n + k), ident[:])
                    ins.then_inc(done, 1)

            def of_xn(t, k):
                return xn[:, t, k * P:(k + 1) * P]

            def stream_transposes(count):
                for half in range(2):
                    pe.wait_ge(x_done, count + half)
                    transposes(lambda t, k: X[:, t, k * P:(k + 1) * P], xn_T, (2 * half, 2 * half + 1), UK * half)

            def of_hT(k, t):
                return hT_hi[:, k, t * P:(t + 1) * P], hT_lo[:, k, t * P:(t + 1) * P]

            pe.wait_ge(consts, 9)
            pe.wait_ge(par_in, 16 * 4)
            pe.wait_ge(par_in2, 16 * 3)
            nc.tensor.transpose(ps[:, 7, 0:96], par_rows[:], ident[0:96, 0:96]).then_inc(par_T, 1)
            pe.wait_ge(xn_done, 2)
            transposes(of_xn, xn_T)
            def lru_gates(ch):
                for g, (bank0, done, read) in enumerate(((4, gate_r, sig_r), (6, gate_i, sig_i))):
                    for i in range(4):
                        c = 4 * ch + i
                        if g == 0:
                            pe.wait_ge(conv_done, c + 1)
                        if i == 0 and ch:
                            pe.wait_ge(read, 4)
                        mm(ps[:, bank0 + i // 2, (i % 2) * T:(i % 2 + 1) * T], wax[:, g, c], xc[:, c],
                           start=i % 2 == 0, stop=True, skip_group_check=True).then_inc(done, 1)

            for n in range(8):
                if n < 2:
                    pe.wait_ge(h_lo, 4 * n + 4)
                if n == 0:
                    pe.wait_ge(par_done, 1)
                weights_unit(n, (4, 6, 0, 2)[n // 2], n % 2)
                if n == 4:
                    pe.wait_ge(wax_in, 32)
                    pe.wait_ge(xp_in, 4)
                    for ch in range(2):
                        lru_gates(ch)
            for i in range(4):
                if i < 2:
                    pe.wait_ge(z_lo, i + 1)
                tokens_unit(N_IN + i, None, of_hT, UK * (i % 2), TT, lambda t: ps[:, 2 * (i // 2) + t],
                            i % 2 == 0, i % 2 == 1)

            pe.wait_ge(xn_done, 4)
            transposes(of_xn, xn_T)

            def ffn_down(c):
                pe.wait_ge(f_alo, c + 1)
                for j in range(2):
                    tokens_unit(N_FFN + down(c) + j, None,
                                lambda k, t: (fT_hi[:, c % 2, k, t * P:(t + 1) * P],
                                              fT_lo[:, c % 2, k, t * P:(t + 1) * P]),
                                0, TT, lambda t: ps[:, 4 + 2 * j + t], c == 0, c == FC - 1)

            for c in range(FC):
                n = N_FFN + base(c)
                for half in range(2):
                    if c == 0:
                        pe.wait_ge(h_lo, 8 + 4 * half + 4)
                    elif half == 0:
                        pe.wait_ge(f_silu, c)
                    weights_unit(n + half, 0, half)
                if c:
                    pe.wait_ge(f_act, c)
                for half in range(2):
                    weights_unit(n + 2 + half, 2, half)
                if c:
                    ffn_down(c - 1)
            ffn_down(FC - 1)

            stream_transposes(3)

            def qk_transposes(q):
                pe.wait_ge(qn_done, q + 1)
                src = xn[:, q % 2].rearrange("p (t n) -> p t n", t=TT)
                for c in range(4):
                    for t in range(TT):
                        ins = nc.tensor.transpose(ps[:, 2 * q + c // 2, (c % 2) * T + t * P:(c % 2) * T + (t + 1) * P],
                                                  src[:, t, c * P:(c + 1) * P], ident[:])
                ins.then_inc(qk_T, 1)

            for cc in range(6):
                if cc == 3:
                    pe.wait_ge(f_negF, 1)
                if cc >= 4:
                    pe.wait_ge(qk_lo, cc - 3)
                for half in range(2):
                    if cc == 0:
                        pe.wait_ge(h_lo, 16 + 4 * half + 4)
                    tokens_unit(N_FOX + 2 * cc + half, None, of_hT, UK * half, TT,
                                lambda t: ps[:, 2 * (cc % 4) + t], half == 0, half == 1)
                if cc == 0:
                    pe.wait_ge(small_lo, 2)
                    for t in range(TT):
                        for k in range(KT):
                            hi, lo = of_hT(k, t)
                            for n, a in enumerate((hi, lo)):
                                ins = mm(ps[:, 7, t * 2 * H:(t + 1) * 2 * H], a, wf2[:, k],
                                         start=t == 0 and k == 0 and n == 0, stop=k == KT - 1 and n == 1,
                                         skip_group_check=True)
                    ins.then_inc(f_mm, 1)
                if cc == 1:
                    pe.wait_ge(f_log, 1)
                    mm(ps[:, 7, 64:64 + H], upper[:], fx[:, 7, 0], start=True, stop=True, skip_group_check=True)
                    mm(ps[:, 7, 64 + H:64 + 2 * H], ones[:], fx[:, 7, 0], start=False, stop=False, skip_group_check=True)
                    mm(ps[:, 7, 64 + H:64 + 2 * H], upper[:], fx[:, 7, 1], start=False, stop=True,
                       skip_group_check=True).then_inc(f_cum, 1)
                if cc == 4:
                    pe.wait_ge(qk_lo, 3)
                    for t in range(TT):
                        ins = nc.tensor.transpose(ps[0:H, 4, t * P:(t + 1) * P], nF[:, t], ident[:])
                    ins.then_inc(f_T, 1)
                if 1 <= cc <= 4:
                    qk_transposes(cc - 1)

            def scores(i):
                s, p = i // 2, i % 2
                rows = slice(p * HD, (p + 1) * HD)
                for qt in range(TT):
                    for part in range(1 + qt):
                        bank = 3 * (i % 2) + qt + part
                        js = range(4) if qt == 0 else range(2 * part, 2 * part + 2)
                        w = (qt + 1) * P
                        for n, j in enumerate(js):
                            h = 8 * s + 2 * j + p
                            mm(ps[:, bank, n * w:(n + 1) * w], head_row[:, h:h + 1].to_broadcast([P, P]), nFT[:, 0:w],
                               start=n == 0, stop=False, skip_group_check=True)
                        mm(ps[:, bank].rearrange("p (j k) -> p j k", k=w), ident_r[:],
                           mask_r[:, T - w:T].unsqueeze(1).to_broadcast([P, CW // w, w]), start=False, stop=False,
                           skip_group_check=True)
                        for n, j in enumerate(js):
                            c = 4 * s + j
                            dst = ps[:, bank, n * w:(n + 1) * w]
                            qs = slice(qt * P, (qt + 1) * P)
                            mm(dst, qT_hi[rows, c, qs], kT_hi[rows, c, 0:w], start=False, stop=False,
                               skip_group_check=True)
                            mm(dst, qT_hi[rows, c, qs], kT_lo[rows, c, 0:w], start=False, stop=False,
                               skip_group_check=True)
                            ins = mm(dst, qT_lo[rows, c, qs], kT_hi[rows, c, 0:w], start=False, stop=True,
                                     skip_group_check=True)
                ins.then_inc(scored, 1)

            def probs_transposes(*rounds):
                for r in rounds:
                    i = r // 3
                    pe.wait_ge(exped, 8 * i + 8)
                    for a in range(4):
                        ins = nc.tensor.transpose(ps[:, 3 * (i % 2) + r % 3, a * P:(a + 1) * P],
                                                  probs[i % 2][:, 4 * (r % 3) + a], ident[:])
                    ins.then_inc(probs_T, 1)

            def values(*rounds):
                for r in rounds:
                    i = r // 3
                    s, p, qt = i // 2, i % 2, int(r % 3 > 0)
                    pe.wait_ge(pT_lo_done, r + 1)
                    for a in range(4):
                        j = a if qt == 0 else 2 * (r % 3 - 1) + a // 2
                        kt = 0 if qt == 0 else a % 2
                        h = 8 * s + 2 * j + p
                        vs = slice(h * HD, (h + 1) * HD)
                        dst = ps[:, 3 * (i % 2), (4 * qt + j) * HD:(4 * qt + j + 1) * HD]
                        mm(dst, pT_hi[:, r % 2, a], V_hi[:, kt, vs], start=r % 3 == 0 and a == 0, stop=False,
                           skip_group_check=True)
                        mm(dst, pT_hi[:, r % 2, a], V_lo[:, kt, vs], start=False, stop=False, skip_group_check=True)
                        ins = mm(dst, pT_lo[:, r % 2, a], V_hi[:, kt, vs], start=False, stop=kt == qt,
                                 skip_group_check=True)
                    ins.then_inc(pv_done, 1)

            def gate_unit(n):
                tokens_unit(N_FOX + 12 + n, None, of_hT, UK * (n % 2), TT, lambda t: ps[:, 6 + t], n % 2 == 0,
                            n % 2 == 1)

            def gated(t, k):
                return sg[k // UK][:, t, (k % UK) * P:(k % UK + 1) * P]

            def out_unit(n):
                pe.wait_ge(o_lo, 2 * (n // 2) + 2)
                tokens_unit(N_FOXOUT + n, None,
                            lambda k, t: (qT_hi[:, k, t * P:(t + 1) * P], qT_lo[:, k, t * P:(t + 1) * P]),
                            UK * (n // 2), TT, lambda t: ps[:, X_BANKS[n % 2] + t], n // 2 == 0, n // 2 == 1)

            pe.wait_ge(qk_lo, 4)
            gate_unit(0)
            pe.wait_ge(v_lo, 2)
            pe.wait_ge(fT_lo_done, 1)
            pe.wait_ge(const_r, 3)
            scores(0)
            gate_unit(1)
            scores(1)
            probs_transposes(0, 1)
            pe.wait_ge(g_sig, 2)
            gate_unit(2)
            values(0)
            probs_transposes(2)
            values(1, 2)
            probs_transposes(3, 4)
            pe.wait_ge(o_done, 8)
            scores(2)
            gate_unit(3)
            values(3)
            probs_transposes(5)
            values(4, 5)
            probs_transposes(6, 7)
            pe.wait_ge(o_done, 16)
            scores(3)
            values(6)
            probs_transposes(8)
            pe.wait_ge(g_sig, 4)
            transposes(gated, o_T, O_BANKS[0:2], 0)
            values(7, 8)
            probs_transposes(9, 10)
            out_unit(0)
            values(9)
            probs_transposes(11)
            values(10, 11)
            out_unit(1)
            pe.wait_ge(o_done, 32)
            transposes(gated, o_T, O_BANKS[2:4], UK)
            out_unit(2)
            out_unit(3)

            stream_transposes(5)
            for k in range(KT):
                pe.wait_ge(h_lo, 24 + k + 1)
                for t in range(TT):
                    hi, lo = of_hT(k, t)
                    for n, a in enumerate((hi, lo)):
                        ins = mm(ps[:, 7, t * 2 * E:(t + 1) * 2 * E], a, rw2[:, k],
                                 start=t == 0 and k == 0 and n == 0, stop=k == KT - 1 and n == 1,
                                 skip_group_check=True)
            ins.then_inc(routed, 1)
            pe.wait_ge(picked, 1)
            sel = tk[:, 9]
            mm(ps[:, 7, 32:32 + E], upper[:], sel[:, 0], start=True, stop=True, skip_group_check=True)
            mm(ps[:, 7, 40:40 + E], ones[:], sel[:, 0], start=False, stop=False, skip_group_check=True)
            mm(ps[:, 7, 40:40 + E], upper[:], sel[:, 1], start=False, stop=True, skip_group_check=True)
            mm(ps[:, 7, 64:64 + E], ones[:], sel[:, 0], start=False, stop=False, skip_group_check=True)
            mm(ps[:, 7, 64:64 + E], ones[:], sel[:, 1], start=False, stop=True,
               skip_group_check=True).then_inc(slotted, 1)

            def gather(b):
                pe.wait_ge(m_S, at(1, 1, b))
                for q, h in enumerate((hn_hi, hn_lo)):
                    if q:
                        pe.wait_ge(hn_lo_done, 2)
                    for k in range(KT):
                        for t in range(TT):
                            ins = mm(ps[:, 2 + 2 * q + k // 4, (k % 4) * P:(k % 4 + 1) * P],
                                     h[:, t, k * P:(k + 1) * P], S[:, t], start=k % 4 == 0 and t == 0, stop=t == 1,
                                     skip_group_check=True)
                    ins.then_inc(m_gat, 1)

            def scatter(j):
                for t in range(TT):
                    for q, y in enumerate((y_hi, y_lo)):
                        ins = mm(ps[:, SCATTER_BANKS[j][t]], ST[:, t * P:(t + 1) * P], y[:, j * CW:(j + 1) * CW],
                                 start=q == 0, stop=q == 1)
                ins.then_inc(m_scat, 1)

            def act_transposes(b, c):
                pe.wait_ge(m_act, at(c + 2, FC, b))
                for a in range(4):
                    ins = nc.tensor.transpose(ps[:, 6, a * P:(a + 1) * P], act_s[:, c % 2, a * P:(a + 1) * P], ident[:])
                ins.then_inc(m_T, 1)

            def moe_unit(b, i, src, k0, bank, first, last):
                tokens_unit(N_MOE + i, b, src, k0, 1, lambda t: ps[:, bank], first, last)

            def of_xg(k, t):
                return xg_hi[:, k], xg_lo[:, k]

            pe.wait_ge(hn_hi_done, 2)
            pe.wait_ge(blocks, 1)
            nblk = pe.value_load(nblk_i[0:1, 0:1], min_val=E, max_val=2 * E)
            with pe.Fori(0, nblk) as b:
                gather(b)
                pe.wait_ge(m_ylo, at(1, 1, b))
                pe.wait_ge(m_xh, at(1, 1, b))
                for j in range(2):
                    scatter(j)
                pe.wait_ge(m_xl, at(1, 1, b))
                for c in range(FC):
                    if c == 1:
                        pe.wait_ge(m_acc, at(3, 2, b))
                    pe.wait_ge(m_silu, at(max(c, 1), FC, b))
                    for half in range(2):
                        moe_unit(b, base(c) + half, of_xg, UK * half, 4 + c % 2, half == 0, half == 1)
                        if c == 1 and half == 0:
                            act_transposes(b, 0)
                            for t in range(TT):
                                ins = mm(ps[:, 7, t * P:(t + 1) * P], S[:, t], ident_r[:], start=t == 0, stop=True,
                                         skip_group_check=True)
                            ins.then_inc(m_TS, 1)
                    pe.wait_ge(m_act, at(max(c, 1), FC, b))
                    if c == 0:
                        pe.wait_ge(m_acc, at(2, 2, b))
                    for half in range(2):
                        moe_unit(b, base(c) + 2 + half, of_xg, UK * half, 2 + c % 2, half == 0, half == 1)
                    for d in ([c - 1] if c else []) + ([c] if c == FC - 1 else []):
                        pe.wait_ge(m_tlo, at(d + 1, FC, b))
                        for j in range(2):
                            moe_unit(b, down(d) + j,
                                     lambda k, t: (aT_hi[:, d % 2, k], aT_lo[:, d % 2, k]), 0, j, d == 0, d == FC - 1)
                            if j == 0 and d < FC - 1:
                                act_transposes(b, d + 1)
            pe.wait_ge(m_ST, nblk)
            for j in range(2):
                pe.wait_ge(m_ylo, at(1 + j, 1, nblk))
                scatter(j)

        @block.vector
        def _(dve):
            links = [0]

            def link(ins):
                links[0] += 1
                ins.then_inc(chain, 1)
                dve.wait_ge(chain, links[0])

            nxt = [0]

            def lo_to(n, b=None):
                first = 0 if b is None else N_MOE
                last = N_MOE + HR - 1 if b is None else N_MOE + FFN_UNITS - 1
                while first + nxt[0] <= min(first + n, last):
                    m = first + nxt[0]
                    dve.wait_ge(hi_done, at(m + 1, FFN_UNITS, b))
                    n_early = early_at(m, b)
                    src = raw[:, raw_place(m, b)[0] % RR] if n_early is None else early[n_early]
                    nc.vector.tensor_tensor(wlo[:, m % HR], src, whi[:, m % HR].bitcast(F32),
                                            ALU.subtract).then_inc(lo_done, 1)
                    nxt[0] += 1

            def mean_squares(r):
                nc.vector.tensor_tensor_reduce(xn[:, 1], X[:, 1], X[:, 1], 1.0, 0.0, ALU.mult, ALU.add,
                                               ss[:, 2 * r + 1:2 * r + 2]).then_inc(sumsq_v, 1)
                dve.wait_ge(sumsq, r + 1)
                dve.wait_ge(sumsq_v, r + 1)
                nc.vector.tensor_scalar(ms[:, 2 * r:2 * r + 2], ss[:, 2 * r:2 * r + 2], 1.0 / D, EPS, ALU.mult, ALU.add
                                        ).then_inc(ms_done, 1)

            def stream_mean_squares(r, half):
                dve.wait_ge(sumsq, 4 * r - 4 + 2 * half)
                m = ms[:, 2 * r:2 * r + 2]
                if half == 0:
                    link(nc.vector.tensor_scalar(m, ssh[:, r % 2, 0], 1.0 / D, EPS, ALU.mult, ALU.add))
                else:
                    nc.vector.scalar_tensor_tensor(out=m, in0=ssh[:, r % 2, 1], scalar=1.0 / D, in1=m, op0=ALU.mult,
                                                   op1=ALU.add).then_inc(ms_done, 1)

            def normalise(r, count):
                dve.wait_ge(pow_done, count)
                for t in range(TT):
                    nc.vector.tensor_scalar(xn[:, t], X[:, t], rstd[:, 2 * r + t:2 * r + t + 1], None, ALU.mult
                                            ).then_inc(xn_done, 1)

            def transposed_lo(r):
                for k in range(KT):
                    dve.wait_ge(h_hi, 8 * r + 2 * (k // 2) + 2)
                    nc.vector.scalar_tensor_tensor(out=hT_lo[:, k], in0=ps[:, k // 2, (k % 2) * T:(k % 2 + 1) * T],
                                                   scalar=par[:, GAIN[r] + k:GAIN[r] + k + 1],
                                                   in1=hT_hi[:, k].bitcast(F32), op0=ALU.mult, op1=ALU.subtract
                                                   ).then_inc(h_lo, 1)

            def log1p(y, tmp):
                den, s, s2 = tmp
                link(nc.vector.tensor_scalar(den, y, 2.0, None, ALU.add))
                link(nc.vector.reciprocal(den, den))
                link(nc.vector.tensor_tensor(s, y, den, ALU.mult))
                link(nc.vector.tensor_tensor(s2, s, s, ALU.mult))
                link(nc.vector.tensor_scalar(den, s2, 1.0 / 17, None, ALU.mult))
                for odd in (15, 13, 11, 9, 7, 5, 3):
                    link(nc.vector.scalar_tensor_tensor(out=den, in0=den, scalar=1.0 / odd, in1=s2, op0=ALU.add,
                                                        op1=ALU.mult))
                link(nc.vector.scalar_tensor_tensor(out=den, in0=den, scalar=1.0, in1=s, op0=ALU.add, op1=ALU.mult))
                return den

            def add_to_x(bank, j):
                xj = X[:, :, j * CW:(j + 1) * CW]
                nc.vector.tensor_tensor(xj, ps[:, bank:bank + 2], xj, ALU.add).then_inc(x_done, 1)

            dve.wait_ge(x_in, 32)
            mean_squares(0)
            nc.vector.memset(xpad[:, :, 0:CONV - 1], 0.0).then_inc(edges, 1)
            normalise(0, 1)
            dve.wait_ge(par_T, 1)
            nc.vector.tensor_copy(par[:], ps[:, 7, 0:96]).then_inc(par_done, 1)
            lo_to(0)
            dve.wait_ge(par_done, 1)
            transposed_lo(0)
            lo_to(2)
            lam = par[:, PAR_LAM:PAR_LAM + KT]
            nc.vector.scalar_tensor_tensor(out=lt[:, 0], in0=lam, scalar=-1.0, in1=lam, op0=ALU.mult, op1=ALU.min
                                           ).then_inc(lam_neg, 1)
            dve.wait_ge(lam_exp, 1)
            half_log = log1p(lt[:, 1], (lt[:, 2], lt[:, 3], lt[:, 4]))
            link(nc.vector.tensor_scalar(lt[:, 3], lam, -1.0, 0.0, ALU.mult, ALU.max))
            link(nc.vector.scalar_tensor_tensor(out=lt[:, 1], in0=half_log, scalar=2.0, in1=lt[:, 3], op0=ALU.mult,
                                                op1=ALU.add))
            nc.vector.tensor_scalar(lt[:, 4], lt[:, 1], -LRU_C, None, ALU.mult).then_inc(lam_done, 1)
            nc.vector.tensor_scalar(lt[:, 5], lt[:, 1], LRU_C, None, ALU.mult).then_inc(lam_done, 1)
            dve.wait_ge(edges, 1)
            for ch in range(2):
                lo_to(2 * ch + 3)
                cs = range(4 * ch, 4 * ch + 4)
                for w in range(CONV):
                    for c in cs:
                        src = xpad[:, c, w:w + T]
                        scale = par[:, PAR_CONVW + 8 * w + c:PAR_CONVW + 8 * w + c + 1]
                        if w == 0:
                            dve.wait_ge(xp_in, c // 2 + 1)
                            ins = nc.vector.tensor_scalar(xc[:, c], src, scale, par[:, PAR_CONVB + c:PAR_CONVB + c + 1],
                                                          ALU.mult, ALU.add)
                        else:
                            ins = nc.vector.scalar_tensor_tensor(out=xc[:, c], in0=src, scalar=scale, in1=xc[:, c],
                                                                 op0=ALU.mult, op1=ALU.add)
                        if w == CONV - 1:
                            ins.then_inc(conv_done, 1)
                        elif c == cs[-1]:
                            link(ins)
            lo_to(7)
            def z_to_lo(g):
                cs = slice(4 * g, 4 * g + 4)
                dve.wait_ge(z_hi, g + 1)
                nc.vector.tensor_tensor(hT_lo[:, cs], yb[:, cs], hT_hi[:, cs].bitcast(F32), ALU.subtract
                                        ).then_inc(z_lo, 1)

            for g in range(2):
                q = qf[:, 4 * g:4 * g + 4]
                dve.wait_ge(a_exp, 4 * g + 4)
                link(nc.vector.tensor_tensor(q, av[:, 4 * g:4 * g + 4], av[:, 4 * g:4 * g + 4], ALU.mult))
                dve.wait_ge(th_done, 4 * g + 4)
                nc.vector.scalar_tensor_tensor(out=q, in0=q, scalar=1.0, in1=rg[:, 4 * g:4 * g + 4], op0=ALU.add,
                                               op1=ALU.mult).then_inc(m2_done, 1)
                if g == 0:
                    lo_to(8)
            for g in range(2):
                cs = slice(4 * g, 4 * g + 4)
                dve.wait_ge(mult_done, g + 1)
                dve.wait_ge(gx_done, 2 * g + 2)
                link(nc.vector.tensor_tensor(gi[:, cs], qf[:, cs], gi[:, cs], ALU.mult))
                if g == 1:
                    z_to_lo(0)
                for c in range(4 * g, 4 * g + 4):
                    ins = nc.vector.tensor_tensor_scan(xc[:, c], av[:, c], gi[:, c], 0.0, ALU.mult, ALU.add)
                link(ins)
                dve.wait_ge(gelu, g + 1)
                nc.vector.tensor_tensor(yb[:, cs], xc[:, cs], yb[:, cs], ALU.mult).then_inc(z_done, 1)
            lo_to(9)
            z_to_lo(1)
            dve.wait_ge(consts, 10)
            nc.vector.tensor_copy(ident_r[:], ident[:]).then_inc(const_r, 1)
            nc.vector.tensor_tensor(head_row[:], ident[:, 0:H], ident[:, 32:32 + H], ALU.add).then_inc(const_r, 1)
            nc.vector.tensor_copy(mask_r[:], mask[:]).then_inc(const_r, 1)
            dve.wait_ge(small_in, 16 * 7)
            nc.vector.tensor_scalar(qkg[:, 0:1], qkg[:, 0:1], float(HD) ** -0.5, None, ALU.mult).then_inc(qkg_done, 1)
            for j in range(2):
                lo_to(N_IN + 2 * j + 3)
                dve.wait_ge(used, N_IN + 2 * j + 2)
                add_to_x(2 * j, j)

                if j == 0:
                    dve.wait_ge(small_hi, 2)
                    nc.vector.tensor_tensor(wf2[:, :, H:], wf[:], wf2[:, :, 0:H].bitcast(F32), ALU.subtract
                                            ).then_inc(small_lo, 1)
                    nc.vector.tensor_tensor(rw2[:, :, E:], rw[:], rw2[:, :, 0:E].bitcast(F32), ALU.subtract
                                            ).then_inc(small_lo, 1)

            dve.wait_ge(x_done, 2)
            mean_squares(1)
            normalise(1, 2)
            transposed_lo(1)
            for c in range(FC):
                lo_to(N_FFN + base(c) + 5)
                dve.wait_ge(used, N_FFN + base(c) + 4)
                dve.wait_ge(f_silu, c + 1)
                nc.vector.tensor_tensor(sil[:].rearrange("p c t -> p (c t)"), sil[:].rearrange("p c t -> p (c t)"),
                                        ps[:, 2:4].rearrange("p b n -> p (b n)"), ALU.mult).then_inc(f_act, 1)
                lo_to(N_FFN + base(c) + 6)
                dve.wait_ge(f_ahi, c + 1)
                nc.vector.tensor_tensor(fT_lo[:, c % 2], sil[:], fT_hi[:, c % 2].bitcast(F32), ALU.subtract
                                        ).then_inc(f_alo, 1)
            for j in range(2):
                lo_to(N_FOX + j)
                dve.wait_ge(used, N_FOX - 1 + j)
                add_to_x(4 + 2 * j, j)

            transposed_lo(2)
            stream_mean_squares(2, 0)
            stream_mean_squares(2, 1)
            dve.wait_ge(pow_done, 3)
            link(nc.vector.tensor_tensor(rms2[:], rstd[:, 4:6], rstd[:, 4:6], ALU.mult))
            link(nc.vector.tensor_scalar(rms2[:], rms2[:], 1.0 / HD, None, ALU.mult))
            for cc in range(6):
                m = N_FOX + 2 * cc + 1
                bank = 2 * (cc % 4)
                lo_to(m + 2)
                if cc < 4:
                    dve.wait_ge(squared, cc + 1)
                    nc.vector.tensor_reduce(ssq[:, 0], junk[:].rearrange("p (h d) -> p h d", d=HD), AX_X, ALU.add
                                            ).then_inc(ssq_done, 1)
                    dve.wait_ge(ssq_done, 2 * cc + 1)
                    for t in range(TT):
                        heads = slice(8 * t, 8 * t + 8)
                        ins = nc.vector.tensor_scalar(ssq[:, 1, heads], ssq[:, 0, heads], rms2[:, t:t + 1], EPS,
                                                      ALU.mult, ALU.add)
                    ins.then_inc(ssq_done, 1)
                else:
                    dve.wait_ge(v_hi, 2 * cc - 6)
                    cols = slice((cc - 4) * CW, (cc - 3) * CW)
                    for t in range(TT):
                        ins = nc.vector.scalar_tensor_tensor(out=V_lo[:, t, cols], in0=ps[:, bank + t],
                                                             scalar=rstd[:, 4 + t:5 + t],
                                                             in1=V_hi[:, t, cols].bitcast(F32), op0=ALU.mult,
                                                             op1=ALU.subtract)
                    ins.then_inc(v_lo, 1)
                if cc < 4:
                    dve.wait_ge(pow_done, 3 + 2 * cc + 2)
                    nc.vector.tensor_tensor(xn[:, cc % 2].rearrange("p (h d) -> p h d", d=HD),
                                            ps[:, bank:bank + 2].rearrange("p b (h d) -> p (b h) d", d=HD),
                                            ssq[:, 2].unsqueeze(2).to_broadcast([P, TT * 8, HD]), ALU.mult
                                            ).then_inc(qn_done, 1)
                if cc == 0:
                    dve.wait_ge(f_mm, 1)
                    for part in range(2):
                        for t in range(TT):
                            c0 = (2 * t + part) * H
                            ins = nc.vector.scalar_tensor_tensor(out=fx[:, 0, t], in0=ps[:, 7, c0:c0 + H],
                                                                 scalar=rstd[:, 4 + t:5 + t],
                                                                 in1=fx[:, 0, t] if part else bf[:], op0=ALU.mult,
                                                                 op1=ALU.add)
                        link(ins)
                    nc.vector.scalar_tensor_tensor(out=fx[:, 1], in0=fx[:, 0], scalar=-1.0, in1=fx[:, 0], op0=ALU.mult,
                                                   op1=ALU.min).then_inc(f_neg, 1)
                    dve.wait_ge(f_exp, 1)
                    half_log = log1p(fx[:, 2], (fx[:, 3], fx[:, 4], fx[:, 5]))
                    link(nc.vector.tensor_scalar(fx[:, 6], fx[:, 0], 0.0, None, ALU.min))
                    nc.vector.scalar_tensor_tensor(out=fx[:, 7], in0=half_log, scalar=-2.0, in1=fx[:, 6], op0=ALU.mult,
                                                   op1=ALU.add).then_inc(f_log, 1)
                if cc == 1:
                    dve.wait_ge(f_cum, 1)
                    nc.vector.tensor_scalar(nF[:].rearrange("p t h -> p (t h)"), ps[:, 7, 64:64 + 2 * H], -1.0, None,
                                            ALU.mult).then_inc(f_negF, 1)
                if cc == 4:
                    dve.wait_ge(fT_hi_done, 1)
                    nc.vector.tensor_tensor(nFT[32:32 + H, :], ps[0:H, 4, 0:T], nFT[0:H, :].bitcast(F32),
                                            ALU.subtract).then_inc(fT_lo_done, 1)
                if 1 <= cc <= 4:
                    q = cc - 1
                    hi, lo = (a[:, 4 * (q % 2):4 * (q % 2) + 4].rearrange("p c t -> p (c t)")
                              for a in ((qT_hi, qT_lo) if q < 2 else (kT_hi, kT_lo)))
                    dve.wait_ge(qk_hi, q + 1)
                    dve.wait_ge(qkg_done, 1)
                    nc.vector.scalar_tensor_tensor(out=lo, in0=ps[:, 2 * q:2 * q + 2].rearrange("p b n -> p (b n)"),
                                                   scalar=qkg[:, q // 2:q // 2 + 1], in1=hi.bitcast(F32),
                                                   op0=ALU.mult, op1=ALU.subtract).then_inc(qk_lo, 1)
            def row_max(i):
                a = 3 * (i % 2)
                dve.wait_ge(scored, i + 1)
                nc.vector.tensor_reduce(nm[:, i, 0:4], ps[:, a].rearrange("p (j k) -> p j k", k=P), AX_X, ALU.max,
                                        negate=True).then_inc(nmax, 1)
                nc.vector.tensor_reduce(nm[:, i, 4:8],
                                        ps[:, a + 1:a + 3].rearrange("p b (j k) -> p (b j) k", k=T), AX_X,
                                        ALU.max, negate=True).then_inc(nmax, 1)

            def probs_lo(*rounds):
                for r in rounds:
                    dve.wait_ge(pT_hi_done, r + 1)
                    nc.vector.tensor_tensor(pT_lo[:, r % 2].rearrange("p a k -> p (a k)"),
                                            ps[:, 3 * (r // 3 % 2) + r % 3],
                                            pT_hi[:, r % 2].rearrange("p a k -> p (a k)").bitcast(F32),
                                            ALU.subtract).then_inc(pT_lo_done, 1)

            def outputs(i):
                s, p = i // 2, i % 2
                dve.wait_ge(exped, 8 * i + 8)
                link(nc.vector.reciprocal(rinv[:, i], sm[:, i]))
                dve.wait_ge(pv_done, 3 * i + 3)
                dve.wait_ge(g_sig, 2 * s + 2)
                for qt in range(TT):
                    for j in range(4):
                        h = 8 * s + 2 * j + p
                        g = sg[s][:, qt, (h - 8 * s) * HD:(h - 8 * s + 1) * HD]
                        r = 4 * qt + j
                        nc.vector.scalar_tensor_tensor(out=g, in0=ps[:, 3 * (i % 2), r * HD:(r + 1) * HD],
                                                       scalar=rinv[:, i, r:r + 1], in1=g, op0=ALU.mult,
                                                       op1=ALU.mult).then_inc(o_done, 1)
            def outputs_T_lo(*rounds):
                for r in rounds:
                    dve.wait_ge(o_hi, r + 1)
                    nc.vector.tensor_tensor(qT_lo[:, 2 * r:2 * r + 2].rearrange("p k t -> p (k t)"), ps[:, O_BANKS[r]],
                                            qT_hi[:, 2 * r:2 * r + 2].rearrange("p k t -> p (k t)").bitcast(F32),
                                            ALU.subtract).then_inc(o_lo, 1)

            row_max(0)
            lo_to(N_FOX + 15)
            row_max(1)
            probs_lo(0, 1, 2)
            outputs(0)
            lo_to(N_FOXOUT)
            lo_to(N_FOXOUT + 1)
            probs_lo(3, 4)
            row_max(2)
            probs_lo(5)
            outputs(1)
            lo_to(N_FOXOUT + 2)
            probs_lo(6, 7)
            row_max(3)
            probs_lo(8)
            outputs_T_lo(0, 1)
            outputs(2)
            probs_lo(9, 10)
            probs_lo(11)
            lo_to(N_FOXOUT + 3)
            outputs(3)
            outputs_T_lo(2, 3)
            for j in range(2):
                lo_to(N_MOE + j)
                dve.wait_ge(used, N_FOXOUT + j + 3)
                add_to_x(X_BANKS[j], j)

            rank = tk[:, 1]
            for t in range(TT):
                ins = nc.vector.tensor_scalar(rank[:, t], iota[:, 0:E], -1.0, float(E + 1), ALU.mult, ALU.add)
            link(ins)
            nc.vector.memset(act_s[:, 0, 0:2], 0.0).then_inc(m_act, 1)
            nc.vector.memset(tk[:, 11, 0], 0.0).then_inc(m_acc, 1)
            stream_mean_squares(3, 0)
            transposed_lo(3)
            stream_mean_squares(3, 1)

            def bc(a):
                return a.unsqueeze(2).to_broadcast([P, TT, E])
            dve.wait_ge(routed, 1)
            dve.wait_ge(pow_done, 12)
            halves = ps[:, 7, 0:TT * 2 * E].rearrange("p (t h e) -> p t h e", t=TT, h=2)
            for t in range(TT):
                ins = nc.vector.tensor_scalar(tk[:, 10, t], halves[:, t, 0], rstd[:, 6 + t:7 + t], None, ALU.mult)
            link(ins)
            for t in range(TT):
                ins = nc.vector.scalar_tensor_tensor(out=tk[:, 0, t], in0=halves[:, t, 1], scalar=rstd[:, 6 + t:7 + t],
                                                     in1=tk[:, 10, t], op0=ALU.mult, op1=ALU.add)
            link(ins)

            def pick(src, top, eq, first):
                link(nc.vector.tensor_reduce(tv[:, top], src, AX_X, ALU.max))
                for t in range(TT):
                    ins = nc.vector.scalar_tensor_tensor(out=eq[:, t], in0=src[:, t], scalar=tv[:, top, t:t + 1],
                                                         in1=rank[:, t], op0=ALU.is_equal, op1=ALU.mult)
                link(ins)
                link(nc.vector.tensor_reduce(tv[:, 7], eq, AX_X, ALU.max))
                link(nc.vector.tensor_tensor(first, eq, bc(tv[:, 7]), ALU.is_equal))
            pick(tk[:, 0], 0, tk[:, 2], tk[:, 3])
            link(nc.vector.scalar_tensor_tensor(out=tk[:, 4], in0=tk[:, 3], scalar=-BIG, in1=tk[:, 0], op0=ALU.mult,
                                                op1=ALU.add))
            pick(tk[:, 4], 1, tk[:, 5], tk[:, 6])
            nc.vector.tensor_tensor(tk[:, 9], tk[:, 3], tk[:, 6], ALU.add).then_inc(picked, 1)
            nc.vector.tensor_tensor(tv[:, 2], tv[:, 1], tv[:, 0], ALU.subtract).then_inc(w_diff, 1)
            dve.wait_ge(gb_in, 16)
            for t in range(TT):
                nc.vector.scalar_tensor_tensor(out=hn[:, t], in0=X[:, t], scalar=rstd[:, 6 + t:7 + t], in1=gb[:],
                                               op0=ALU.mult, op1=ALU.mult).then_inc(hn_done, 1)
            dve.wait_ge(slotted, 1)
            dve.wait_ge(zeros, 2)
            nc.vector.tensor_tensor(posb[:, :, 0:E], ps[:, 7, 32:48].rearrange("p (t e) -> p t e", e=E), tk[:, 9],
                                    ALU.mult)
            link(nc.vector.tensor_reduce(cnt[:, 0:1], ps[:, 7, 64:64 + E], AX_X, ALU.max))
            nc.vector.tensor_copy(pcol[:], posb[:, :, 0]).then_inc(m_col, 1)
            link(nc.vector.tensor_scalar(cnt[:, 1:2], cnt[:, 0:1], float(P) + 0.5, float(E), ALU.is_gt, ALU.mult))
            dve.wait_ge(m_col, 1)
            for t in range(TT):
                ins = nc.vector.tensor_scalar(S[:, t], iota[:], pcol[:, t:t + 1], None, ALU.is_equal)
            ins.then_inc(m_S, 1)
            link(nc.vector.tensor_scalar(cnt[:, 0:1], cnt[:, 1:2], float(E), None, ALU.add))
            nc.vector.tensor_copy(nblk_i[:], cnt[:, 0:1]).then_inc(blocks, 1)
            for t in range(TT):
                dve.wait_ge(hn_hi_done, t + 1)
                nc.vector.tensor_tensor(hn_lo[:, t], hn[:, t], hn_hi[:, t].bitcast(F32), ALU.subtract
                                        ).then_inc(hn_lo_done, 1)
            dve.wait_ge(zeros, 5)
            nc.vector.memset(tk[:, 11, 1], 0.0).then_inc(m_ylo, 1)
            lo_to(N_MOE + 2)
            nc.vector.tensor_scalar(posb[:, :, E:2 * E], posb[:, :, 0:E], -float(P), None, ALU.add)
            dve.wait_ge(w_exp, 1)
            link(nc.vector.tensor_scalar(tv[:, 4], tv[:, 3], 1.0, None, ALU.add))
            link(nc.vector.reciprocal(tv[:, 5], tv[:, 4]))
            link(nc.vector.tensor_tensor(tv[:, 6], tv[:, 3], tv[:, 5], ALU.mult))
            link(nc.vector.tensor_tensor(tk[:, 7], tk[:, 3], bc(tv[:, 5]), ALU.mult))
            link(nc.vector.tensor_tensor(tk[:, 8], tk[:, 6], bc(tv[:, 6]), ALU.mult))
            for half in range(2):
                ins = nc.vector.tensor_tensor(combt[:, :, 1 + half * E:1 + (half + 1) * E], tk[:, 7], tk[:, 8], ALU.add)
            link(ins)

            def one_hot(col, count):
                nc.vector.tensor_copy(pcol[:], posb[:, :, col].rearrange("p t o -> p (t o)")).then_inc(m_col, 1)
                dve.wait_ge(m_col, count)
                for t in range(TT):
                    ins = nc.vector.tensor_scalar(S[:, t], iota[:], pcol[:, t:t + 1], None, ALU.is_equal)
                ins.then_inc(m_S, 1)

            def gathered_lo(b):
                dve.wait_ge(m_gat, at(2, 2, b))
                nc.vector.tensor_copy(xg_lo[:].rearrange("p k s -> p (k s)"),
                                      ps[:, 4:6].rearrange("p b n -> p (b n)")).then_inc(m_xl, 1)

            def y_to_lo(b, count, first, last):
                dve.wait_ge(m_yhi, at(count, 1, b))
                cols = slice(first * CW, last * CW)
                nc.vector.tensor_tensor(y_lo[:, cols], ps[:, first:last].rearrange("p b n -> p (b n)"),
                                        y_hi[:, cols].bitcast(F32), ALU.subtract).then_inc(m_ylo, 1)

            def weight_column(b):
                nc.vector.tensor_copy(ccol[:], combt[:, :, bass.ds(b, 1)].rearrange("p t o -> p (t o)")
                                      ).then_inc(m_col, 1)

            def accumulate(b, each=None):
                dve.wait_ge(m_acc, at(1, 2, b))
                dve.wait_ge(m_col, at(2, 2, b))
                for j in range(2):
                    dve.wait_ge(m_scat, at(1 + j, 2, b))
                    for t in range(TT):
                        xj = X[:, t, j * CW:(j + 1) * CW]
                        ins = nc.vector.scalar_tensor_tensor(out=xj, in0=ps[:, SCATTER_BANKS[j][t]],
                                                             scalar=ccol[:, t:t + 1], in1=xj, op0=ALU.mult,
                                                             op1=ALU.add)
                        if each is not None:
                            ins.then_inc(each, 1)
                    if each is None:
                        ins.then_inc(m_acc, 1)

            def act_T_lo(b, c):
                dve.wait_ge(m_thi, at(c + 1, FC, b))
                nc.vector.tensor_tensor(aT_lo[:, c % 2].rearrange("p a s -> p (a s)"), ps[:, 6],
                                        aT_hi[:, c % 2].rearrange("p a s -> p (a s)").bitcast(F32), ALU.subtract
                                        ).then_inc(m_tlo, 1)

            def expert_block(b, converted, first=False):
                nxt[0] = converted
                lo_to(1, b)
                if not first:
                    y_to_lo(b, 0, 0, 2)
                weight_column(b)
                gathered_lo(b)
                lo_to(2, b)
                accumulate(b)
                for c in range(FC):
                    lo_to(base(c) + 5, b)
                    dve.wait_ge(used, at(N_MOE + base(c) + 4, FFN_UNITS, b))
                    dve.wait_ge(m_silu, at(c + 2, FC, b))
                    nc.vector.tensor_tensor(act_s[:, c % 2], gt[:, c % 2], ps[:, 2 + c % 2], ALU.mult
                                            ).then_inc(m_act, 1)
                    lo_to(base(c) + 6, b)
                    act_T_lo(b, c)
                    if c == 2:
                        dve.wait_ge(m_TS, at(1, 1, b))
                        one_hot(bass.ds(b + 1, 1), at(3, 2, b))
                lo_to(FFN_UNITS - 1, b)

            expert_block(0, HR, first=True)
            dve.wait_ge(blocks, 1)
            nblk = dve.value_load(nblk_i[0:1, 0:1], min_val=E, max_val=2 * E)
            with dve.Fori(1, nblk) as b:
                expert_block(b, 0)
            weight_column(nblk)
            for j in range(2):
                y_to_lo(nblk, j, j, j + 1)
            accumulate(nblk, m_fin)


_INS = ['x', 'norm_mix', 'norm_ffn', 'lru_w_in', 'lru_conv_w', 'lru_conv_b', 'lru_w_a', 'lru_b_a', 'lru_w_x',
        'lru_b_x', 'lru_log_lambda', 'lru_w_out', 'fox_w_in', 'fox_b_f', 'fox_q_gain', 'fox_k_gain', 'fox_w_out',
        'ffn_w_gate', 'ffn_w_up', 'ffn_w_down', 'moe_router', 'moe_w_gate', 'moe_w_up', 'moe_w_down']
_OUTS = [((1, T, D), 'float32')]


def kernel(**inputs):
    import numpy as _np
    import concourse.bacc as _bacc
    from concourse import mybir as _mybir
    from concourse.bass_utils import run_bass_kernel_spmd as _run

    nc = _bacc.Bacc("TRN2", target_bir_lowering=False, num_devices=1)
    arrays, args = {}, []
    for name in _INS:
        a = _np.ascontiguousarray(inputs[name])
        arrays[f"in_{name}_dram"] = a
        args.append(nc.dram_tensor(f"in_{name}_dram", a.shape, _mybir.dt.from_np(a.dtype), kind="ExternalInput").ap())
    for i, (shape, dtype) in enumerate(_OUTS):
        dt = _mybir.dt.from_np(_np.dtype(dtype))
        args.append(nc.dram_tensor(f"out_{i}_dram", shape, dt, kind="ExternalOutput").ap())
    hybrid_trunk(nc, *args)
    r = _run(nc, [arrays], core_ids=[0])
    return r.results[0]["out_0_dram"]
```
